# Optimizing a Trainium2 kernel written in Bass

```python
import math
import jax
import jax.numpy as jnp
from jax import lax
import numpy as np
import jax, jax.numpy as jnp

D_MODEL = 1024
BATCH = 1
SEQ = 512
DEPTH = 2

GRID_W = 64
CTX_LEN = 256

N_MIXERS = 2
D_FF = 4 * D_MODEL
N_MOD = 6
NORM_EPS = 1e-6

MLA_HEADS = 8
MLA_NOPE = 128
MLA_ROPE = 64
MLA_V = 128
MLA_Q_RANK = 384
MLA_KV_RANK = 256
ROPE_BASE = 10000.0
Q_BLOCK = 128

GLA_HEADS = 4
GLA_DK = D_MODEL // 2 // GLA_HEADS
GLA_DV = D_MODEL // GLA_HEADS
GLA_GATE_RANK = 16
GLA_TAU = 16.0
GLA_CHUNK = 64


def rms_norm(x, g):
    xf = x.astype(jnp.float32)
    y = xf * lax.rsqrt(jnp.mean(xf * xf, axis=-1, keepdims=True) + NORM_EPS)
    return (y * g.astype(jnp.float32)).astype(x.dtype)

def modulate(h, shift, scale):
    return h * (1.0 + scale) + shift

def sqrelu_mlp(h, w1, w2):
    return jnp.square(jax.nn.relu(h @ w1)) @ w2

def axial_rope_tables(n_tokens):
    rows = n_tokens // GRID_W
    row = jnp.repeat(jnp.arange(rows, dtype=jnp.float32), GRID_W)
    col = jnp.tile(jnp.arange(GRID_W, dtype=jnp.float32), rows)
    half = MLA_ROPE // 2
    inv_freq = ROPE_BASE ** (-jnp.arange(0, half, 2, dtype=jnp.float32) / half)
    ang_r = row[:, None] * inv_freq
    ang_c = col[:, None] * inv_freq
    return (jnp.cos(ang_r), jnp.sin(ang_r), jnp.cos(ang_c), jnp.sin(ang_c))

def _rotate_half(x, cos, sin):
    x1, x2 = jnp.split(x, 2, axis=-1)
    return jnp.concatenate([x1 * cos - x2 * sin, x1 * sin + x2 * cos], axis=-1)

def apply_axial_rope(x, rope):
    cos_r, sin_r, cos_c, sin_c = rope
    if x.ndim == 4:
        cos_r, sin_r, cos_c, sin_c = (t[:, None, :] for t in rope)
    x_r, x_c = jnp.split(x, 2, axis=-1)
    out = jnp.concatenate([_rotate_half(x_r, cos_r, sin_r), _rotate_half(x_c, cos_c, sin_c)], axis=-1)
    return out.astype(x.dtype)

def mla_attend(q_nope, q_rope, k_nope, k_rope, v):
    scale = (MLA_NOPE + MLA_ROPE) ** -0.5
    s = (jnp.einsum('bqhd,bkhd->bhqk', q_nope, k_nope, preferred_element_type=jnp.float32)
         + jnp.einsum('bqhr,bkr->bhqk', q_rope, k_rope, preferred_element_type=jnp.float32))
    p = jax.nn.softmax(s * scale, axis=-1)
    return jnp.einsum('bhqk,bkhd->bqhd', p.astype(v.dtype), v)

def mla_mixer(h_ctx, h_lat, rope, need_ctx, w_dq, g_q, w_uq, w_dkv, g_kv, w_ukv, w_o):
    B, C, _ = h_ctx.shape
    S = h_lat.shape[1]
    T = C + S
    h_all = jnp.concatenate([h_ctx, h_lat], axis=1)
    cq = rms_norm(h_all @ w_dq, g_q)
    q = (cq @ w_uq).reshape(B, T, MLA_HEADS, MLA_NOPE + MLA_ROPE)
    ckv = h_all @ w_dkv
    c_kv = rms_norm(ckv[..., :MLA_KV_RANK], g_kv)
    kv = (c_kv @ w_ukv).reshape(B, T, MLA_HEADS, MLA_NOPE + MLA_V)
    q_nope, q_rope = q[..., :MLA_NOPE], q[..., MLA_NOPE:]
    k_nope, v = kv[..., :MLA_NOPE], kv[..., MLA_NOPE:]
    k_rope = ckv[..., MLA_KV_RANK:]
    q_rope = jnp.concatenate([q_rope[:, :C], apply_axial_rope(q_rope[:, C:], rope)], axis=1)
    k_rope = jnp.concatenate([k_rope[:, :C], apply_axial_rope(k_rope[:, C:], rope)], axis=1)

    nb = S // Q_BLOCK
    def to_blocks(a):
        return jnp.moveaxis(a.reshape(B, nb, Q_BLOCK, *a.shape[2:]), 1, 0)
    qn_blk = to_blocks(q_nope[:, C:])
    qr_blk = to_blocks(q_rope[:, C:])
    o_lat = lax.map(lambda qb: mla_attend(qb[0], qb[1], k_nope, k_rope, v), (qn_blk, qr_blk))
    o_lat = jnp.moveaxis(o_lat, 0, 1).reshape(B, S, MLA_HEADS * MLA_V)
    y_lat = o_lat @ w_o

    y_ctx = None
    if need_ctx:
        o_ctx = mla_attend(q_nope[:, :C], q_rope[:, :C], k_nope[:, :C], k_rope[:, :C], v[:, :C])
        y_ctx = o_ctx.reshape(B, C, MLA_HEADS * MLA_V) @ w_o
    return y_ctx, y_lat

def gla_log_gate(h, w1, w2, b):
    return jax.nn.log_sigmoid(((h @ w1) @ w2 + b).astype(jnp.float32)) / GLA_TAU

def gla_chunk_scan(q, k, v, g, s0):
    B, T, H, _ = q.shape
    n = T // GLA_CHUNK
    def to_chunks(a):
        return a.reshape(B, n, GLA_CHUNK, H, a.shape[-1]).transpose(1, 0, 3, 2, 4).astype(jnp.float32)
    mask = jnp.tril(jnp.ones((GLA_CHUNK, GLA_CHUNK), dtype=bool))
    def step(s, inp):
        qc, kc, vc, gc = inp
        G = jnp.cumsum(gc, axis=2)
        G_last = G[:, :, -1:, :]
        q_t = qc * jnp.exp(G)
        k_t = kc * jnp.exp(-G)
        a = jnp.where(mask, jnp.einsum('bhid,bhjd->bhij', q_t, k_t), 0.0)
        o = jnp.einsum('bhij,bhjv->bhiv', a, vc) + jnp.einsum('bhid,bhdv->bhiv', q_t, s)
        k_end = kc * jnp.exp(G_last - G)
        s_new = jnp.exp(G_last[:, :, 0, :])[..., None] * s + jnp.einsum('bhjd,bhjv->bhdv', k_end, vc)
        return s_new, o
    s_fin, o = lax.scan(step, s0, (to_chunks(q), to_chunks(k), to_chunks(v), to_chunks(g)))
    o = o.transpose(1, 0, 3, 2, 4).reshape(B, T, H, v.shape[-1])
    return o, s_fin

def gla_mixer(h_ctx, h_lat, need_ctx, w_q, w_k, w_v, w_r, w_gate1, w_gate2, b_gate, g_o, w_o):
    B, C, _ = h_ctx.shape
    S = h_lat.shape[1]
    T = C + S
    h_all = jnp.concatenate([h_ctx, h_lat], axis=1)
    def heads(a, d):
        return a.reshape(B, T, GLA_HEADS, d)
    q = heads(h_all @ w_q, GLA_DK) * (GLA_DK ** -0.5)
    k = heads(h_all @ w_k, GLA_DK)
    v = heads(h_all @ w_v, GLA_DV)
    g_fwd = heads(gla_log_gate(h_all, w_gate1[0], w_gate2[0], b_gate[0]), GLA_DK)
    g_bwd = heads(gla_log_gate(h_all, w_gate1[1], w_gate2[1], b_gate[1]), GLA_DK)
    flip = lambda a: jnp.flip(a, axis=1)
    zeros = jnp.zeros((B, GLA_HEADS, GLA_DK, GLA_DV), jnp.float32)
    qc, kc, vc = q[:, :C], k[:, :C], v[:, :C]
    ql, kl, vl = q[:, C:], k[:, C:], v[:, C:]
    o_cf, s_cf = gla_chunk_scan(qc, kc, vc, g_fwd[:, :C], zeros)
    o_cb, s_cb = gla_chunk_scan(flip(qc), flip(kc), flip(vc), flip(g_bwd[:, :C]), zeros)
    o_lf, _ = gla_chunk_scan(ql, kl, vl, g_fwd[:, C:], s_cf)
    o_lb, _ = gla_chunk_scan(flip(ql), flip(kl), flip(vl), flip(g_bwd[:, C:]), s_cb)
    def out(o, h):
        y = rms_norm(o, g_o).astype(h.dtype).reshape(B, -1, GLA_HEADS * GLA_DV)
        return (y * jax.nn.silu(h @ w_r)) @ w_o
    y_lat = out(o_lf + flip(o_lb), h_lat)
    y_ctx = out(o_cf + flip(o_cb), h_ctx) if need_ctx else None
    return y_ctx, y_lat

def first_inputs(seed: int = 0) -> dict:
    key = jax.random.key(seed)
    ks = jax.random.split(key, 32)
    D = D_MODEL
    n_a = (DEPTH + N_MIXERS - 1) // N_MIXERS
    n_b = DEPTH // N_MIXERS
    def nrm(k, shape, scale):
        return jax.random.normal(k, shape, jnp.float32) * scale
    return {
        'x': nrm(ks[0], (BATCH, SEQ, D), 1.0),
        'c': nrm(ks[1], (BATCH, D), 1.0),
        'ctx': nrm(ks[2], (BATCH, CTX_LEN, D), 1.0),
        'c_ctx': nrm(ks[3], (D,), 1.0),
        'ada_w': nrm(ks[4], (DEPTH, D, N_MOD * D), 0.5 * D ** -0.5),
        'ada_b': nrm(ks[5], (DEPTH, N_MOD * D), 0.02),
        'norm_g': 1.0 + nrm(ks[6], (DEPTH, 4, D), 0.02),
        'mlp_w1': nrm(ks[7], (DEPTH, D, D_FF), D ** -0.5),
        'mlp_w2': nrm(ks[8], (DEPTH, D_FF, D), D_FF ** -0.5),
        'mla_w_dq': nrm(ks[9], (n_a, D, MLA_Q_RANK), D ** -0.5),
        'mla_g_q': 1.0 + nrm(ks[10], (n_a, MLA_Q_RANK), 0.02),
        'mla_w_uq': nrm(ks[11], (n_a, MLA_Q_RANK, MLA_HEADS * (MLA_NOPE + MLA_ROPE)), MLA_Q_RANK ** -0.5),
        'mla_w_dkv': nrm(ks[12], (n_a, D, MLA_KV_RANK + MLA_ROPE), D ** -0.5),
        'mla_g_kv': 1.0 + nrm(ks[13], (n_a, MLA_KV_RANK), 0.02),
        'mla_w_ukv': nrm(ks[14], (n_a, MLA_KV_RANK, MLA_HEADS * (MLA_NOPE + MLA_V)), MLA_KV_RANK ** -0.5),
        'mla_w_o': nrm(ks[15], (n_a, MLA_HEADS * MLA_V, D), (MLA_HEADS * MLA_V) ** -0.5),
        'gla_w_q': nrm(ks[16], (n_b, D, GLA_HEADS * GLA_DK), D ** -0.5),
        'gla_w_k': nrm(ks[17], (n_b, D, GLA_HEADS * GLA_DK), D ** -0.5),
        'gla_w_v': nrm(ks[18], (n_b, D, GLA_HEADS * GLA_DV), D ** -0.5),
        'gla_w_r': nrm(ks[19], (n_b, D, GLA_HEADS * GLA_DV), D ** -0.5),
        'gla_w_gate1': nrm(ks[20], (n_b, 2, D, GLA_GATE_RANK), D ** -0.5),
        'gla_w_gate2': nrm(ks[21], (n_b, 2, GLA_GATE_RANK, GLA_HEADS * GLA_DK), GLA_GATE_RANK ** -0.5),
        'gla_b_gate': nrm(ks[22], (n_b, 2, GLA_HEADS * GLA_DK), 0.1),
        'gla_g_o': 1.0 + nrm(ks[23], (n_b, GLA_DV), 0.02),
        'gla_w_o': nrm(ks[24], (n_b, GLA_HEADS * GLA_DV, D), (GLA_HEADS * GLA_DV) ** -0.5),
    }

def first_block(x, c, ctx, c_ctx, ada_w, ada_b, norm_g, mlp_w1, mlp_w2,
              mla_w_dq, mla_g_q, mla_w_uq, mla_w_dkv, mla_g_kv, mla_w_ukv, mla_w_o,
              gla_w_q, gla_w_k, gla_w_v, gla_w_r, gla_w_gate1, gla_w_gate2, gla_b_gate,
              gla_g_o, gla_w_o):
    B, S, D = x.shape
    rope = axial_rope_tables(S)
    silu_c = jax.nn.silu(c)
    silu_cc = jax.nn.silu(c_ctx)
    x_lat, x_ctx = x, ctx
    for i in range(DEPTH):
        need_ctx = i < DEPTH - 1
        j = i // N_MIXERS
        m_lat = (silu_c @ ada_w[i] + ada_b[i]).reshape(B, N_MOD, 1, D)
        m_ctx = (silu_cc @ ada_w[i] + ada_b[i]).reshape(N_MOD, D)
        h_lat = modulate(rms_norm(x_lat, norm_g[i, 0]), m_lat[:, 0], m_lat[:, 1])
        h_ctx = modulate(rms_norm(x_ctx, norm_g[i, 0]), m_ctx[0], m_ctx[1])
        if i % N_MIXERS == 0:
            y_ctx, y_lat = mla_mixer(h_ctx, h_lat, rope, need_ctx, mla_w_dq[j], mla_g_q[j], mla_w_uq[j],
                                     mla_w_dkv[j], mla_g_kv[j], mla_w_ukv[j], mla_w_o[j])
        else:
            y_ctx, y_lat = gla_mixer(h_ctx, h_lat, need_ctx, gla_w_q[j], gla_w_k[j], gla_w_v[j], gla_w_r[j],
                                     gla_w_gate1[j], gla_w_gate2[j], gla_b_gate[j], gla_g_o[j], gla_w_o[j])
        x_lat = x_lat + m_lat[:, 2] * rms_norm(y_lat, norm_g[i, 1])
        h = modulate(rms_norm(x_lat, norm_g[i, 2]), m_lat[:, 3], m_lat[:, 4])
        x_lat = x_lat + m_lat[:, 5] * rms_norm(sqrelu_mlp(h, mlp_w1[i], mlp_w2[i]), norm_g[i, 3])
        if need_ctx:
            x_ctx = x_ctx + m_ctx[2] * rms_norm(y_ctx, norm_g[i, 1])
            h = modulate(rms_norm(x_ctx, norm_g[i, 2]), m_ctx[3], m_ctx[4])
            x_ctx = x_ctx + m_ctx[5] * rms_norm(sqrelu_mlp(h, mlp_w1[i], mlp_w2[i]), norm_g[i, 3])
    return x_lat


N_MIXERS_2 = 4
DN_ALPHA = (2.0 * DEPTH) ** 0.25
DN_BETA = (8.0 * DEPTH) ** -0.25
LN_EPS = 1e-5

GDN_HEADS = 8
GDN_DK = D_MODEL // GDN_HEADS
GDN_DV = D_MODEL // GDN_HEADS
GDN_CONV = 4
GDN_CHUNK = 64
RET_HEADS = 4
RET_DK = D_MODEL // RET_HEADS
RET_DV = 2 * D_MODEL // RET_HEADS
RET_CHUNK = 128
RET_ROPE_BASE = 10000.0
GMLP_CHUNK = 128
GMLP_WIDTH = 2 * D_MODEL
GMLP_GROUPS = 8
SB_HEADS = 16
SB_DH = D_MODEL // SB_HEADS
SB_BLOCK = 128
FFN_HIDDEN = ((8 * D_MODEL // 3 + 255) // 256) * 256
FFN_CONV = 3


F32 = jnp.float32

def _standardize(x, eps):
    xf = x.astype(F32)
    mu = jnp.mean(xf, axis=-1, keepdims=True)
    xc = xf - mu
    var = jnp.mean(xc * xc, axis=-1, keepdims=True)
    return xc * lax.rsqrt(var + eps)

def layer_norm(x, g, b):
    return (_standardize(x, LN_EPS) * g.astype(F32) + b.astype(F32)).astype(x.dtype)

def _l2norm(x, eps=1e-6):
    return x * lax.rsqrt(jnp.sum(x * x, axis=-1, keepdims=True) + eps)

def causal_dwconv(x, w):
    k_w = w.shape[0]
    s = x.shape[1]
    xp = jnp.pad(x, ((0, 0), (k_w - 1, 0), (0, 0)))
    y = xp[:, k_w - 1:k_w - 1 + s] * w[k_w - 1]
    for j in range(k_w - 1):
        y = y + xp[:, j:j + s] * w[j]
    return y

def _chunk_heads(t, n_heads, chunk):
    b, s, hd = t.shape
    return t.astype(F32).reshape(b, s // chunk, chunk, n_heads, hd // n_heads).transpose(0, 3, 1, 2, 4)

def _unchunk_heads(t):
    b, h, n, c, d = t.shape
    return t.transpose(0, 2, 3, 1, 4).reshape(b, n * c, h, d)

def gated_deltanet(h, w_in, conv_w, a_log, dt_bias, norm_w, w_out):
    H, dk, dv, C = GDN_HEADS, GDN_DK, GDN_DV, GDN_CHUNK
    b_, s, _ = h.shape
    n_qkv = 2 * H * dk + H * dv
    proj = h @ w_in
    qkv, z, a, bt = jnp.split(proj, [n_qkv, n_qkv + H * dv, n_qkv + H * dv + H], axis=-1)
    qkv = jax.nn.silu(causal_dwconv(qkv, conv_w))
    q, k, v = jnp.split(qkv, [H * dk, 2 * H * dk], axis=-1)
    q = _l2norm(_chunk_heads(q, H, C)) * (dk ** -0.5)
    k = _l2norm(_chunk_heads(k, H, C))
    v = _chunk_heads(v, H, C)
    beta = jax.nn.sigmoid(_chunk_heads(bt, H, C)[..., 0])
    g = -jnp.exp(a_log.astype(F32))[:, None, None] * jax.nn.softplus(
        _chunk_heads(a, H, C)[..., 0] + dt_bias.astype(F32)[:, None, None])
    gc = jnp.cumsum(g, axis=-1)
    idx = jnp.arange(C)
    causal = idx[:, None] >= idx[None, :]
    strict = idx[:, None] > idx[None, :]
    diff = gc[..., :, None] - gc[..., None, :]
    decay = jnp.where(causal, jnp.exp(jnp.where(causal, diff, 0.0)), 0.0)
    kb = k * beta[..., None]
    kk = jnp.where(strict, jnp.einsum('bhncd,bhnmd->bhncm', kb, k) * decay, 0.0)
    eye = jnp.eye(C, dtype=F32)
    rhs = jnp.concatenate([v * beta[..., None], kb * jnp.exp(gc)[..., None]], axis=-1)
    sol = lax.linalg.triangular_solve(kk + eye, rhs, left_side=True, lower=True, unit_diagonal=True)
    u, w = sol[..., :dv], sol[..., dv:]
    qk = jnp.where(causal, jnp.einsum('bhncd,bhnmd->bhncm', q, k) * decay, 0.0)

    def step(state, inp):
        q_n, k_n, u_n, w_n, qk_n, g_n = inp
        v_new = u_n - jnp.einsum('bhck,bhkv->bhcv', w_n, state)
        o = (jnp.einsum('bhck,bhkv->bhcv', q_n * jnp.exp(g_n)[..., None], state)
             + jnp.einsum('bhcm,bhmv->bhcv', qk_n, v_new))
        g_last = g_n[..., -1:]
        state = (state * jnp.exp(g_last)[..., None]
                 + jnp.einsum('bhck,bhcv->bhkv', k_n * jnp.exp(g_last - g_n)[..., None], v_new))
        return state, o

    xs = tuple(jnp.moveaxis(t, 2, 0) for t in (q, k, u, w, qk, gc))
    state0 = jnp.zeros((b_, H, dk, dv), F32)
    _, o = lax.scan(step, state0, xs)
    o = _unchunk_heads(jnp.moveaxis(o, 0, 2))
    o = o * lax.rsqrt(jnp.mean(o * o, axis=-1, keepdims=True) + 1e-6) * norm_w.astype(F32)
    o = o * jax.nn.silu(z.astype(F32).reshape(b_, s, H, dv))
    return o.reshape(b_, s, H * dv).astype(h.dtype) @ w_out

def retention(h, w_in, w_out):
    H, dk, dv, C = RET_HEADS, RET_DK, RET_DV, RET_CHUNK
    b_, s, _ = h.shape
    q, k, v, gate = jnp.split(h @ w_in, [H * dk, 2 * H * dk, 2 * H * dk + H * dv], axis=-1)
    pos = jnp.arange(s, dtype=F32)
    inv_freq = RET_ROPE_BASE ** (-jnp.linspace(0.0, 1.0, dk // 2, dtype=F32))
    ang = pos[:, None] * inv_freq[None, :]
    cos_a, sin_a = jnp.cos(ang)[:, None, :], jnp.sin(ang)[:, None, :]

    def rot(t):
        t = t.astype(F32).reshape(b_, s, H, dk)
        t1, t2 = t[..., :dk // 2], t[..., dk // 2:]
        return jnp.concatenate([t1 * cos_a - t2 * sin_a, t1 * sin_a + t2 * cos_a], axis=-1).reshape(b_, s, H * dk)

    q = _chunk_heads(rot(q), H, C)
    k = _chunk_heads(rot(k), H, C) * (dk ** -0.5)
    v = _chunk_heads(v, H, C)
    log_gamma = jnp.log(1.0 - jnp.power(2.0, -5.0 - jnp.arange(H, dtype=F32)))
    idx = jnp.arange(C, dtype=F32)
    rel = idx[:, None] - idx[None, :]
    dmask = jnp.where(rel >= 0, jnp.exp(jnp.maximum(rel, 0.0) * log_gamma[:, None, None]), 0.0)
    scores = jnp.einsum('bhncd,bhnmd->bhncm', q, k) * dmask[None, :, None]
    intra = jnp.einsum('bhncm,bhnmv->bhncv', scores, v)
    zeta = jnp.exp((C - 1.0 - idx)[None, :] * log_gamma[:, None])
    xi = jnp.exp((idx + 1.0)[None, :] * log_gamma[:, None])
    gamma_c = jnp.exp(C * log_gamma)

    def step(state, inp):
        q_n, k_n, v_n = inp
        o = jnp.einsum('bhck,bhkv->bhcv', q_n, state) * xi[None, :, :, None]
        state = (state * gamma_c[None, :, None, None]
                 + jnp.einsum('bhck,bhcv->bhkv', k_n * zeta[None, :, :, None], v_n))
        return state, o

    xs = tuple(jnp.moveaxis(t, 2, 0) for t in (q, k, v))
    _, inter = lax.scan(step, jnp.zeros((b_, H, dk, dv), F32), xs)
    o = _unchunk_heads(intra + jnp.moveaxis(inter, 0, 2))
    o = _standardize(o, 1e-6).reshape(b_, s, H * dv)
    o = o * jax.nn.silu(gate.astype(F32))
    return o.astype(h.dtype) @ w_out

def chunked_gmlp(h, w_in, ln_g, ln_b, w_s, b_s, w_out):
    C, G, W = GMLP_CHUNK, GMLP_GROUPS, GMLP_WIDTH
    b_, s, _ = h.shape
    u, v = jnp.split(jax.nn.gelu(h @ w_in, approximate=False), 2, axis=-1)
    v = layer_norm(v, ln_g, ln_b).reshape(b_, s // C, C, G, W // G)
    causal = jnp.tril(jnp.ones((C, C), dtype=bool))
    ws = jnp.where(causal, w_s, 0.0).astype(v.dtype)
    vs = jnp.einsum('gts,bnsgd->bntgd', ws, v) + b_s.T.astype(v.dtype)[None, None, :, :, None]
    return (u * vs.reshape(b_, s, W)) @ w_out

def stick_breaking(h, w_in, w_out):
    H, dh, T = SB_HEADS, SB_DH, SB_BLOCK
    b_, s, _ = h.shape
    nb = s // T
    q, k, v = jnp.split(h @ w_in, 3, axis=-1)
    q, k, v = (t.reshape(b_, s, H, dh).transpose(0, 2, 1, 3) for t in (q, k, v))
    qb = q.reshape(b_, H, nb, T, dh).transpose(2, 0, 1, 3, 4)
    key_pos = jnp.arange(s)
    scale = dh ** -0.5

    def block(args):
        q_blk, blk = args
        z = jnp.einsum('bhtd,bhsd->bhts', q_blk, k).astype(F32) * scale
        q_pos = blk * T + jnp.arange(T)
        strict = key_pos[None, :] < q_pos[:, None]
        log_1mb = jnp.where(strict, jax.nn.log_sigmoid(-z), 0.0)
        after = lax.cumsum(log_1mb, axis=3, reverse=True) - log_1mb
        a = jnp.where(strict, jnp.exp(jax.nn.log_sigmoid(z) + after), 0.0)
        return jnp.einsum('bhts,bhsd->bhtd', a.astype(v.dtype), v)

    o = lax.map(block, (qb, jnp.arange(nb)))
    o = o.transpose(1, 0, 3, 2, 4).reshape(b_, s, H * dh)
    return o @ w_out

def conv_ffn(h, w_up, conv_w, conv_b, w_down):
    gate, up = jnp.split(h @ w_up, 2, axis=-1)
    gate = causal_dwconv(gate, conv_w) + conv_b
    return (jax.nn.silu(gate) * up) @ w_down

def second_inputs(seed: int = 0) -> dict:
    key = jax.random.key(seed)
    ks = jax.random.split(key, 32)
    D, F = D_MODEL, FFN_HIDDEN

    def nrm(i, shape, scale):
        return jax.random.normal(ks[i], shape, F32) * scale

    gdn_qkv = 2 * GDN_HEADS * GDN_DK + GDN_HEADS * GDN_DV
    gdn_in = gdn_qkv + GDN_HEADS * GDN_DV + 2 * GDN_HEADS
    ret_in = 2 * RET_HEADS * RET_DK + 2 * RET_HEADS * RET_DV
    a_vals = jax.random.uniform(ks[14], (GDN_HEADS,), F32, 1.0, 16.0)
    dt = jnp.exp(jax.random.uniform(ks[15], (GDN_HEADS,), F32, math.log(1e-3), math.log(1e-1)))
    return {
        'x': nrm(0, (BATCH, SEQ, D), 1.0),
        'c': nrm(1, (BATCH, D), 1.0),
        'cond_w': nrm(2, (D, D), D ** -0.5),
        'cond_b': nrm(3, (D,), 0.01),
        'ada_w': nrm(4, (DEPTH, D, 6 * D), 0.1 * D ** -0.5),
        'ada_b': nrm(5, (DEPTH, 6 * D), 0.01),
        'ln_g': 1.0 + nrm(6, (DEPTH, 2, D), 0.02),
        'ln_b': nrm(7, (DEPTH, 2, D), 0.02),
        'ffn_up': nrm(8, (DEPTH, D, 2 * F), D ** -0.5),
        'ffn_conv_w': nrm(9, (DEPTH, FFN_CONV, F), FFN_CONV ** -0.5),
        'ffn_conv_b': nrm(10, (DEPTH, F), 0.01),
        'ffn_down': nrm(11, (DEPTH, F, D), DN_BETA * F ** -0.5),
        'gdn_w_in': nrm(12, (D, gdn_in), D ** -0.5),
        'gdn_conv_w': nrm(13, (GDN_CONV, gdn_qkv), GDN_CONV ** -0.5),
        'gdn_a_log': jnp.log(a_vals),
        'gdn_dt_bias': dt + jnp.log(-jnp.expm1(-dt)),
        'gdn_norm_w': 1.0 + nrm(16, (GDN_DV,), 0.02),
        'gdn_w_out': nrm(17, (GDN_HEADS * GDN_DV, D), DN_BETA * (GDN_HEADS * GDN_DV) ** -0.5),
        'ret_w_in': nrm(18, (D, ret_in), D ** -0.5),
        'ret_w_out': nrm(19, (RET_HEADS * RET_DV, D), DN_BETA * (RET_HEADS * RET_DV) ** -0.5),
        'gmlp_w_in': nrm(20, (D, 2 * GMLP_WIDTH), D ** -0.5),
        'gmlp_ln_g': 1.0 + nrm(21, (GMLP_WIDTH,), 0.02),
        'gmlp_ln_b': nrm(22, (GMLP_WIDTH,), 0.02),
        'gmlp_w_s': nrm(23, (GMLP_GROUPS, GMLP_CHUNK, GMLP_CHUNK), GMLP_CHUNK ** -0.5),
        'gmlp_b_s': 1.0 + nrm(24, (GMLP_GROUPS, GMLP_CHUNK), 0.01),
        'gmlp_w_out': nrm(25, (GMLP_WIDTH, D), DN_BETA * GMLP_WIDTH ** -0.5),
        'sb_w_in': nrm(26, (D, 3 * D), D ** -0.5),
        'sb_w_out': nrm(27, (D, D), DN_BETA * D ** -0.5),
    }

def second_block(x, c, cond_w, cond_b, ada_w, ada_b, ln_g, ln_b, ffn_up, ffn_conv_w, ffn_conv_b, ffn_down,
              gdn_w_in, gdn_conv_w, gdn_a_log, gdn_dt_bias, gdn_norm_w, gdn_w_out,
              ret_w_in, ret_w_out,
              gmlp_w_in, gmlp_ln_g, gmlp_ln_b, gmlp_w_s, gmlp_b_s, gmlp_w_out,
              sb_w_in, sb_w_out):
    mixers = (
        lambda t: gated_deltanet(t, gdn_w_in, gdn_conv_w, gdn_a_log, gdn_dt_bias, gdn_norm_w, gdn_w_out),
        lambda t: retention(t, ret_w_in, ret_w_out),
        lambda t: chunked_gmlp(t, gmlp_w_in, gmlp_ln_g, gmlp_ln_b, gmlp_w_s, gmlp_b_s, gmlp_w_out),
        lambda t: stick_breaking(t, sb_w_in, sb_w_out),
    )
    e = jax.nn.silu(c @ cond_w + cond_b)
    for i in range(DEPTH):
        mod = (e @ ada_w[i] + ada_b[i])[:, None, :]
        sh1, sc1, g1, sh2, sc2, g2 = jnp.split(mod, 6, axis=-1)
        y = mixers[i % N_MIXERS_2](x * (1.0 + sc1) + sh1)
        x = layer_norm(DN_ALPHA * x + (1.0 + g1) * y, ln_g[i, 0], ln_b[i, 0])
        y = conv_ffn(x * (1.0 + sc2) + sh2, ffn_up[i], ffn_conv_w[i], ffn_conv_b[i], ffn_down[i])
        x = layer_norm(DN_ALPHA * x + (1.0 + g2) * y, ln_g[i, 1], ln_b[i, 1])
    return x


def setup_inputs(seed=0):
    out = dict(first_inputs(seed))
    for name, value in second_inputs(seed + 1).items():
        if name != "x":
            out[name + "_2"] = value
    return out


def reference(
    x, c, ctx, c_ctx, ada_w, ada_b, norm_g, mlp_w1, mlp_w2, mla_w_dq, mla_g_q, mla_w_uq,
    mla_w_dkv, mla_g_kv, mla_w_ukv, mla_w_o, gla_w_q, gla_w_k, gla_w_v, gla_w_r, gla_w_gate1,
    gla_w_gate2, gla_b_gate, gla_g_o, gla_w_o, c_2, cond_w_2, cond_b_2, ada_w_2, ada_b_2,
    ln_g_2, ln_b_2, ffn_up_2, ffn_conv_w_2, ffn_conv_b_2, ffn_down_2, gdn_w_in_2, gdn_conv_w_2,
    gdn_a_log_2, gdn_dt_bias_2, gdn_norm_w_2, gdn_w_out_2, ret_w_in_2, ret_w_out_2, gmlp_w_in_2,
    gmlp_ln_g_2, gmlp_ln_b_2, gmlp_w_s_2, gmlp_b_s_2, gmlp_w_out_2, sb_w_in_2, sb_w_out_2,
):
    x = first_block(
        x, c, ctx, c_ctx, ada_w, ada_b, norm_g, mlp_w1, mlp_w2, mla_w_dq, mla_g_q, mla_w_uq,
        mla_w_dkv, mla_g_kv, mla_w_ukv, mla_w_o, gla_w_q, gla_w_k, gla_w_v, gla_w_r,
        gla_w_gate1, gla_w_gate2, gla_b_gate, gla_g_o, gla_w_o,
    )
    return second_block(
        x, c_2, cond_w_2, cond_b_2, ada_w_2, ada_b_2, ln_g_2, ln_b_2, ffn_up_2, ffn_conv_w_2,
        ffn_conv_b_2, ffn_down_2, gdn_w_in_2, gdn_conv_w_2, gdn_a_log_2, gdn_dt_bias_2,
        gdn_norm_w_2, gdn_w_out_2, ret_w_in_2, ret_w_out_2, gmlp_w_in_2, gmlp_ln_g_2,
        gmlp_ln_b_2, gmlp_w_s_2, gmlp_b_s_2, gmlp_w_out_2, sb_w_in_2, sb_w_out_2,
    )


_drawn_inputs = setup_inputs


def setup_inputs(seed=0):
    import zlib

    import numpy as np

    out = dict(_drawn_inputs(seed))
    spreads = {}
    factors = {'mla_g_q': 8.0,
     'mla_g_kv': 5.35,
     'gla_b_gate': 3.069,
     'gla_g_o': 51.139,
     'cond_b_2': 34.928,
     'ada_b_2': 4.539,
     'ffn_conv_b_2': 8.0,
     'gdn_norm_w_2': 21.352}
    for name, (base, spread) in spreads.items():
        noise = np.random.default_rng([zlib.crc32(name.encode()), seed]).standard_normal(out[name].shape)
        drawn = base * np.exp(spread * noise) if base else spread * noise
        out[name] = jnp.asarray(drawn.astype(out[name].dtype))
    for name, factor in factors.items():
        out[name] = (out[name] * factor).astype(out[name].dtype)
    return out
```

```python
import numpy as np
import concourse.bass as bass
from concourse import mybir
from contextlib import ExitStack

ACT = mybir.ActivationFunctionType
ALU = mybir.AluOpType
F32 = mybir.dt.float32
U32 = mybir.dt.uint32
XY = mybir.AxisListType.XY

P = 128
D = 1024
DB = D // P
CTX, SEQ = 256, 512
T = CTX + SEQ
HALF = T // 2
FF = 4096
FFB = FF // P
HID = 2816
HIDB = HID // P
MLA_H, NOPE, ROPE, Q_RANK, KV_RANK = 8, 128, 64, 384, 256
GLA_H, GLA_DV, GATE_RANK = 4, 256, 16
GDN_H = 8
RET_H, RET_DV = 4, 512
ALPHA = (2.0 * 2) ** 0.25
QT, KT = T // P, T // P
LT = SEQ // P
LEVELS = [1, 2, 4, 8, 16, 32, 64]

VEC = {}
_rows = 0
for _name, _n in [
    ("ada_b", 96), ("c", 8), ("c_ctx", 8), ("c_2", 8), ("cond_b", 8),
    ("ada_b_2", 96), ("ln_g_2", 32),
    ("norm_g", 64), ("ln_b_2", 32), ("mla_g_q", 3), ("mla_g_kv", 2), ("gla_b_gate", 8), ("gla_g_o", 2),
    ("gdn_norm_w", 1), ("pad", 16),
    ("conv_w0", 66), ("conv_b", 44), ("pad2", 18),
    ("conv_w1", 66), ("pad3", 62),
    ("gdn_conv_w", 96), ("pad4", 32),
]:
    VEC[_name] = (_rows // P, _rows % P, _n)
    _rows += _n
VEC_TILES = _rows // P

STAGES = [
    ("cond", 1, 2, 0), ("ada0", 6, 2, 0), ("ada1", 6, 2, 0), ("ada2", 6, 2, 0), ("ada3", 6, 2, 0),
    ("mla_in", 1, 2, 6), ("mla_rope", 1, 0, 2), ("mla_pair", 4, 2, 34), ("mla_out", 1, 2, 8),
    ("mlp0_up", 4, 2, 8), ("mlp0_down", 4, 2, 2),
    ("gla_gate", 1, 0, 2), ("gla_head", 4, 4, 18), ("gla_out", 1, 2, 8),
    ("mlp1_up", 4, 2, 8), ("mlp1_down", 4, 2, 2),
    ("gdn_gate", 1, 0, 2), ("gdn_pair", 4, 4, 50), ("gdn_out", 1, 2, 8),
    ("ffn0_up", 11, 2, 2), ("ffn0_down", 4, 2, 2),
    ("ret_head", 4, 4, 12), ("ret_out", 1, 4, 8),
    ("ffn1_up", 11, 2, 2), ("ffn1_down", 4, 2, 2),
]
GROUP0, UNIT0, GROUPS, UNITS = {}, {}, {}, {}
_g = _u = 0
for _s, _n, _gi, _ui in STAGES:
    GROUP0[_s], UNIT0[_s], GROUPS[_s], UNITS[_s] = _g, _u, _gi, _ui
    _g, _u = _g + _n * _gi, _u + _n * _ui
    assert _gi % 2 == 0 and _ui % 2 == 0

NORMS = {}
_b = 0
for _k, (_s, _n) in enumerate([
    ("h0", 8), ("cq", 3), ("ckv", 2), ("y0", 8), ("h0m", 8), ("y0m", 8),
    ("h1", 8), ("y1", 8), ("h1m", 8), ("y1m", 8),
    ("ln0", 8), ("ln0f", 8), ("ln1", 8), ("ln1f", 8),
]):
    NORMS[_s] = (_k, _b, _n)
    _b += _n


class Steps:

    def __init__(self, eng, sem):
        self.eng, self.sem, self.n, self.it, self.per, self.local = eng, sem, 0, None, 0, 0

    def did(self, ins):
        ins.then_inc(self.sem, 1)
        if self.it is None:
            self.n += 1
        else:
            self.local += 1

    def settle(self):
        v = self.n if self.it is None else self.it * self.per + (self.n + self.local)
        self.eng.wait_ge(self.sem, v)

    def enter(self, it, per):
        self.it, self.per, self.local = it, per, 0

    def leave(self, iterations):
        assert self.local == self.per, (self.local, self.per)
        self.n, self.it = self.n + iterations * self.per, None


def first_and_second_block(nc, A, out):
    ctx = ExitStack()
    with ctx:
        def sb(name, shape, dt=F32):
            return ctx.enter_context(nc.sbuf_tensor(name, shape, dt))

        def sem(name):
            return ctx.enter_context(nc.semaphore(name))

        xT = sb("xT", [P, DB, T])
        hT = sb("hT", [P, DB, T])
        arena = sb("arena", [P, FFB * T])
        wring = [sb(f"wring{s}", [P, 4096]) for s in range(2)]
        base_tab = sb("base_tab", [P, 2 * P])
        ident, ones = base_tab[:, 0:P], base_tab[:, P:2 * P]
        tab = sb("tab", [P, 1664])
        cols = sb("cols", [P, VEC_TILES, P])
        cs = sb("cs", [P, DB, 4])
        mod = sb("mod", [P, 4, 48, 2])
        dcol = sb("dcol", [P, 4, 4, DB, 2])
        eps = sb("eps", [P, 2])
        sq = sb("sq", [P, 2, T])
        rstd = sb("rstd", [P, T])
        gate1 = sb("gate1", [P, DB, 2, GATE_RANK])
        gate2 = sb("gate2", [GATE_RANK, 2, P])
        w_ab = sb("w_ab", [P, DB, 16])
        a_dt = sb("a_dt", [GDN_H, 3])
        d_row = sb("d_row", [GDN_H, 2, SEQ])
        d_col = sb("d_col", [P, 5, LT, GDN_H])
        acc = ctx.enter_context(nc.psum_tensor("acc", [P, 2, 2, 512], F32))
        sc = ctx.enter_context(nc.psum_tensor("sc", [P, 2, 2, 512], F32))

        at = [0]

        def carve(*shape):
            n = int(np.prod(shape))
            a = arena[:, at[0]:at[0] + n]
            at[0] += n
            assert at[0] <= FFB * T, at[0]
            if len(shape) == 1:
                return a
            names = " ".join(f"a{i}" for i in range(len(shape)))
            return a.rearrange(f"p ({names}) -> p {names}", **{f"a{i}": s for i, s in enumerate(shape)})

        x_tok = carve(QT, D)
        vrow = carve(VEC_TILES, P)
        at[0] = 0
        o_tok = carve(LT, D)
        at[0] = 0
        hid = carve(FFB, T)
        relu = sq
        at[0] = 0
        hid2 = carve(HIDB, SEQ)
        gpad = carve(2, SEQ + 2)
        gconv = carve(2, SEQ)
        gsilu = carve(2, SEQ)
        at[0] = 0
        cq = carve(3, T)
        ckv = carve(2, T)
        krope = carve(2, T)
        kraw = carve(T)
        ktmp = carve(SEQ)
        qn = carve(2, T)
        qr = carve(T)
        qraw = carve(T)
        kn = carve(2, T)
        vtok = carve(QT, 256)
        prob = carve(2, T)
        probT = carve(2, T)
        attn = carve(MLA_H, T)
        small = carve(2, 4)
        at[0] = 0
        hgate = carve(2, T)
        g_q = carve(SEQ)
        g_k = carve(T)
        g_v = carve(QT, GLA_DV)
        g_r = carve(2, SEQ)
        g_zl = carve(2, T)
        g_z, g_l = g_zl[:, 0, :], g_zl[:, 1, :]
        g_o = g_zl[:, :, 0:SEQ]
        g_g = carve(T)
        g_G = carve(T)
        g_tot = carve(2, 12)
        g_et = carve(2, 12)
        g_dec = carve(2, QT)
        g_qt = carve(2, SEQ)
        g_kt = carve(2, SEQ)
        g_ke = carve(2, T)
        g_qS = carve(2, SEQ)
        g_kE = carve(2, T)
        g_kEt = carve(2, 5 * P)
        g_AT = carve(2, SEQ)
        g_S = carve(2, 5, GLA_DV)
        g_out = carve(DB, SEQ)
        at[0] = 0
        d_cp = carve(2, 2, SEQ + 3)
        d_q = carve(2, SEQ)
        d_k = carve(2, SEQ)
        d_v = carve(2, SEQ)
        d_z = carve(2, SEQ)
        d_gcR = carve(2, SEQ)
        d_o = d_gcR
        d_bR = carve(2, SEQ)
        d_ET = carve(2, SEQ)
        d_LT = carve(2, SEQ)
        d_Lm = carve(2, 2, SEQ)
        d_T = carve(2, SEQ)
        d_U = carve(2, SEQ)
        d_Y = carve(2, SEQ)
        d_QK = carve(2, SEQ)
        d_kend = carve(2, SEQ)
        d_V = carve(2, SEQ)
        d_qE = carve(2, SEQ)
        d_S = carve(2, P)
        d_r = carve(2, P)
        d_vn = carve(2, P)
        d_out = carve(GDN_H, SEQ)
        at[0] = 0
        r_tab = carve(6, SEQ)
        r_raw = carve(2, 2, SEQ)
        r_sqr = r_raw.rearrange("p a b n -> p (a b) n")
        r_tmp = carve(2, SEQ)
        r_rot = carve(2, 2, SEQ)
        r_v = carve(LT, RET_DV)
        r_gate = carve(4, SEQ)
        r_s = carve(LT, SEQ)
        r_o = carve(4, SEQ)
        r_out = carve(16, SEQ)

        rot2, dup, rotdup = tab[:, 0:P], tab[0:64, P:2 * P], tab[0:64, 2 * P:3 * P]
        rcos, rsin = tab[:, 384:384 + SEQ], tab[:, 896:896 + SEQ]
        keep64, tri_fb = tab[:, 0:T], tab[:, T:T + 2 * P]
        lvl_mask = [tab[:, l * P:(l + 1) * P] for l in range(7)]
        causal, last_row, keep128 = tab[:, 896:1024], tab[:, 1024:1152], tab[:, 1152:1664]

        const_in = sem("const_in")
        x_in = sem("x_in")
        gate1_in, ab_in = sem("gate1_in"), sem("ab_in")
        tab_in, rtab_in = sem("tab_in"), sem("rtab_in")
        gate2_in = sem("gate2_in")
        out_done = sem("out_done")
        w_loaded = [sem(f"w_loaded{s}") for s in range(2)]
        w_used = sem("w_used")
        acc_ready = sem("acc_ready")
        acc_free = [sem(f"acc_free{s}") for s in range(2)]
        dve_step, act_step = sem("dve_step"), sem("act_step")
        vec_turned, cols_ready = sem("vec_turned"), sem("cols_ready")
        x_turned, x_moved = sem("x_turned"), sem("x_moved")
        c_ready, cond_done, e_ready = sem("c_ready"), sem("cond_done"), sem("e_ready")
        ada_done, mod_ready = sem("ada_done"), sem("mod_ready")
        x_ready = sem("x_ready")
        n_sq, n_used = sem("n_sq"), sem("n_used")
        n_std = sem("n_std")
        n_mul, h_ready = sem("n_mul"), sem("h_ready")
        n_mean, n_cent = sem("n_mean"), sem("n_cent")
        lat_ready, krope_ready = sem("lat_ready"), sem("krope_ready")
        qrope_ready, s_ready = sem("qrope_ready"), sem("s_ready")
        p_max, p_exp, p_ready = sem("p_max"), sem("p_exp"), sem("p_ready")
        relu_free = sem("relu_free")
        gl_ready, gG_ready, gE_ready = sem("gl_ready"), sem("gG_ready"), sem("gE_ready")
        gk_ready, gsq_ready = sem("gk_ready"), sem("gsq_ready")
        g_done = sem("g_done")
        d_rows, d_cols, d_ga, d_gc = sem("d_rows"), sem("d_cols"), sem("d_ga"), sem("d_gc")
        d_masked, d_conv, d_silu = sem("d_masked"), sem("d_conv"), sem("d_silu")
        d_sq, d_std, d_norm, d_diff = sem("d_sq"), sem("d_std"), sem("d_norm"), sem("d_diff")
        d_exp, d_lt, d_lm, d_qe = sem("d_exp"), sem("d_lt"), sem("d_lm"), sem("d_qe")
        d_init, d_rr, d_done, d_glr = sem("d_init"), sem("d_rr"), sem("d_done"), sem("d_glr")
        f_conv, f_silu = sem("f_conv"), sem("f_silu")
        r_rotd, r_cent, r_sq, r_done = sem("r_rotd"), sem("r_cent"), sem("r_sq"), sem("r_done")
        o_turned, o_moved = sem("o_turned"), sem("o_moved")

        def unit(stage, j):
            return acc[:, (UNIT0[stage] + j) % 2]

        def flat(a):
            return a.rearrange("p a n -> p (a n)")

        def halves(a):
            return a.rearrange("p (h n) -> p h n", h=2)

        def chunks(a):
            return a.rearrange("p e (c n) -> p (e c) n", n=P)

        def loaded(eng, stage, it, j):
            g = GROUP0[stage] + j
            eng.wait_ge(w_loaded[g % 2], 16 * (g // 2 + 1) + it * (8 * GROUPS[stage]))
            return g % 2

        def finished(eng, stage, it, j):
            eng.wait_ge(acc_ready, UNIT0[stage] + j + 1 + it * UNITS[stage])

        def emptied(eng, stage, it, j):
            u = UNIT0[stage] + j
            eng.wait_ge(acc_free[u % 2], u // 2 + 1 + it * (UNITS[stage] // 2))

        def claim(eng, stage, it, j):
            u = UNIT0[stage] + j
            if u >= 2:
                eng.wait_ge(acc_free[u % 2], u // 2 + it * (UNITS[stage] // 2))

        def free(ins, stage, j):
            ins.then_inc(acc_free[(UNIT0[stage] + j) % 2], 1)

        def col(name, i):
            t, r, _ = VEC[name]
            return cols[:, t, r + i:r + i + 1]

        def vec(name, i, n):
            t, r, _ = VEC[name]
            return cols[:, t, r + i:r + i + n]

        def dyncol(name, i):
            t, r, _ = VEC[name]
            return cols[:, t, bass.ds(i + r, 1)]

        rows = lambda a: a.rearrange("(r p) -> r p", p=P)
        rows2 = lambda a: a.rearrange("l (r p) -> (l r) p", p=P)
        rows3 = lambda a: a.rearrange("l i (r p) -> (l i r) p", p=P)
        vec_sources = [
            ("ada_b", rows2(A["ada_b"])), ("c", rows2(A["c"])), ("c_ctx", rows(A["c_ctx"])), ("c_2", rows2(A["c_2"])),
            ("cond_b", rows(A["cond_b_2"])), ("ada_b_2", rows2(A["ada_b_2"])), ("ln_g_2", rows3(A["ln_g_2"])),
            ("norm_g", rows3(A["norm_g"])), ("ln_b_2", rows3(A["ln_b_2"])), ("mla_g_q", rows2(A["mla_g_q"])),
            ("mla_g_kv", rows2(A["mla_g_kv"])), ("gla_b_gate", rows3(A["gla_b_gate"])), ("gla_g_o", rows2(A["gla_g_o"])),
            ("gdn_norm_w", rows(A["gdn_norm_w_2"])), ("conv_w0", rows2(A["ffn_conv_w_2"][0])),
            ("conv_b", rows2(A["ffn_conv_b_2"])), ("conv_w1", rows2(A["ffn_conv_w_2"][1])),
            ("gdn_conv_w", rows2(A["gdn_conv_w_2"])),
        ]
        consts = 16 * (1 + len(vec_sources))
        vec_rows = [max(VEC[n][1] + VEC[n][2] for n, _ in vec_sources if VEC[n][0] == t) for t in range(VEC_TILES)]

        block = ctx.enter_context(nc.Block())

        @block.sync
        def _(sp):
            def slot_free(stage, it, j):
                g = GROUP0[stage] + j
                if g >= 2:
                    sp.wait_ge(w_used, g + it * GROUPS[stage])
                return g % 2

            def load(stage, it, j, src, k, n):
                s = slot_free(stage, it, j)
                dst = wring[s][:, 0:k * n].rearrange("p (k n) -> p k n", k=k)
                sp.dma_start(dst, src).then_inc(w_loaded[s], 16)

            def blocks(w):
                return w.rearrange("(k p) n -> p k n", p=P)

            cw = blocks(A["cond_w_2"])
            for j in range(2):
                load("cond", 0, j, cw[:, :, j * 512:(j + 1) * 512], DB, 512)
            for l in range(4):
                aw = blocks(A["ada_w" if l < 2 else "ada_w_2"][l % 2])
                with sp.Fori(0, 6) as it:
                    for j in range(2):
                        load(f"ada{l}", it, j, aw[:, :, bass.ds(it * 1024 + j * 512, 512)], DB, 512)

            def in_columns(stage, w, n, k):
                wv, its = blocks(w), w.shape[1] // n // 2
                if dict((s, i) for s, i, _, _ in STAGES)[stage] == 1:
                    for j in range(2 * its):
                        load(stage, 0, j, wv[:, :, j * n:(j + 1) * n], k, n)
                    return
                with sp.Fori(0, its) as it:
                    for j in range(2):
                        load(stage, it, j, wv[:, :, bass.ds(it * (2 * n) + j * n, n)], k, n)

            load("mla_in", 0, 0, blocks(A["mla_w_dq"][0]), DB, Q_RANK)
            load("mla_in", 0, 1, blocks(A["mla_w_dkv"][0]), DB, KV_RANK + ROPE)
            uq, ukv = blocks(A["mla_w_uq"][0]), blocks(A["mla_w_ukv"][0])
            with sp.Fori(0, MLA_H // 2) as it:
                load("mla_pair", it, 0, uq[:, :, bass.ds(it * 384, 384)], 3, 384)
                load("mla_pair", it, 1, ukv[:, :, bass.ds(it * 512, 512)], 2, 512)
            in_columns("mla_out", A["mla_w_o"][0], 512, DB)
            in_columns("mlp0_up", A["mlp_w1"][0], 512, DB)
            in_columns("mlp0_down", A["mlp_w2"][0], P, FFB)
            gq, gk, gv, gr = (blocks(A[n][0]) for n in ("gla_w_q", "gla_w_k", "gla_w_v", "gla_w_r"))
            w2 = A["gla_w_gate2"][0].rearrange("d r n -> r d n")
            with sp.Fori(0, GLA_H) as it:
                sp.wait_ge(acc_ready, UNIT0["gla_head"] - UNITS["gla_head"] + 8 + it * UNITS["gla_head"])
                sp.dma_start(gate2[:, :, :], w2[:, :, bass.ds(it * P, P)]).then_inc(gate2_in, 16)
                load("gla_head", it, 0, gq[:, :, bass.ds(it * P, P)], DB, P)
                load("gla_head", it, 1, gk[:, :, bass.ds(it * P, P)], DB, P)
                load("gla_head", it, 2, gv[:, :, bass.ds(it * GLA_DV, GLA_DV)], DB, GLA_DV)
                load("gla_head", it, 3, gr[:, :, bass.ds(it * GLA_DV, GLA_DV)], DB, GLA_DV)
            in_columns("gla_out", A["gla_w_o"][0], 512, DB)
            in_columns("mlp1_up", A["mlp_w1"][1], 512, DB)
            in_columns("mlp1_down", A["mlp_w2"][1], P, FFB)
            gi = blocks(A["gdn_w_in_2"])
            with sp.Fori(0, GDN_H // 2) as it:
                for j in range(4):
                    load("gdn_pair", it, j, gi[:, :, bass.ds(it * 256 + j * D, 256)], DB, 256)
            in_columns("gdn_out", A["gdn_w_out_2"], 512, DB)

            def ffn(i):
                up = blocks(A["ffn_up_2"][i])
                with sp.Fori(0, HIDB // 2) as it:
                    for j in range(2):
                        load(f"ffn{i}_up", it, j, up[:, :, bass.ds(it * 256 + j * HID, 256)], DB, 256)
                in_columns(f"ffn{i}_down", A["ffn_down_2"][i], P, HIDB)

            ffn(0)
            ri = blocks(A["ret_w_in_2"])
            with sp.Fori(0, RET_H) as it:
                load("ret_head", it, 0, ri[:, :, bass.ds(it * 256, 256)], DB, 256)
                load("ret_head", it, 1, ri[:, :, bass.ds(it * 256 + D, 256)], DB, 256)
                load("ret_head", it, 2, ri[:, :, bass.ds(it * 512 + 2 * D, 512)], DB, 512)
                load("ret_head", it, 3, ri[:, :, bass.ds(it * 512 + 4 * D, 512)], DB, 512)
            ro = blocks(A["ret_w_out_2"])
            for j in range(4):
                load("ret_out", 0, j, ro[:, :, j * 256:(j + 1) * 256], 16, 256)
            ffn(1)
            for t in range(LT):
                sp.wait_ge(o_moved, t + 1)
                sp.dma_start(out[0, t * P:(t + 1) * P, :], o_tok[:, t, :]).then_inc(out_done, 16)
            sp.wait_ge(out_done, 16 * LT)

        @block.tensor
        def _(pe):
            def group(stage, it, j, k, n):
                s = loaded(pe, stage, it, j)
                begun[0] = True
                return wring[s][:, 0:k * n].rearrange("p (k n) -> p k n", k=k)

            begun = [False]

            def mm(o, lhsT, rhs, start, stop):
                ins = pe.matmul(o, lhsT, rhs, start=start, stop=stop)
                if begun[0]:
                    ins.then_inc(w_used, 1)
                    begun[0] = False
                return ins

            def linear(u, w, m, x, n, nk, rows=P, at=0):
                for k in range(nk):
                    if n == T:
                        for h in range(2):
                            last = mm(u[at:at + rows, h, 0:HALF], w[:, k, m:m + rows],
                                      x(k)[:, h * HALF:(h + 1) * HALF], k == 0, k == nk - 1)
                    else:
                        last = mm(u[at:at + rows, 0, 0:n], w[:, k, m:m + rows], x(k), k == 0, k == nk - 1)
                return last

            def square_sum(name, n):
                _, b0, nb = NORMS[name]
                for b in range(nb):
                    pe.wait_ge(n_sq, b0 + b + 1)
                    s = sq[:, (b0 + b) % 2]
                    if n == T:
                        for h in range(2):
                            last = pe.matmul(sc[:, 0, h, 0:HALF], ones, s[:, h * HALF:(h + 1) * HALF],
                                             start=b == 0, stop=b == nb - 1)
                    else:
                        last = pe.matmul(sc[:, 0, 0, 0:n], ones, s[:, 0:n], start=b == 0, stop=b == nb - 1)
                    last.then_inc(n_used, 1)

            def mean_sum(stage):
                for b in range(DB):
                    emptied(pe, stage, *divmod(b, UNITS[stage]))
                    last = pe.matmul(sc[:, 0, 1, :], ones, xT[:, b, CTX:T], start=b == 0, stop=b == DB - 1)
                last.then_inc(n_mean, 1)

            seq_h = lambda k: hT[:, k, CTX:T]
            all_h = lambda k: hT[:, k, :]

            pe.wait_ge(const_in, consts)
            for t in range(VEC_TILES):
                n = vec_rows[t]
                last = pe.transpose(flat(acc[:, 0])[:, t * P:t * P + n], vrow[0:n, t, :], ident[0:n, 0:n])
            last.then_inc(vec_turned, 1)
            pe.wait_ge(x_in, 32)
            for b in range(DB):
                if b >= 2:
                    pe.wait_ge(x_moved, b - 1)
                for t in range(QT):
                    last = pe.transpose(flat(sc[:, b % 2])[:, t * P:(t + 1) * P],
                                        x_tok[:, t, b * P:(b + 1) * P], ident)
                last.then_inc(x_turned, 1)
            pe.wait_ge(c_ready, 1)
            pe.wait_ge(x_moved, DB)
            for j in range(2):
                w = group("cond", 0, j, DB, 512)
                for m in range(4):
                    for k in range(DB):
                        last = mm(sc[:, 1, 0, 4 * j + m:4 * j + m + 1], w[:, k, m * P:(m + 1) * P],
                                  vec("c_2", k, 1), k == 0, k == DB - 1)
            last.then_inc(cond_done, 1)
            for l in range(4):
                if l == 2:
                    pe.wait_ge(e_ready, 1)
                first = 2 * (l // 2)
                with pe.Fori(0, 6) as it:
                    for j in range(2):
                        w = group(f"ada{l}", it, j, DB, 512)
                        for m in range(4):
                            for k in range(DB):
                                last = mm(sc[:, 1, 1, bass.ds(it * 16 + (l * 96 + (4 * j + m) * 2), 2)],
                                          w[:, k, m * P:(m + 1) * P], cs[:, k, first:first + 2],
                                          k == 0, k == DB - 1)
                    last.then_inc(ada_done, 1)

            square_sum("h0", T)
            pe.wait_ge(h_ready, 8)
            w = group("mla_in", 0, 0, DB, Q_RANK)
            for j in range(6):
                if j == 3:
                    w = group("mla_in", 0, 1, DB, KV_RANK + ROPE)
                claim(pe, "mla_in", 0, j)
                linear(unit("mla_in", j), w, (j % 3) * P, all_h, T, DB,
                       rows=P if j < 5 else ROPE).then_inc(acc_ready, 1)
            emptied(pe, "mla_in", 0, 5)
            pe.wait_ge(tab_in, 16)
            claim(pe, "mla_rope", 0, 0)
            for h in range(2):
                last = pe.matmul(unit("mla_rope", 0)[:, h, 0:HALF], dup, kraw[0:64, h * HALF:(h + 1) * HALF],
                                 start=True, stop=True)
            last.then_inc(acc_ready, 1)
            claim(pe, "mla_rope", 0, 1)
            pe.matmul(unit("mla_rope", 1)[:, 0, :], rotdup, kraw[0:64, CTX:T], start=True,
                      stop=True).then_inc(acc_ready, 1)
            square_sum("cq", T)
            square_sum("ckv", T)
            pe.wait_ge(lat_ready, 5)
            pe.wait_ge(krope_ready, 1)
            S = "mla_pair"
            with pe.Fori(0, MLA_H // 2) as it:
                wq = group(S, it, 0, 3, 384)
                for j, m in ((0, 0), (1, 192)):
                    claim(pe, S, it, j)
                    linear(unit(S, j), wq, m, lambda k: cq[:, k, :], T, 3).then_inc(acc_ready, 1)
                claim(pe, S, it, 2)
                linear(unit(S, 2), wq, 128, lambda k: cq[:, k, :], T, 3, rows=64)
                linear(unit(S, 2), wq, 320, lambda k: cq[:, k, :], T, 3, rows=64, at=64).then_inc(acc_ready, 1)
                wkv = group(S, it, 1, 2, 512)
                for j, m in ((3, 0), (4, 256)):
                    claim(pe, S, it, j)
                    linear(unit(S, j), wkv, m, lambda k: ckv[:, k, :], T, 2).then_inc(acc_ready, 1)
                wv = wkv.rearrange("p k (h s n) -> p k h s n", h=2, s=2)
                for j in range(3):
                    claim(pe, S, it, 5 + j)
                    for i in range(2):
                        t = 2 * j + i
                        for k in range(2):
                            last = mm(unit(S, 5 + j)[:, i, 0:256], ckv[:, k, t * P:(t + 1) * P],
                                      wv[:, k, :, 1, :], k == 0, k == 1)
                    last.then_inc(acc_ready, 1)
                emptied(pe, S, it, 2)
                for j in range(2):
                    claim(pe, S, it, 8 + j)
                    pe.matmul(unit(S, 8 + j)[:, 0, 0:256], rot2, qraw[:, CTX + 256 * j:CTX + 256 * (j + 1)],
                              start=True, stop=True).then_inc(acc_ready, 1)
                pe.wait_ge(qrope_ready, it * 1 + 1)

                def scores(n):
                    e, t = n // QT, n % QT
                    spans = [(0, 0, CTX)] if t < 2 else [(h, h * HALF, HALF) for h in range(2)]
                    for h, k0, w in spans:
                        pe.matmul(sc[:, n % 2, h, 0:w], qn[:, e, t * P:(t + 1) * P], kn[:, e, k0:k0 + w],
                                  start=True, stop=False)
                        last = pe.matmul(sc[:, n % 2, h, 0:w], qr[:, t * P:(t + 1) * P], krope[:, e, k0:k0 + w],
                                         start=False, stop=True)
                    last.then_inc(s_ready, 1)

                def weigh(n):
                    e, t = n // QT, n % QT
                    nk = 2 if t < 2 else KT
                    pe.wait_ge(p_ready, it * 12 + n + 1)
                    claim(pe, S, it, 10 + 2 * n)
                    for k in range(nk):
                        last = pe.transpose(flat(unit(S, 10 + 2 * n))[:, k * P:(k + 1) * P],
                                            prob[:, n % 2, k * P:(k + 1) * P], ident)
                    last.then_inc(acc_ready, 1)
                    emptied(pe, S, it, 10 + 2 * n)
                    claim(pe, S, it, 11 + 2 * n)
                    for k in range(nk):
                        last = pe.matmul(unit(S, 11 + 2 * n)[:, 0, 0:P], vtok[:, k, e * P:(e + 1) * P],
                                         probT[:, n % 2, k * P:(k + 1) * P], start=k == 0, stop=k == nk - 1)
                    last.then_inc(acc_ready, 1)

                scores(0)
                for n in range(2 * QT):
                    if n + 1 < 2 * QT:
                        scores(n + 1)
                    weigh(n)

            def out_proj(stage, x, n, nk, per):
                for j in range(8):
                    if j % per == 0:
                        w = group(stage, 0, j // per, nk, per * P)
                    claim(pe, stage, 0, j)
                    linear(unit(stage, j), w, (j % per) * P, x, n, nk).then_inc(acc_ready, 1)

            emptied(pe, "mla_pair", 3, 33)
            out_proj("mla_out", lambda k: attn[:, k, :], T, DB, 4)

            def mlp(i, n, x, h):
                up, down = f"mlp{i}_up", f"mlp{i}_down"
                with pe.Fori(0, 4) as it:
                    for j in range(8):
                        if j % 4 == 0:
                            w = group(up, it, j // 4, DB, 512)
                        claim(pe, up, it, j)
                        linear(unit(up, j), w, (j % 4) * P, x, n, DB).then_inc(acc_ready, 1)
                pe.wait_ge(relu_free, 32 * (i + 1) + 2)
                with pe.Fori(0, 4) as it:
                    for j in range(2):
                        w = group(down, it, j, FFB, P)
                        claim(pe, down, it, j)
                        linear(unit(down, j), w, 0, h, n, FFB).then_inc(acc_ready, 1)

            square_sum("y0", T)
            square_sum("h0m", T)
            pe.wait_ge(h_ready, 16)
            mlp(0, T, all_h, lambda k: hid[:, k, :])
            square_sum("y0m", T)

            square_sum("h1", T)
            pe.wait_ge(h_ready, 24)
            pe.wait_ge(gate1_in, 16 * 2)
            for d in range(2):
                claim(pe, "gla_gate", 0, d)
                linear(unit("gla_gate", d), gate1[:, :, d, :], 0, all_h, T, DB,
                       rows=GATE_RANK).then_inc(acc_ready, 1)
            emptied(pe, "gla_gate", 0, 1)
            S = "gla_head"
            with pe.Fori(0, GLA_H) as it:
                w = group(S, it, 0, DB, P)
                claim(pe, S, it, 0)
                linear(unit(S, 0), w, 0, seq_h, SEQ, DB).then_inc(acc_ready, 1)
                w = group(S, it, 1, DB, P)
                claim(pe, S, it, 1)
                linear(unit(S, 1), w, 0, all_h, T, DB).then_inc(acc_ready, 1)
                w = group(S, it, 2, DB, GLA_DV)
                for j in range(3):
                    claim(pe, S, it, 2 + j)
                    for i in range(2):
                        t = 2 * j + i
                        for k in range(DB):
                            last = mm(unit(S, 2 + j)[:, i, 0:GLA_DV], hT[:, k, t * P:(t + 1) * P], w[:, k, :],
                                      k == 0, k == DB - 1)
                    last.then_inc(acc_ready, 1)
                w = group(S, it, 3, DB, GLA_DV)
                claim(pe, S, it, 5)
                for b in range(2):
                    for k in range(DB):
                        last = mm(unit(S, 5)[:, b, :], w[:, k, b * P:(b + 1) * P], seq_h(k), k == 0, k == DB - 1)
                last.then_inc(acc_ready, 1)
                pe.wait_ge(gate2_in, it * 16 + 16)
                for d in range(2):
                    claim(pe, S, it, 6 + d)
                    for h in range(2):
                        last = pe.matmul(unit(S, 6 + d)[:, h, 0:HALF], gate2[:, d, :],
                                         hgate[0:GATE_RANK, d, h * HALF:(h + 1) * HALF], start=True, stop=True)
                    last.then_inc(acc_ready, 1)
                order = ([0, 1, 2, 3, 4], [1, 0, 5, 4, 3])
                for d in range(2):
                    pe.wait_ge(gk_ready, it * 2 + d + 1)
                    claim(pe, S, it, 8 + d)
                    for i, t in enumerate(order[d]):
                        last = pe.transpose(flat(unit(S, 8 + d))[:, i * P:(i + 1) * P],
                                            g_kE[:, d, t * P:(t + 1) * P], ident)
                    last.then_inc(acc_ready, 1)
                for d in range(2):
                    emptied(pe, S, it, 8 + d)
                    for i, t in enumerate(order[d]):
                        if i in (0, 4):
                            claim(pe, S, it, 10 + 2 * d + i // 4)
                        u = unit(S, 10 + 2 * d + i // 4)
                        last = pe.matmul(u[:, (i % 4) // 2, (i % 2) * 256:(i % 2) * 256 + 256],
                                         g_kEt[:, d, i * P:(i + 1) * P], g_v[:, t, :], start=True, stop=True)
                        if i in (3, 4):
                            last.then_inc(acc_ready, 1)
                claim(pe, S, it, 14)
                for d in range(2):
                    u = unit(S, 14)[:, d, :]
                    for t in range(LT):
                        a, b = t * P, t * P + 64
                        pe.matmul(u[:, a:a + P], g_kt[:, d, a:a + P], g_qt[:, d, a:a + P], start=True, stop=True)
                        src, dst = (a, b) if d == 0 else (b, a)
                        last = pe.matmul(u[64 * d:64 * d + 64, dst:dst + 64], g_ke[:, d, CTX + src:CTX + src + 64],
                                         g_qt[:, d, dst:dst + 64], start=True, stop=True)
                last.then_inc(acc_ready, 1)
                emptied(pe, S, it, 14)
                for b in range(2):
                    claim(pe, S, it, 15 + b)
                    for t in range(LT):
                        o = unit(S, 15 + b)[:, 0, t * P:(t + 1) * P]
                        v = slice(b * P, (b + 1) * P)
                        tok = slice(t * P, (t + 1) * P)
                        pe.matmul(o, g_v[:, 2 + t, v], g_AT[:, 0, tok], start=True, stop=False)
                        pe.matmul(o, g_v[:, 2 + t, v], g_AT[:, 1, tok], start=False, stop=False)
                        pe.matmul(o, g_S[:, 0, 1 + t, v], g_qS[:, 0, tok], start=False, stop=False)
                        last = pe.matmul(o, g_S[:, 1, 4 - t, v], g_qS[:, 1, tok], start=False, stop=True)
                    last.then_inc(acc_ready, 1)
                claim(pe, S, it, 17)
                pe.wait_ge(gsq_ready, it * 1 + 1)
                for b in range(2):
                    last = pe.matmul(unit(S, 17)[:, 0, :], ones, sq[:, b, 0:SEQ], start=b == 0, stop=b == 1)
                last.then_inc(acc_ready, 1)
            pe.wait_ge(g_done, GLA_H + 1)
            out_proj("gla_out", lambda k: g_out[:, k, :], SEQ, DB, 4)
            square_sum("y1", SEQ)
            square_sum("h1m", SEQ)
            pe.wait_ge(h_ready, 32)
            mlp(1, SEQ, seq_h, lambda k: hid[:, k, 0:SEQ])
            square_sum("y1m", SEQ)

            pe.wait_ge(h_ready, 40)
            pe.wait_ge(ab_in, 48)
            for j in range(2):
                claim(pe, "gdn_gate", 0, j)
                linear(unit("gdn_gate", j), w_ab, 8 * j, seq_h, SEQ, DB, rows=GDN_H).then_inc(acc_ready, 1)
            pe.wait_ge(tab_in, 48)
            pe.wait_ge(d_rows, 2)
            for r in range(2):
                for c in range(LT):
                    last = pe.transpose(sc[:, 1, 0, (r * LT + c) * 8:(r * LT + c) * 8 + 8],
                                        d_row[:, r, c * P:(c + 1) * P], ident[0:GDN_H, 0:GDN_H])
            last.then_inc(d_cols, 1)
            pe.wait_ge(d_gc, 1)
            pe.matmul(sc[:, 1, 1, 0:32], last_row, d_col[:, 1].rearrange("p c h -> p (c h)"), start=True,
                      stop=True).then_inc(d_cols, 1)
            S = "gdn_pair"
            tiles = [(e, c) for e in range(2) for c in range(LT)]
            with pe.Fori(0, GDN_H // 2) as it:
                for j in range(3):
                    w = group(S, it, j, DB, 256)
                    claim(pe, S, it, j)
                    for e in range(2):
                        for k in range(DB):
                            last = mm(unit(S, j)[:, e, :], w[:, k, e * P:(e + 1) * P], seq_h(k), k == 0, k == DB - 1)
                    last.then_inc(acc_ready, 1)
                w = group(S, it, 3, DB, 256)
                for e in range(2):
                    claim(pe, S, it, 3 + e)
                    linear(unit(S, 3 + e), w, e * P, seq_h, SEQ, DB).then_inc(acc_ready, 1)
                for r in range(2):
                    pe.wait_ge(d_masked, it * 2 + r + 1)
                    claim(pe, S, it, 5 + r)
                    for e in range(2):
                        last = pe.matmul(unit(S, 5 + r)[:, e, :], ones[0:GDN_H, :], sq[0:GDN_H, e, 0:SEQ],
                                         start=True, stop=True)
                    last.then_inc(acc_ready, 1)
                for r in range(2):
                    pe.wait_ge(d_sq, it * 3 + r + 1)
                    claim(pe, S, it, 7 + r)
                    for e in range(2):
                        last = pe.matmul(unit(S, 7 + r)[:, e, :], ones, sq[:, e, 0:SEQ], start=True, stop=True)
                    last.then_inc(acc_ready, 1)

                def products(j, left, right, wait=None):
                    claim(pe, S, it, j)
                    for e, c in tiles:
                        t = slice(c * P, (c + 1) * P)
                        last = pe.matmul(unit(S, j)[:, e, t], left[:, e, t], right[:, e, t], start=True, stop=True)
                    last.then_inc(acc_ready, 1)

                pe.wait_ge(d_norm, it * 2 + 2)
                products(9, d_k, d_k)
                products(10, d_k, d_q)
                for j, x in ((11, d_k), (12, d_v)):
                    if j == 12:
                        pe.wait_ge(d_silu, it * 3 + 3)
                    claim(pe, S, it, j)
                    for e, c in tiles:
                        t = slice(c * P, (c + 1) * P)
                        last = pe.transpose(unit(S, j)[:, e, t], x[:, e, t], ident)
                    last.then_inc(acc_ready, 1)
                pe.wait_ge(d_init, it * 1 + 1)
                for l in range(7):
                    j = 13 + 3 * l
                    pe.wait_ge(d_lm, it * 7 + l + 1)
                    if l:
                        emptied(pe, S, it, j - 2)
                    products(j, d_Lm[:, l % 2], d_T)
                    emptied(pe, S, it, j)
                    if l:
                        emptied(pe, S, it, j - 1)
                    if l < 6:
                        products(j + 1, d_U, d_Y)
                    products(j + 2 if l < 6 else j + 1, d_Y, d_U)
                emptied(pe, S, it, 32)
                pe.wait_ge(d_qe, it * 1 + 1)
                for c in range(LT):
                    t, j = slice(c * P, (c + 1) * P), 33 + 4 * c
                    if c:
                        emptied(pe, S, it, j - 1)
                    claim(pe, S, it, j)
                    for e in range(2):
                        last = pe.matmul(unit(S, j)[:, e, 0:P], d_k[:, e, t], d_S[:, e, :], start=True, stop=True)
                    last.then_inc(acc_ready, 1)
                    pe.wait_ge(d_rr, it * LT + c + 1)
                    claim(pe, S, it, j + 1)
                    for e in range(2):
                        last = pe.matmul(unit(S, j + 1)[:, e, 0:P], d_U[:, e, t], d_r[:, e, :], start=True, stop=True)
                    last.then_inc(acc_ready, 1)
                    claim(pe, S, it, j + 2)
                    for e in range(2):
                        pe.matmul(unit(S, j + 2)[:, e, 0:P], d_S[:, e, :], d_qE[:, e, t], start=True, stop=False)
                        if e == 0:
                            emptied(pe, S, it, j + 1)
                        last = pe.matmul(unit(S, j + 2)[:, e, 0:P], d_vn[:, e, :], d_QK[:, e, t], start=False, stop=True)
                    last.then_inc(acc_ready, 1)
                    claim(pe, S, it, j + 3)
                    for e in range(2):
                        last = pe.matmul(unit(S, j + 3)[:, e, 0:P], d_kend[:, e, t], d_vn[:, e, :], start=True, stop=True)
                    last.then_inc(acc_ready, 1)
                pe.wait_ge(d_sq, it * 3 + 3)
                claim(pe, S, it, 49)
                for e in range(2):
                    last = pe.matmul(unit(S, 49)[:, e, :], ones, sq[:, e, 0:SEQ], start=True, stop=True)
                last.then_inc(acc_ready, 1)
            pe.wait_ge(d_done, GDN_H // 2 + 1)
            out_proj("gdn_out", lambda k: d_out[:, k, :], SEQ, DB, 4)

            def ffn(i):
                up, down = f"ffn{i}_up", f"ffn{i}_down"
                with pe.Fori(0, HIDB // 2) as it:
                    for j in range(2):
                        w = group(up, it, j, DB, 256)
                        claim(pe, up, it, j)
                        for b in range(2):
                            for k in range(DB):
                                last = mm(unit(up, j)[:, b, :], w[:, k, b * P:(b + 1) * P], seq_h(k), k == 0, k == DB - 1)
                        last.then_inc(acc_ready, 1)
                emptied(pe, up, HIDB // 2 - 1, 1)
                with pe.Fori(0, 4) as it:
                    for j in range(2):
                        w = group(down, it, j, HIDB, P)
                        claim(pe, down, it, j)
                        linear(unit(down, j), w, 0, lambda k: hid2[:, k, :], SEQ, HIDB).then_inc(acc_ready, 1)

            mean_sum("gdn_out")
            square_sum("ln0", SEQ)
            pe.wait_ge(h_ready, 48)
            ffn(0)
            mean_sum("ffn0_down")
            square_sum("ln0f", SEQ)

            pe.wait_ge(h_ready, 56)
            S = "ret_head"
            with pe.Fori(0, RET_H) as it:
                for j in range(2):
                    w = group(S, it, j, DB, 256)
                    claim(pe, S, it, j)
                    for b in range(2):
                        for k in range(DB):
                            last = mm(unit(S, j)[:, b, :], w[:, k, b * P:(b + 1) * P], seq_h(k), k == 0, k == DB - 1)
                    last.then_inc(acc_ready, 1)
                w = group(S, it, 2, DB, 512)
                for j in range(2):
                    claim(pe, S, it, 2 + j)
                    for i in range(2):
                        t = CTX + (2 * j + i) * P
                        for k in range(DB):
                            last = mm(unit(S, 2 + j)[:, i, :], hT[:, k, t:t + P], w[:, k, :], k == 0, k == DB - 1)
                    last.then_inc(acc_ready, 1)
                w = group(S, it, 3, DB, 512)
                for j in range(2):
                    claim(pe, S, it, 4 + j)
                    for i in range(2):
                        for k in range(DB):
                            m = (2 * j + i) * P
                            last = mm(unit(S, 4 + j)[:, i, :], w[:, k, m:m + P], seq_h(k), k == 0, k == DB - 1)
                    last.then_inc(acc_ready, 1)
                pe.wait_ge(r_rotd, it * 2 + 2)
                for j in range(2):
                    claim(pe, S, it, 6 + j)
                    for i in range(2):
                        t = (2 * j + i) * P
                        for b in range(2):
                            last = pe.matmul(unit(S, 6 + j)[:, i, 0:SEQ - t], r_rot[:, 1, b, t:t + P],
                                             r_rot[:, 0, b, t:SEQ], start=b == 0, stop=b == 1)
                    last.then_inc(acc_ready, 1)
                emptied(pe, S, it, 6)
                emptied(pe, S, it, 7)
                for j in range(2):
                    claim(pe, S, it, 8 + j)
                    for i in range(2):
                        m = (2 * j + i) * P
                        for t in range(LT):
                            last = pe.matmul(unit(S, 8 + j)[:, i, t * P:SEQ], r_v[:, t, m:m + P],
                                             r_s[:, t, 0:SEQ - t * P], start=t == 0, stop=t == LT - 1)
                    last.then_inc(acc_ready, 1)
                emptied(pe, S, it, 8)
                emptied(pe, S, it, 9)
                claim(pe, S, it, 10)
                for b in range(4):
                    last = pe.matmul(unit(S, 10)[:, 0, :], ones, r_o[:, b, :], start=b == 0, stop=b == 3)
                last.then_inc(acc_ready, 1)
                claim(pe, S, it, 11)
                for b in range(4):
                    pe.wait_ge(r_sq, it * 4 + b + 1)
                    last = pe.matmul(unit(S, 11)[:, 0, :], ones, r_sqr[:, b, :], start=b == 0, stop=b == 3)
                last.then_inc(acc_ready, 1)
            pe.wait_ge(r_done, RET_H + 1)
            out_proj("ret_out", lambda k: r_out[:, k, :], SEQ, 16, 2)
            mean_sum("ret_out")
            square_sum("ln1", SEQ)
            pe.wait_ge(h_ready, 64)
            ffn(1)
            mean_sum("ffn1_down")
            square_sum("ln1f", SEQ)
            pe.wait_ge(x_ready, 64)
            for t in range(LT):
                if t >= 2:
                    pe.wait_ge(o_moved, t - 1)
                for b in range(DB):
                    last = pe.transpose(flat(sc[:, t % 2])[:, b * P:(b + 1) * P],
                                        xT[:, b, CTX + t * P:CTX + (t + 1) * P], ident)
                last.then_inc(o_turned, 1)

        @block.scalar
        def _(act):
            st = Steps(act, act_step)
            f = act.activation

            def squares(name, src, n, ready=None):
                _, b0, nb = NORMS[name]
                for b in range(nb):
                    if ready is not None:
                        ready(b)
                    if b0 + b >= 2:
                        act.wait_ge(n_used, b0 + b - 1)
                    f(sq[:, (b0 + b) % 2, 0:n], src(b), ACT.Square).then_inc(n_sq, 1)

            def deviation(name, n, width, e=0):
                k, b0, nb = NORMS[name]
                act.wait_ge(n_used, b0 + nb)
                i, o = (sc[:, 0, :, 0:HALF], halves(rstd)) if n == T else (sc[:, 0, 0, 0:n], rstd[:, 0:n])
                f(o, i, ACT.Sqrt, scale=1.0 / width, bias=eps[:, e:e + 1]).then_inc(n_std, 1)

            def affine(l, q, n, mul0):
                for b in range(DB):
                    act.wait_ge(n_mul, mul0 + b + 1)
                    if n == T:
                        f(hT[:, b, 0:CTX], hT[:, b, 0:CTX], ACT.Identity, scale=dcol[:, l, q, b, 1:2],
                          bias=mod[:, l, 24 * (q // 2) + b, 1:2])
                    f(hT[:, b, CTX:T], hT[:, b, CTX:T], ACT.Identity, scale=dcol[:, l, q, b, 0:1],
                      bias=mod[:, l, 24 * (q // 2) + b, 0:1]).then_inc(h_ready, 1)

            def modulate(l, q, x0):
                for b in range(DB):
                    act.wait_ge(x_ready, x0 + b + 1)
                    f(hT[:, b, CTX:T], xT[:, b, CTX:T], ACT.Identity, scale=dcol[:, l, q, b, 0:1],
                      bias=mod[:, l, 24 * (q // 2) + b, 0:1]).then_inc(h_ready, 1)

            def layer_norm_out(l, i, mul0):
                for b in range(DB):
                    act.wait_ge(n_mul, mul0 + b + 1)
                    f(xT[:, b, CTX:T], xT[:, b, CTX:T], ACT.Identity, scale=col("ln_g_2", (2 * l + i) * DB + b),
                      bias=col("ln_b_2", (2 * l + i) * DB + b)).then_inc(x_ready, 1)

            def x_at(b0, seq=False):
                return lambda b: act.wait_ge(x_ready, b0 + b + 1)

            def y_at(stage):
                return lambda b: emptied(act, stage, *divmod(b, UNITS[stage]))

            def const(dst, src, s):
                act.dma_start(dst, src).then_inc(s, 16)

            const(base_tab[:, :], A["tab_base"], const_in)
            for name, src in vec_sources:
                t, r, rows = VEC[name]
                const(vrow[r:r + rows, t, :], src, const_in)
            const(x_tok[:, 0:2, :], A["ctx"][0].rearrange("(t p) d -> p t d", p=P), x_in)
            const(x_tok[:, 2:QT, :], A["x"][0].rearrange("(t p) d -> p t d", p=P), x_in)
            const(tab[:, 0:1408], A["tab_mla"], tab_in)
            for d in range(2):
                const(gate1[:, :, d, :], A["gla_w_gate1"][0, d].rearrange("(k p) r -> p k r", p=P), gate1_in)
            const(w_ab[:, :, :], A["gdn_w_in_2"][:, 4 * D:4 * D + 16].rearrange("(k p) n -> p k n", p=P), ab_in)
            const(a_dt[:, 0:1], A["gdn_a_log_2"].rearrange("(h a) -> h a", a=1), ab_in)
            const(a_dt[:, 1:2], A["gdn_dt_bias_2"].rearrange("(h a) -> h a", a=1), ab_in)
            act.wait_ge(cols_ready, 1)
            f(cs[:, :, 0], vec("c", 0, DB), ACT.Silu)
            f(cs[:, :, 1], vec("c_ctx", 0, DB), ACT.Silu).then_inc(c_ready, 1)
            for b in range(DB):
                act.wait_ge(x_turned, b + 1)
                f(xT[:, b, :], flat(sc[:, b % 2])[:, 0:T], ACT.Copy).then_inc(x_moved, 1)
            act.wait_ge(cond_done, 1)
            for i in (2, 3):
                for k in range(DB):
                    last = f(cs[:, k, i:i + 1], sc[:, 1, 0, k:k + 1], ACT.Silu, bias=col("cond_b", k))
            last.then_inc(e_ready, 1)

            act.wait_ge(relu_free, 2)
            act.wait_ge(x_moved, DB)
            squares("h0", lambda b: xT[:, b, :], T)
            deviation("h0", T, D)
            act.wait_ge(mod_ready, 1)
            affine(0, 0, T, 0)
            squares("cq", lambda b: cq[:, b, :], T, lambda b: emptied(act, "mla_in", 0, b))
            deviation("cq", T, Q_RANK)
            squares("ckv", lambda b: ckv[:, b, :], T, lambda b: emptied(act, "mla_in", 0, 3 + b))
            act.wait_ge(lat_ready, 3)
            deviation("ckv", T, KV_RANK)
            scale = (NOPE + ROPE) ** -0.5
            with act.Fori(0, MLA_H // 2) as it:
                for n in range(2 * QT):
                    act.wait_ge(p_max, it * 12 + n + 1)
                    if n % QT < 2:
                        i, o = sc[:, n % 2, 0, 0:CTX], prob[:, n % 2, 0:CTX]
                    else:
                        i, o = sc[:, n % 2, :, 0:HALF], halves(prob[:, n % 2, :])
                    f(o, i, ACT.Exp, bias=small[:, n % 2, 1:2], scale=scale,
                      accum_out=small[:, n % 2, 2:3]).then_inc(p_exp, 1)

            def mlp(i, n):
                up = f"mlp{i}_up"
                with act.Fori(0, 4) as it:
                    for j in range(8):
                        finished(act, up, it, j)
                        act.wait_ge(relu_free, it * 8 + (32 * i + j + 1))
                        u = unit(up, j)
                        if n == T:
                            ins = f(halves(relu[:, j % 2, :]), u[:, :, 0:HALF], ACT.Relu)
                        else:
                            ins = f(relu[:, j % 2, 0:n], u[:, 0, 0:n], ACT.Relu)
                        free(ins, up, j)

            y_all = lambda b: hT[:, b, :]
            y_seq = lambda b: hT[:, b, CTX:T]
            x_all = lambda b: xT[:, b, :]
            x_seq = lambda b: xT[:, b, CTX:T]
            squares("y0", y_all, T, y_at("mla_out"))
            deviation("y0", T, D)
            const(tab[:, 0:1024], A["tab_gla"], tab_in)
            squares("h0m", x_all, T, x_at(0))
            deviation("h0m", T, D)
            affine(0, 2, T, 8)
            mlp(0, T)
            squares("y0m", y_all, T, y_at("mlp0_down"))
            deviation("y0m", T, D)

            squares("h1", x_all, T, x_at(8))
            deviation("h1", T, D)
            affine(1, 0, T, 16)
            S = "gla_head"
            with act.Fori(0, GLA_H) as it:
                st.enter(it, 4)
                finished(act, S, it, 0)
                free(f(g_q, unit(S, 0)[:, 0, :], ACT.Copy, scale=P ** -0.5), S, 0)
                finished(act, S, it, 1)
                free(f(halves(g_k), unit(S, 1)[:, :, 0:HALF], ACT.Copy), S, 1)
                act.wait_ge(g_done, it * 1 + 1)
                finished(act, S, it, 5)
                free(f(g_r, unit(S, 5), ACT.Silu), S, 5)
                for d in range(2):
                    emptied(act, S, it, 6 + d)
                    st.did(f(g_l, g_z, ACT.Abs))
                    st.settle()
                    st.did(f(g_l, g_l, ACT.Exp, scale=-1.0))
                    st.settle()
                    f(g_l, g_l, ACT.Ln, bias=1.0).then_inc(gl_ready, 1)
                    act.wait_ge(gG_ready, it * 2 + d + 1)
                    f(g_qt[:, d, :], g_G[:, CTX:T], ACT.Exp, scale=1 / 16)
                    f(g_kt[:, d, :], g_G[:, CTX:T], ACT.Exp, scale=-1 / 16)
                    f(g_ke[:, d, :], g_z, ACT.Exp, scale=1 / 16)
                    f(g_et[:, d, :], g_tot[:, d, :], ACT.Exp, scale=1 / 16).then_inc(gE_ready, 1)
                for d in range(2):
                    finished(act, S, it, 8 + d)
                    free(f(g_kEt[:, d, :], flat(unit(S, 8 + d))[:, 0:5 * P], ACT.Copy), S, 8 + d)
                emptied(act, S, it, 15)
                emptied(act, S, it, 16)
                f(sq[:, :, 0:SEQ], g_o, ACT.Square).then_inc(gsq_ready, 1)
                finished(act, S, it, 17)
                free(f(rstd[:, 0:SEQ], unit(S, 17)[:, 0, :], ACT.Sqrt, scale=1.0 / GLA_DV, bias=eps[:, 0:1]), S, 17)
            st.leave(GLA_H)
            squares("y1", y_seq, SEQ, y_at("gla_out"))
            deviation("y1", SEQ, D)
            const(tab[:, 0:1664], A["tab_gdn"], tab_in)
            squares("h1m", x_seq, SEQ, x_at(16))
            deviation("h1m", SEQ, D)
            affine(1, 2, SEQ, 24)
            mlp(1, SEQ)
            squares("y1m", y_seq, SEQ, y_at("mlp1_down"))
            deviation("y1m", SEQ, D)

            modulate(2, 0, 24)
            act.wait_ge(ab_in, 48)
            f(a_dt[:, 2:3], a_dt[:, 0:1], ACT.Exp).then_inc(d_ga, 1)
            finished(act, "gdn_gate", 0, 1)
            free(f(d_row[:, 0, :], unit("gdn_gate", 1)[0:GDN_H, 0, :], ACT.Sigmoid), "gdn_gate", 1)
            emptied(act, "gdn_gate", 0, 0)
            st.did(f(sq[0:GDN_H, 0, 0:SEQ], rstd[0:GDN_H, 0:SEQ], ACT.Abs))
            st.settle()
            st.did(f(sq[0:GDN_H, 0, 0:SEQ], sq[0:GDN_H, 0, 0:SEQ], ACT.Exp, scale=-1.0))
            st.settle()
            f(sq[0:GDN_H, 0, 0:SEQ], sq[0:GDN_H, 0, 0:SEQ], ACT.Ln, bias=1.0).then_inc(d_ga, 1)
            act.wait_ge(d_glr, 1)
            f(d_col[:, 2], d_col[:, 1], ACT.Exp)
            f(d_col[:, 4], d_col[:, 4], ACT.Exp)
            f(d_col[:, 3], d_col[:, 3], ACT.Exp).then_inc(d_ga, 1)
            S = "gdn_pair"
            with act.Fori(0, GDN_H // 2) as it:
                for j in range(3):
                    finished(act, S, it, j)
                    act.wait_ge(d_conv, it * 3 + max(2, j + 1))
                    free(f(d_cp[:, j % 2, :, 3:SEQ + 3], unit(S, j), ACT.Copy), S, j)
                act.wait_ge(d_done, it * 1 + 1)
                for e in range(2):
                    finished(act, S, it, 3 + e)
                    free(f(d_z[:, e, :], unit(S, 3 + e)[:, 0, :], ACT.Silu), S, 3 + e)
                for j, x in enumerate((d_q, d_k, d_v)):
                    act.wait_ge(d_conv, it * 3 + j + 3)
                    f(x, x, ACT.Silu).then_inc(d_silu, 1)
                for r, x in enumerate((d_gcR, d_bR)):
                    finished(act, S, it, 5 + r)
                    free(f(x, unit(S, 5 + r), ACT.Copy), S, 5 + r)
                for r, (x, y) in enumerate(((d_q, d_Y), (d_k, d_U))):
                    act.wait_ge(d_silu, it * 3 + r + 1)
                    if r:
                        finished(act, S, it, 7)
                    f(sq[:, :, 0:SEQ], x, ACT.Square).then_inc(d_sq, 1)
                    finished(act, S, it, 7 + r)
                    free(f(y, unit(S, 7 + r), ACT.Sqrt, bias=eps[:, 0:1]), S, 7 + r)
                act.wait_ge(d_diff, it * 1 + 1)
                f(d_ET, d_ET, ACT.Exp).then_inc(d_exp, 1)
                finished(act, S, it, 12)
                f(d_v, d_gcR, ACT.Exp).then_inc(d_exp, 1)
                for l in range(7):
                    finished(act, S, it, 13 + 3 * l)
                    free(f(d_Y, unit(S, 13 + 3 * l), ACT.Copy), S, 13 + 3 * l)
                for c in range(LT):
                    t, j = slice(c * P, (c + 1) * P), 33 + 4 * c
                    finished(act, S, it, j + 1)
                    free(f(d_vn, unit(S, j + 1)[:, :, 0:P], ACT.Copy), S, j + 1)
                    finished(act, S, it, j + 2)
                    free(f(d_o[:, :, t], unit(S, j + 2)[:, :, 0:P], ACT.Copy), S, j + 2)
                emptied(act, S, it, 47)
                f(sq[:, :, 0:SEQ], d_o, ACT.Square).then_inc(d_sq, 1)
                finished(act, S, it, 49)
                free(f(d_Y, unit(S, 49), ACT.Sqrt, scale=1.0 / P, bias=eps[:, 0:1]), S, 49)

            def layer_norm(stage, name, l, i, x0, mul0):
                squares(name, x_seq, SEQ, lambda b: act.wait_ge(n_cent, x0 - 32 + b + 1))
                deviation(name, SEQ, D, 1)
                layer_norm_out(l, i, mul0)

            def ffn(i):
                up = f"ffn{i}_up"
                with act.Fori(0, HIDB // 2) as it:
                    finished(act, up, it, 0)
                    act.wait_ge(f_conv, it * 1 + (HIDB // 2 * i + i + 1))
                    free(f(gpad[:, :, 2:SEQ + 2], unit(up, 0), ACT.Copy), up, 0)
                    act.wait_ge(f_conv, it * 1 + (HIDB // 2 * i + i + 2))
                    f(gsilu, gconv, ACT.Silu).then_inc(f_silu, 1)

            layer_norm("gdn_out", "ln0", 0, 0, 32, 32)
            modulate(2, 2, 32)
            ffn(0)
            layer_norm("ffn0_down", "ln0f", 0, 1, 40, 40)

            const(r_tab[:, :, :], A["tab_ret"].rearrange("p (a n) -> p a n", a=6), rtab_in)
            modulate(3, 0, 40)
            S = "ret_head"
            with act.Fori(0, RET_H) as it:
                finished(act, S, it, 0)
                free(f(r_raw[:, 0], unit(S, 0), ACT.Copy), S, 0)
                finished(act, S, it, 1)
                free(f(r_raw[:, 1], unit(S, 1), ACT.Copy, scale=1 / 16), S, 1)
                act.wait_ge(r_done, it * 1 + 1)
                for j in range(2):
                    finished(act, S, it, 4 + j)
                    free(f(r_gate[:, 2 * j:2 * j + 2, :], unit(S, 4 + j), ACT.Silu), S, 4 + j)
                for b in range(4):
                    if b < 3:
                        act.wait_ge(r_cent, it * 3 + b + 1)
                    else:
                        emptied(act, S, it, 10)
                    f(r_sqr[:, b, :], r_o[:, b, :], ACT.Square).then_inc(r_sq, 1)
                finished(act, S, it, 11)
                free(f(rstd[:, 0:SEQ], unit(S, 11)[:, 0, :], ACT.Sqrt, scale=1.0 / RET_DV, bias=eps[:, 0:1]), S, 11)
            layer_norm("ret_out", "ln1", 1, 0, 48, 48)
            modulate(3, 2, 48)
            ffn(1)
            layer_norm("ffn1_down", "ln1f", 1, 1, 56, 56)

        @block.vector
        def _(dve):
            st = Steps(dve, dve_step)
            tt, ts, stt, cp = dve.tensor_tensor, dve.tensor_scalar, dve.scalar_tensor_tensor, dve.tensor_copy
            MUL, ADD, SUB, MIN, MAX = ALU.mult, ALU.add, ALU.subtract, ALU.min, ALU.max

            def reciprocal_of(name, n):
                k, _, _ = NORMS[name]
                dve.wait_ge(n_std, k + 1)
                st.did(dve.reciprocal(rstd[:, 0:n], rstd[:, 0:n]))
                st.settle()

            def normed(name, n):
                reciprocal_of(name, n)
                for b in range(DB):
                    tt(hT[:, b, T - n:T], xT[:, b, T - n:T], rstd[:, 0:n], MUL).then_inc(n_mul, 1)

            def residual(name, n, l, q):
                reciprocal_of(name, n)
                for b in range(DB):
                    st.did(tt(hT[:, b, T - n:T], hT[:, b, T - n:T], rstd[:, 0:n], MUL))
                st.settle()
                for b in range(DB):
                    if n == T:
                        stt(xT[:, b, 0:CTX], hT[:, b, 0:CTX], dcol[:, l, q, b, 1:2], xT[:, b, 0:CTX], MUL, ADD)
                    stt(xT[:, b, CTX:T], hT[:, b, CTX:T], dcol[:, l, q, b, 0:1], xT[:, b, CTX:T],
                        MUL, ADD).then_inc(x_ready, 1)

            dve.memset(eps[:, 0:1], 1e-6).then_inc(relu_free, 1)
            dve.memset(eps[:, 1:2], 1e-5 / ALPHA ** 2).then_inc(relu_free, 1)
            dve.wait_ge(vec_turned, 1)
            for t in range(VEC_TILES):
                n = vec_rows[t]
                last = cp(cols[:, t, 0:n], flat(acc[:, 0])[:, t * P:t * P + n])
            last.then_inc(cols_ready, 1)
            dve.wait_ge(cols_ready, 1)
            dve.wait_ge(ada_done, 24)
            for l in range(4):
                for v in range(2):
                    b = vec("ada_b" if l < 2 else "ada_b_2", 48 * (l % 2), 48)
                    st.did(tt(mod[:, l, :, v], sc[:, 1, 1, 96 * l:96 * (l + 1)].rearrange("p (i v) -> p i v", v=2)[:, :, v],
                              b, ADD))
            st.settle()
            for l in range(4):
                for q, (m, plus) in enumerate(((1, 1.0), (2, 0.0), (4, 1.0), (5, 0.0))):
                    for v in range(2):
                        src = mod[:, l, m * DB:(m + 1) * DB, v]
                        if l < 2:
                            st.did(stt(dcol[:, l, q, :, v], src, plus, vec("norm_g", (4 * l + q) * DB, DB), ADD, MUL))
                        else:
                            st.did(ts(dcol[:, l, q, :, v], src, 1.0, 1.0 if plus else 1.0 / ALPHA, ADD, MUL))
            st.settle()
            dve.memset(krope[:, :, :], 0.0).then_inc(mod_ready, 1)

            normed("h0", T)
            for j in range(5):
                finished(dve, "mla_in", 0, j)
                free(cp(halves(cq[:, j, :] if j < 3 else ckv[:, j - 3, :]), unit("mla_in", j)[:, :, 0:HALF]), "mla_in", j)
            finished(dve, "mla_in", 0, 5)
            free(cp(halves(kraw[0:64]), unit("mla_in", 5)[0:64, :, 0:HALF]), "mla_in", 5)
            finished(dve, "mla_rope", 0, 0)
            free(cp(halves(qraw), unit("mla_rope", 0)[:, :, 0:HALF]), "mla_rope", 0)
            finished(dve, "mla_rope", 0, 1)
            free(tt(ktmp, unit("mla_rope", 1)[:, 0, :], rsin, MUL), "mla_rope", 1)
            emptied(dve, "mla_rope", 0, 0)
            emptied(dve, "mla_rope", 0, 1)
            dve.wait_ge(mod_ready, 1)
            st.did(tt(qr[:, CTX:T], qraw[:, CTX:T], rcos, MUL))
            st.settle()
            for e in range(2):
                h = slice(64 * e, 64 * e + 64)
                cp(krope[h, e, 0:CTX], qraw[h, 0:CTX])
                last = tt(krope[h, e, CTX:T], qr[h, CTX:T], ktmp[h, :], ADD)
            last.then_inc(krope_ready, 1)
            for name, x, nb, g in (("cq", cq, 3, "mla_g_q"), ("ckv", ckv, 2, "mla_g_kv")):
                reciprocal_of(name, T)
                for b in range(nb):
                    stt(x[:, b, :], x[:, b, :], col(g, b), rstd[:, :], MUL, MUL).then_inc(lat_ready, 1)
            S = "mla_pair"
            scale = (NOPE + ROPE) ** -0.5
            with dve.Fori(0, MLA_H // 2) as it:
                st.enter(it, 1 + 12 * 2)
                for j, o in ((0, qn[:, 0]), (1, qn[:, 1]), (2, qraw), (3, kn[:, 0]), (4, kn[:, 1])):
                    finished(dve, S, it, j)
                    free(cp(halves(o), unit(S, j)[:, :, 0:HALF]), S, j)
                for j in range(3):
                    finished(dve, S, it, 5 + j)
                    free(cp(vtok[:, 2 * j:2 * j + 2, :], unit(S, 5 + j)[:, :, 0:256]), S, 5 + j)
                emptied(dve, S, it, 2)
                cp(qr[:, 0:CTX], qraw[:, 0:CTX])
                st.did(tt(qr[:, CTX:T], qraw[:, CTX:T], rcos, MUL))
                for j in range(2):
                    finished(dve, S, it, 8 + j)
                    free(tt(ktmp[:, 256 * j:256 * j + 256], unit(S, 8 + j)[:, 0, 0:256],
                            rsin[:, 256 * j:256 * j + 256], MUL), S, 8 + j)
                emptied(dve, S, it, 8)
                emptied(dve, S, it, 9)
                st.settle()
                tt(qr[:, CTX:T], qr[:, CTX:T], ktmp, ADD).then_inc(qrope_ready, 1)
                for n in range(2 * QT + 1):
                    e, t, s = n // QT, n % QT, n % 2
                    if n < 2 * QT:
                        dve.wait_ge(s_ready, it * 12 + n + 1)
                        i = sc[:, s, 0:1, 0:CTX] if t < 2 else sc[:, s, :, 0:HALF]
                        st.did(dve.tensor_reduce(small[:, s, 0:1], i, XY, MAX))
                        st.settle()
                        ts(small[:, s, 1:2], small[:, s, 0:1], -scale, None, MUL).then_inc(p_max, 1)
                    if n:
                        nk = 2 if (n - 1) % QT < 2 else KT
                        u = 10 + 2 * (n - 1)
                        finished(dve, S, it, u)
                        free(cp(probT[:, (n - 1) % 2, 0:nk * P], flat(unit(S, u))[:, 0:nk * P]), S, u)
                    if n < 2 * QT:
                        w = CTX if t < 2 else T
                        dve.wait_ge(p_exp, it * 12 + n + 1)
                        st.did(dve.reciprocal(small[:, s, 3:4], small[:, s, 2:3]))
                        st.settle()
                        ts(prob[:, s, 0:w], prob[:, s, 0:w], small[:, s, 3:4], None, MUL).then_inc(p_ready, 1)
                    if n:
                        m, u = n - 1, 11 + 2 * (n - 1)
                        finished(dve, S, it, u)
                        free(cp(attn[:, bass.ds(it * 2 + m // QT, 1), (m % QT) * P:(m % QT) * P + P],
                                unit(S, u)[:, 0:1, 0:P]), S, u)
            st.leave(MLA_H // 2)

            def out_y(stage, n):
                for j in range(8):
                    finished(dve, stage, 0, j)
                    if n == T:
                        ins = cp(halves(hT[:, j, :]), unit(stage, j)[:, :, 0:HALF])
                    else:
                        ins = cp(hT[:, j, CTX:T], unit(stage, j)[:, 0, :])
                    free(ins, stage, j)

            def mlp(i, n):
                up, down = f"mlp{i}_up", f"mlp{i}_down"
                with dve.Fori(0, 4) as it:
                    for j in range(8):
                        emptied(dve, up, it, j)
                        r = relu[:, j % 2:j % 2 + 1, 0:n]
                        tt(hid[:, bass.ds(it * 8 + j, 1), 0:n], r, r, MUL).then_inc(relu_free, 1)
                with dve.Fori(0, 4) as it:
                    for j in range(2):
                        finished(dve, down, it, j)
                        if n == T:
                            ins = cp(hT[:, bass.ds(it * 2 + j, 1), :].rearrange("p a (h n) -> p (a h) n", h=2),
                                     unit(down, j)[:, :, 0:HALF])
                        else:
                            ins = cp(hT[:, bass.ds(it * 2 + j, 1), CTX:T], unit(down, j)[:, 0:1, :])
                        free(ins, down, j)

            out_y("mla_out", T)
            residual("y0", T, 0, 1)
            normed("h0m", T)
            mlp(0, T)
            residual("y0m", T, 0, 3)

            normed("h1", T)
            for d in range(2):
                finished(dve, "gla_gate", 0, d)
                free(cp(halves(hgate[0:GATE_RANK, d, :]), unit("gla_gate", d)[0:GATE_RANK, :, 0:HALF]), "gla_gate", d)
            dve.memset(g_AT[:, :, :], 0.0).then_inc(g_done, 1)
            dve.wait_ge(g_done, 1)
            dve.wait_ge(tab_in, 32)
            S = "gla_head"
            c64 = lambda a: a.rearrange("p (c n) -> p c n", n=64)
            with dve.Fori(0, GLA_H) as it:
                st.enter(it, 19)
                for j in range(3):
                    finished(dve, S, it, 2 + j)
                    free(cp(g_v[:, 2 * j:2 * j + 2, :], unit(S, 2 + j)[:, :, 0:GLA_DV]), S, 2 + j)
                for d in range(2):
                    finished(dve, S, it, 6 + d)
                    free(ts(halves(g_z), unit(S, 6 + d)[:, :, 0:HALF], dyncol("gla_b_gate", it * 1 + 4 * d), None, ADD), S, 6 + d)
                    dve.wait_ge(gl_ready, it * 2 + d + 1)
                    st.did(stt(g_g, g_z, 0.0, g_l, MIN, SUB))
                    st.settle()
                    st.did(dve.tensor_tensor_scan(g_G, keep64, g_g, 0.0, MUL, ADD))
                    st.settle()
                    if d == 0:
                        st.did(cp(g_tot[:, 0, :], c64(g_G)[:, :, 63]))
                        st.settle()
                    else:
                        st.did(cp(g_tot[:, 1, :], c64(g_G)[:, :, 63]))
                        st.did(tt(g_g, g_G, g_g, SUB))
                        st.settle()
                        st.did(tt(c64(g_G), g_tot[:, 1, :].unsqueeze(2).to_broadcast([P, 12, 64]), c64(g_g), SUB))
                        st.settle()
                    tt(c64(g_z), g_tot[:, d, :].unsqueeze(2).to_broadcast([P, 12, 64]), c64(g_G), SUB).then_inc(gG_ready, 1)
                    dve.wait_ge(gE_ready, it * 2 + d + 1)
                    emptied(dve, S, it, 0)
                    emptied(dve, S, it, 1)
                    tt(g_qt[:, d, :], g_qt[:, d, :], g_q, MUL)
                    tt(g_kt[:, d, :], g_kt[:, d, :], g_k[:, CTX:T], MUL)
                    st.did(tt(g_ke[:, d, :], g_ke[:, d, :], g_k, MUL))
                    st.settle()
                    q4, s4 = (x[:, d, :].rearrange("p (t a n) -> p t a n", a=2, n=64) for x in (g_qt, g_qS))
                    e4, k4 = (x[:, d, :].rearrange("p (t a n) -> p t a n", a=2, n=64) for x in (g_ke, g_kE))
                    et = g_et[:, d, :].rearrange("p (t a) -> p t a", a=2)
                    near, far = (0, 1) if d == 0 else (1, 0)
                    cp(s4[:, :, near], q4[:, :, near])
                    tt(s4[:, :, far], q4[:, :, far], et[:, 2:QT, near].unsqueeze(2).to_broadcast([P, LT, 64]), MUL)
                    cp(k4[:, :, far], e4[:, :, far])
                    tt(k4[:, :, near], e4[:, :, near], et[:, :, far].unsqueeze(2).to_broadcast([P, QT, 64]), MUL)
                    tt(g_dec[:, d, :], et[:, :, 0], et[:, :, 1], MUL).then_inc(gk_ready, 1)
                order = ([0, 1, 2, 3, 4], [1, 0, 5, 4, 3])
                for d in range(2):
                    for i, t in enumerate(order[d]):
                        if i in (0, 4):
                            finished(dve, S, it, 10 + 2 * d + i // 4)
                        if d == 1 and i == 4:
                            finished(dve, S, it, 14)
                        p = unit(S, 10 + 2 * d + i // 4)[:, (i % 4) // 2, (i % 2) * 256:(i % 2) * 256 + 256]
                        if i == 0:
                            ins = cp(g_S[:, d, 0, :], p)
                        else:
                            ins = stt(g_S[:, d, i, :], g_S[:, d, i - 1, :], g_dec[:, d, t:t + 1], p, MUL, ADD)
                        if i == 3:
                            free(ins, S, 10 + 2 * d)
                            emptied(dve, S, it, 10 + 2 * d)
                        elif i == 4:
                            free(ins, S, 11 + 2 * d)
                        else:
                            st.did(ins)
                            st.settle()
                tri = tri_fb.bitcast(U32).rearrange("p (d n) -> p d n", d=2).unsqueeze(2).to_broadcast([P, 2, LT, P])
                free(dve.copy_predicated(g_AT.rearrange("p d (t n) -> p d t n", n=P), tri,
                                         unit(S, 14).rearrange("p d (t n) -> p d t n", n=P)), S, 14)
                for b in range(2):
                    finished(dve, S, it, 15 + b)
                    free(cp(g_o[:, b, :], unit(S, 15 + b)[:, 0, :]), S, 15 + b)
                emptied(dve, S, it, 17)
                st.did(dve.reciprocal(rstd[:, 0:SEQ], rstd[:, 0:SEQ]))
                st.settle()
                for b in range(2):
                    st.did(stt(g_o[:, b, :], g_o[:, b, :], col("gla_g_o", b), rstd[:, 0:SEQ], MUL, MUL))
                st.settle()
                tt(g_out[:, bass.ds(it * 2, 2), :], g_o, g_r, MUL).then_inc(g_done, 1)
            st.leave(GLA_H)
            out_y("gla_out", SEQ)
            residual("y1", SEQ, 1, 1)
            normed("h1m", SEQ)
            mlp(1, SEQ)
            residual("y1m", SEQ, 1, 3)

            finished(dve, "gdn_gate", 0, 0)
            dve.wait_ge(d_ga, 1)
            free(ts(rstd[0:GDN_H, 0:SEQ], unit("gdn_gate", 0)[0:GDN_H, 0, :], a_dt[:, 1:2], None, ADD), "gdn_gate", 0)
            dve.wait_ge(d_ga, 2)
            st.did(stt(rstd[0:GDN_H, 0:SEQ], rstd[0:GDN_H, 0:SEQ], 0.0, sq[0:GDN_H, 0, 0:SEQ], MAX, ADD))
            st.settle()
            st.did(ts(rstd[0:GDN_H, 0:SEQ], rstd[0:GDN_H, 0:SEQ], a_dt[:, 2:3], -1.0, MUL, MUL))
            st.settle()
            dve.wait_ge(tab_in, 48)
            dve.tensor_tensor_scan(d_row[:, 1, :], keep128[0:GDN_H, :], rstd[0:GDN_H, 0:SEQ], 0.0, MUL, ADD).then_inc(d_rows, 1)
            emptied(dve, "gdn_gate", 0, 1)
            dve.memset(d_S[:, :, :], 0.0).then_inc(d_rows, 1)
            dve.wait_ge(d_cols, 1)
            cp(d_col[:, 0:2].rearrange("p r c h -> p (r c h)"), sc[:, 1, 0, 0:64]).then_inc(d_gc, 1)
            dve.wait_ge(d_gc, 1)
            dve.wait_ge(d_cols, 2)
            gl = sc[:, 1, 1, 0:32].rearrange("p (c h) -> p c h", c=LT)
            cp(d_col[:, 4], gl)
            tt(d_col[:, 3], gl, d_col[:, 1], SUB).then_inc(d_glr, 1)
            dve.wait_ge(d_ga, 3)
            st.did(ts(d_col[:, 2], d_col[:, 2], -1.0, None, MUL))
            st.settle()
            for j in range(2):
                dve.memset(d_cp[:, j, :, 0:3], 0.0).then_inc(d_conv, 1)
            dve.memset(d_r[:, :, :], 0.0).then_inc(d_done, 1)
            dve.wait_ge(d_done, 1)
            dve.wait_ge(d_conv, 2)
            S = "gdn_pair"
            colh = lambda r, c, it, e: d_col[:, r, c, bass.ds(it * 2 + e, 1)]
            with dve.Fori(0, GDN_H // 2) as it:
                st.enter(it, 31)
                for j, x in enumerate((d_q, d_k, d_v)):
                    emptied(dve, S, it, j)
                    for tap in (3, 0, 1, 2):
                        for e in range(2):
                            w = dyncol("gdn_conv_w", it * 2 + (24 * tap + 8 * j + e))
                            s = d_cp[:, j % 2, e, tap:tap + SEQ]
                            if tap == 3:
                                ins = ts(x[:, e, :], s, w, None, MUL)
                            else:
                                ins = stt(x[:, e, :], s, w, x[:, e, :], MUL, ADD)
                            if tap == 2 and e == 1:
                                ins.then_inc(d_conv, 1)
                            else:
                                st.did(ins)
                        if tap != 2:
                            st.settle()
                for r in range(2):
                    if r:
                        finished(dve, S, it, 5)
                    for e in range(2):
                        ins = ts(sq[0:GDN_H, e, 0:SEQ], d_row[:, 1 - r, :], ident[0:GDN_H, bass.ds(it * 2 + e, 1)], None, MUL)
                    ins.then_inc(d_masked, 1)
                emptied(dve, S, it, 7)
                st.did(dve.reciprocal(d_Y, d_Y))
                st.settle()
                stt(d_q, d_q, P ** -0.5, d_Y, MUL, MUL).then_inc(d_norm, 1)
                emptied(dve, S, it, 5)
                for e in range(2):
                    for c in range(LT):
                        t = slice(c * P, (c + 1) * P)
                        last = ts(d_ET[:, e, t], d_gcR[:, e, t], colh(1, c, it, e), 0.0, SUB, MIN)
                last.then_inc(d_diff, 1)
                emptied(dve, S, it, 8)
                st.did(dve.reciprocal(d_U, d_U))
                st.settle()
                tt(d_k, d_k, d_U, MUL).then_inc(d_norm, 1)
                dve.wait_ge(d_exp, it * 2 + 1)
                emptied(dve, S, it, 6)
                st.did(tt(d_LT, d_ET, d_bR, MUL))
                st.settle()
                finished(dve, S, it, 9)
                free(tt(d_LT, d_LT, unit(S, 9), MUL), S, 9)
                emptied(dve, S, it, 9)
                c8 = lambda m: m.unsqueeze(1).to_broadcast([P, 2 * LT, P])
                cp(chunks(d_T), c8(ident))
                cp(chunks(d_U), c8(ident)).then_inc(d_init, 1)

                def level_mask(l):
                    tt(chunks(d_Lm[:, l % 2]), chunks(d_LT), c8(lvl_mask[l]), MUL).then_inc(d_lm, 1)

                level_mask(0)
                level_mask(1)
                st.did(tt(chunks(d_ET), chunks(d_ET), c8(causal), MUL))
                st.settle()
                finished(dve, S, it, 10)
                free(tt(d_QK, d_ET, unit(S, 10), MUL), S, 10)
                finished(dve, S, it, 11)
                for e in range(2):
                    for c in range(LT):
                        t = slice(c * P, (c + 1) * P)
                        last = ts(d_kend[:, e, t], unit(S, 11)[:, e, t], colh(3, c, it, e), None, MUL)
                free(last, S, 11)
                finished(dve, S, it, 12)
                free(cp(d_V, unit(S, 12)), S, 12)
                for l in range(7):
                    j = 13 + 3 * l
                    if l < 6:
                        finished(dve, S, it, j + 1)
                        free(tt(d_T, d_T, unit(S, j + 1), SUB), S, j + 1)
                    k = j + 2 if l < 6 else j + 1
                    finished(dve, S, it, k)
                    free(tt(d_U, d_U, unit(S, k), SUB), S, k)
                    emptied(dve, S, it, k)
                    if l < 6:
                        emptied(dve, S, it, j + 1)
                    if l + 2 < 7:
                        level_mask(l + 2)
                    if l == 0:
                        dve.wait_ge(d_exp, it * 2 + 2)
                        tt(d_qE, d_q, d_v, MUL)
                        dve.memset(d_S[:, :, :], 0.0).then_inc(d_qe, 1)
                for c in range(LT):
                    t, j = slice(c * P, (c + 1) * P), 33 + 4 * c
                    finished(dve, S, it, j)
                    for e in range(2):
                        ins = stt(d_r[:, e, :], unit(S, j)[:, e, 0:P], colh(2, c, it, e), d_V[:, e, t], MUL, ADD)
                        if e:
                            free(ins, S, j)
                        else:
                            st.did(ins)
                    emptied(dve, S, it, j)
                    st.settle()
                    for e in range(2):
                        ins = ts(d_r[:, e, :], d_r[:, e, :], colh(0, c, it, e), None, MUL)
                    ins.then_inc(d_rr, 1)
                    finished(dve, S, it, j + 3)
                    for e in range(2):
                        ins = stt(d_S[:, e, :], d_S[:, e, :], colh(4, c, it, e), unit(S, j + 3)[:, e, 0:P], MUL, ADD)
                    free(ins, S, j + 3)
                    emptied(dve, S, it, j + 3)
                emptied(dve, S, it, 49)
                st.did(dve.reciprocal(d_Y, d_Y))
                st.settle()
                st.did(stt(d_o, d_o, col("gdn_norm_w", 0), d_Y, MUL, MUL))
                st.settle()
                tt(d_out[:, bass.ds(it * 2, 2), :], d_o, d_z, MUL).then_inc(d_done, 1)
            st.leave(GDN_H // 2)

            def add_residual(stage, l, q, loop):
                if not loop:
                    for j in range(8):
                        finished(dve, stage, 0, j)
                        free(stt(xT[:, j, CTX:T], unit(stage, j)[:, 0, :], dcol[:, l, q, j, 0:1], xT[:, j, CTX:T], MUL, ADD), stage, j)
                    return
                with dve.Fori(0, 4) as it:
                    for j in range(2):
                        finished(dve, stage, it, j)
                        x = xT[:, bass.ds(it * 2 + j, 1), CTX:T]
                        free(stt(x, unit(stage, j)[:, 0:1, :], dcol[:, l, q, bass.ds(it * 2 + j, 1), 0], x, MUL, ADD), stage, j)

            def layer_norm(name, i):
                dve.wait_ge(n_mean, i + 1)
                for b in range(DB):
                    stt(xT[:, b, CTX:T], sc[:, 0, 1, :], -1.0 / D, xT[:, b, CTX:T], MUL, ADD).then_inc(n_cent, 1)
                reciprocal_of(name, SEQ)
                for b in range(DB):
                    tt(xT[:, b, CTX:T], xT[:, b, CTX:T], rstd[:, 0:SEQ], MUL).then_inc(n_mul, 1)

            def ffn(i):
                up = f"ffn{i}_up"
                dve.memset(gpad[:, :, 0:2], 0.0).then_inc(f_conv, 1)
                with dve.Fori(0, HIDB // 2) as it:
                    st.enter(it, 2 * 2)
                    emptied(dve, up, it, 0)
                    for tap in (2, 0, 1):
                        for b in range(2):
                            w = dyncol(f"conv_w{i}", it * 2 + (HIDB * tap + b))
                            s = gpad[:, b, tap:tap + SEQ]
                            if tap == 2:
                                ins = ts(gconv[:, b, :], s, w, dyncol("conv_b", it * 2 + (HIDB * i + b)), MUL, ADD)
                            else:
                                ins = stt(gconv[:, b, :], s, w, gconv[:, b, :], MUL, ADD)
                            if tap == 1 and b == 1:
                                ins.then_inc(f_conv, 1)
                            elif tap == 1:
                                pass
                            else:
                                st.did(ins)
                        if tap != 1:
                            st.settle()
                    dve.wait_ge(f_silu, it * 1 + (HIDB // 2 * i + 1))
                    finished(dve, up, it, 1)
                    free(tt(hid2[:, bass.ds(it * 2, 2), :], gsilu, unit(up, 1), MUL), up, 1)
                st.leave(HIDB // 2)

            add_residual("gdn_out", 2, 1, False)
            layer_norm("ln0", 0)
            ffn(0)
            add_residual("ffn0_down", 2, 3, True)
            layer_norm("ln0f", 1)

            dve.memset(gpad[:, :, 0:2], 0.0).then_inc(r_done, 1)
            dve.wait_ge(rtab_in, 16)
            tcos, tsin = r_tab[:, 0, :], r_tab[:, 1, :]
            S = "ret_head"
            with dve.Fori(0, RET_H) as it:
                st.enter(it, 10)
                for i in range(2):
                    emptied(dve, S, it, i)
                    a, b = r_raw[:, i, 0, :], r_raw[:, i, 1, :]
                    oa, ob = r_rot[:, i, 0, :], r_rot[:, i, 1, :]
                    st.did(tt(r_tmp[:, 0, :], b, tsin, MUL))
                    st.did(tt(r_tmp[:, 1, :], b, tcos, MUL))
                    st.did(tt(oa, a, tcos, MUL))
                    st.did(tt(ob, a, tsin, MUL))
                    st.settle()
                    tt(oa, oa, r_tmp[:, 0, :], SUB)
                    tt(ob, ob, r_tmp[:, 1, :], ADD).then_inc(r_rotd, 1)
                    dve.wait_ge(r_rotd, it * 2 + i + 1)
                for j in range(2):
                    finished(dve, S, it, 2 + j)
                    free(cp(r_v[:, 2 * j:2 * j + 2, :], unit(S, 2 + j)), S, 2 + j)
                for j in range(2):
                    finished(dve, S, it, 6 + j)
                    for i in range(2):
                        t = 2 * j + i
                        w = SEQ - t * P
                        ins = tt(r_s[:, t:t + 1, 0:w], unit(S, 6 + j)[:, i:i + 1, 0:w],
                                 r_tab[:, bass.ds(it * 1 + 2, 1), 0:w], MUL)
                    free(ins, S, 6 + j)
                for j in range(2):
                    finished(dve, S, it, 8 + j)
                    free(cp(r_o[:, 2 * j:2 * j + 2, :], unit(S, 8 + j)), S, 8 + j)
                emptied(dve, S, it, 8)
                emptied(dve, S, it, 9)
                finished(dve, S, it, 10)
                for b in range(4):
                    ins = stt(r_o[:, b, :], unit(S, 10)[:, 0, :], -1.0 / RET_DV, r_o[:, b, :], MUL, ADD)
                    if b < 3:
                        ins.then_inc(r_cent, 1)
                    else:
                        free(ins, S, 10)
                emptied(dve, S, it, 11)
                st.did(dve.reciprocal(rstd[:, 0:SEQ], rstd[:, 0:SEQ]))
                st.settle()
                st.did(tt(r_o, r_o, rstd[:, 0:SEQ].unsqueeze(1).to_broadcast([P, 4, SEQ]), MUL))
                st.settle()
                tt(r_out[:, bass.ds(it * 4, 4), :], r_o, r_gate, MUL).then_inc(r_done, 1)
            st.leave(RET_H)
            add_residual("ret_out", 3, 1, False)
            layer_norm("ln1", 2)
            ffn(1)
            add_residual("ffn1_down", 3, 3, True)
            layer_norm("ln1f", 3)
            for t in range(LT):
                dve.wait_ge(o_turned, t + 1)
                cp(o_tok[:, t, :], flat(sc[:, t % 2])).then_inc(o_moved, 1)


def tables():
    f = np.float32
    eye = np.eye(P, dtype=f)
    base = np.concatenate([eye, np.ones((P, P), f)], 1)
    i, j = np.arange(P)[None, :], np.arange(P)[:, None]
    swap = np.zeros((64, 64), f)
    for g in (0, 32):
        for a in range(16):
            swap[g + a, g + 16 + a], swap[g + 16 + a, g + a] = -1.0, 1.0
    rot2 = np.kron(np.eye(2, dtype=f), swap).T
    pad = np.zeros((64, P), f)
    dup = np.concatenate([np.concatenate([np.eye(64, dtype=f)] * 2, 1), pad], 0)
    rotdup = np.concatenate([np.concatenate([swap.T] * 2, 1), pad], 0)
    tok = np.arange(SEQ)
    inv = (f(10000.0) ** (-np.arange(0, 32, 2, dtype=f) / f(32))).astype(f)
    ang = np.concatenate([inv[:, None] * (tok // 64).astype(f)] * 2 + [inv[:, None] * (tok % 64).astype(f)] * 2, 0)
    ang = np.concatenate([ang, ang], 0).astype(f)
    mla = np.concatenate([rot2, dup, rotdup, np.cos(ang), np.sin(ang)], 1)
    keep = np.ones((P, T), f)
    keep[:, ::64] = 0.0
    gla = np.concatenate([keep, j <= i, j >= i], 1)
    lv = [((i // (2 * s)) == (j // (2 * s))) & ((i // s) % 2 == 1) & ((j // s) % 2 == 0) for s in LEVELS]
    last = np.zeros((P, P), f)
    last[P - 1] = 1.0
    keep = np.ones((P, SEQ), f)
    keep[:, ::P] = 0.0
    gdn = np.concatenate(lv + [j <= i, last, keep], 1)
    inv = (f(10000.0) ** (-np.linspace(0.0, 1.0, P, dtype=f))).astype(f)
    ang = (inv[:, None] * tok.astype(f)[None, :]).astype(f)
    rel = np.arange(SEQ, dtype=f)[None, :] - np.arange(P, dtype=f)[:, None]
    lg = np.log(f(1.0) - np.power(f(2.0), f(-5.0) - np.arange(RET_H, dtype=f))).astype(f)
    dec = [np.where(rel >= 0, np.exp(np.maximum(rel, f(0)) * g), f(0)) for g in lg]
    ret = np.concatenate([np.cos(ang), np.sin(ang)] + dec, 1)
    return {n: np.ascontiguousarray(a, dtype=f) for n, a in
            (("tab_base", base), ("tab_mla", mla), ("tab_gla", gla), ("tab_gdn", gdn), ("tab_ret", ret))}


INPUTS = ["x", "c", "ctx", "c_ctx", "ada_w", "ada_b", "norm_g", "mlp_w1", "mlp_w2", "mla_w_dq", "mla_g_q", "mla_w_uq",
          "mla_w_dkv", "mla_g_kv", "mla_w_ukv", "mla_w_o", "gla_w_q", "gla_w_k", "gla_w_v", "gla_w_r", "gla_w_gate1",
          "gla_w_gate2", "gla_b_gate", "gla_g_o", "gla_w_o", "c_2", "cond_w_2", "cond_b_2", "ada_w_2", "ada_b_2",
          "ln_g_2", "ln_b_2", "ffn_up_2", "ffn_conv_w_2", "ffn_conv_b_2", "ffn_down_2", "gdn_w_in_2", "gdn_conv_w_2",
          "gdn_a_log_2", "gdn_dt_bias_2", "gdn_norm_w_2", "gdn_w_out_2", "ret_w_in_2", "ret_w_out_2"]


def kernel(**inputs):
    import numpy as _np
    import concourse.bacc as _bacc
    from concourse import mybir as _mybir
    from concourse.bass_utils import run_bass_kernel_spmd as _run

    nc = _bacc.Bacc("TRN2", target_bir_lowering=False, num_devices=1)
    given = {n: _np.ascontiguousarray(inputs[n]) for n in INPUTS}
    given.update(tables())
    arrays, A = {}, {}
    for name, a in given.items():
        arrays[f"in_{name}"] = a
        A[name] = nc.dram_tensor(f"in_{name}", a.shape, _mybir.dt.from_np(a.dtype), kind="ExternalInput").ap()
    out = nc.dram_tensor("out_0", (1, SEQ, D), _mybir.dt.float32, kind="ExternalOutput").ap()
    first_and_second_block(nc, A, out)
    r = _run(nc, [arrays], core_ids=[0])
    return r.results[0]["out_0"]
```

```python
import numpy as np
import concourse.bass as bass
from concourse import mybir
from contextlib import ExitStack

ACT = mybir.ActivationFunctionType
ALU = mybir.AluOpType
F32 = mybir.dt.float32
U32 = mybir.dt.uint32
XY = mybir.AxisListType.XY

P = 128
D = 1024
DB = D // P
CTX, SEQ = 256, 512
T = CTX + SEQ
HALF = T // 2
FF = 4096
FFB = FF // P
HID = 2816
HIDB = HID // P
MLA_H, NOPE, ROPE, Q_RANK, KV_RANK = 8, 128, 64, 384, 256
GLA_H, GLA_DV, GATE_RANK = 4, 256, 16
GDN_H = 8
RET_H, RET_DV = 4, 512
ALPHA = (2.0 * 2) ** 0.25
QT, KT = T // P, T // P
LT = SEQ // P
LEVELS = [1, 2, 4, 8, 16, 32, 64]

VEC = {}
_rows = 0
for _name, _n in [
    ("ada_b", 96), ("c", 8), ("c_ctx", 8), ("c_2", 8), ("cond_b", 8),
    ("ada_b_2", 96), ("ln_g_2", 32),
    ("norm_g", 64), ("ln_b_2", 32), ("mla_g_q", 3), ("mla_g_kv", 2), ("gla_b_gate", 8), ("gla_g_o", 2),
    ("gdn_norm_w", 1), ("pad", 16),
    ("conv_w0", 66), ("conv_b", 44), ("pad2", 18),
    ("conv_w1", 66), ("pad3", 62),
    ("gdn_conv_w", 96), ("pad4", 32),
]:
    VEC[_name] = (_rows // P, _rows % P, _n)
    _rows += _n
VEC_TILES = _rows // P

STAGES = [
    ("ada", 1, 4, 0),
    ("mla_in", 1, 2, 6), ("mla_rope", 1, 0, 2), ("mla_pair", 4, 6, 34), ("mla_out", 1, 2, 8),
    ("mlp0_up", 4, 2, 8), ("mlp0_down", 4, 2, 2),
    ("gla_gate", 1, 0, 2), ("gla_head", 4, 4, 16), ("gla_out", 1, 2, 8),
    ("mlp1_up", 4, 2, 8), ("mlp1_down", 4, 2, 2),
    ("gdn_gate", 1, 0, 2), ("gdn_pair", 4, 4, 50), ("gdn_out", 1, 2, 8),
    ("ffn0_up", 11, 2, 2), ("ffn0_down", 4, 2, 2),
    ("ret_head", 4, 4, 12), ("ret_out", 1, 4, 8),
    ("ffn1_up", 11, 2, 2), ("ffn1_down", 4, 2, 2),
]
GROUP0, UNIT0, GROUPS, UNITS = {}, {}, {}, {}
_g = _u = 0
for _s, _n, _gi, _ui in STAGES:
    GROUP0[_s], UNIT0[_s], GROUPS[_s], UNITS[_s] = _g, _u, _gi, _ui
    _g, _u = _g + _n * _gi, _u + _n * _ui
    assert _gi % 2 == 0 and _ui % 2 == 0

MOD_SLOTS, MOD_Q = 4, 2
MOD_K = DB // MOD_Q
MOD_CHUNKS = 6 * DB
MOD_IT, MOD_UNIT = MOD_CHUNKS // 4, MOD_CHUNKS // 8
MOD_AT = 512 - 96

NORMS = {}
_b = 0
for _k, (_s, _n) in enumerate([
    ("h0", 8), ("cq", 3), ("ckv", 2), ("y0", 8), ("h0m", 8), ("y0m", 8),
    ("h1", 8), ("y1", 8), ("h1m", 8), ("y1m", 8),
    ("ln0", 8), ("ln0f", 8), ("ln1", 8), ("ln1f", 8),
]):
    NORMS[_s] = (_k, _b, _n)
    _b += _n


class Steps:

    def __init__(self, eng, sem):
        self.eng, self.sem, self.n, self.it, self.per, self.local = eng, sem, 0, None, 0, 0

    def did(self, ins):
        ins.then_inc(self.sem, 1)
        if self.it is None:
            self.n += 1
        else:
            self.local += 1

    def settle(self):
        v = self.n if self.it is None else self.it * self.per + (self.n + self.local)
        self.eng.wait_ge(self.sem, v)

    def enter(self, it, per):
        self.it, self.per, self.local = it, per, 0

    def leave(self, iterations):
        assert self.local == self.per, (self.local, self.per)
        self.n, self.it = self.n + iterations * self.per, None


def first_and_second_block(nc, A, out):
    ctx = ExitStack()
    with ctx:
        def sb(name, shape, dt=F32):
            return ctx.enter_context(nc.sbuf_tensor(name, shape, dt))

        def sem(name):
            return ctx.enter_context(nc.semaphore(name))

        xT = sb("xT", [P, DB, T])
        hT = sb("hT", [P, DB, T])
        arena = sb("arena", [P, FFB * T])
        wring = [sb(f"wring{s}", [P, 4096]) for s in range(2)]
        base_tab = sb("base_tab", [P, 2 * P])
        ident, ones = base_tab[:, 0:P], base_tab[:, P:2 * P]
        tab = sb("tab", [P, 2048])
        cols = sb("cols", [P, VEC_TILES, P])
        cs = sb("cs", [P, DB, 3])
        mod = sb("mod", [P, 4, 48, 2])
        dcol = sb("dcol", [P, 4, 4, DB, 2])
        eps = sb("eps", [P, 2])
        sq = sb("sq", [P, 2, T])
        rstd = sb("rstd", [P, T])
        gate1 = sb("gate1", [P, DB, 2, GATE_RANK])
        gate2 = sb("gate2", [GATE_RANK, 2, P])
        w_ab = sb("w_ab", [P, DB, 16])
        a_dt = sb("a_dt", [GDN_H, 3])
        d_row = sb("d_row", [GDN_H, 2, SEQ])
        d_col = sb("d_col", [P, 5, LT, GDN_H])
        acc = ctx.enter_context(nc.psum_tensor("acc", [P, 2, 2, 512], F32))
        sc = ctx.enter_context(nc.psum_tensor("sc", [P, 2, 2, 512], F32))

        at = [0]

        def carve(*shape):
            n = int(np.prod(shape))
            a = arena[:, at[0]:at[0] + n]
            at[0] += n
            assert at[0] <= FFB * T, at[0]
            if len(shape) == 1:
                return a
            names = " ".join(f"a{i}" for i in range(len(shape)))
            return a.rearrange(f"p ({names}) -> p {names}", **{f"a{i}": s for i, s in enumerate(shape)})

        x_tok = carve(QT, D)
        vrow = carve(VEC_TILES, P)
        at[0] = 0
        o_tok = carve(LT, D)
        at[0] = 0
        hid = carve(FFB, T)
        relu = sq
        at[0] = 0
        hid2 = carve(HIDB, SEQ)
        gpad = carve(2, SEQ + 2)
        gconv = carve(2, SEQ)
        gsilu = carve(2, SEQ)
        at[0] = 0
        cq = carve(3, T)
        ckv = carve(2, T)
        krope = carve(2, T)
        kraw = carve(T)
        ktmp = carve(SEQ)
        qn = carve(2, T)
        qr = carve(T)
        qraw = carve(T)
        kn = carve(2, T)
        vtok = carve(QT, 256)
        prob = carve(2, T)
        probT = carve(2, T)
        attn = carve(MLA_H, T)
        small = carve(2, 4)
        at[0] = 0
        hgate = carve(2, T)
        g_q = carve(SEQ)
        g_k = carve(T)
        g_v = carve(QT, GLA_DV)
        g_r = carve(2, SEQ)
        g_z = carve(2, T)
        g_l = carve(T)
        g_o = g_z[:, :, 0:SEQ]
        g_g = carve(T)
        g_G = carve(T)
        g_tot = carve(2, 12)
        g_et = carve(2, 12)
        g_dec = carve(2, QT)
        g_qt = carve(2, SEQ)
        g_kt = carve(2, SEQ)
        g_ke = carve(2, T)
        g_qS = carve(2, SEQ)
        g_kE = carve(2, T)
        g_kEt = carve(2, 5 * P)
        g_AT = carve(2, SEQ)
        g_S = carve(2, 5, GLA_DV)
        g_out = carve(DB, SEQ)
        at[0] = 0
        d_cp = carve(2, 2, SEQ + 3)
        d_q = carve(2, SEQ)
        d_k = carve(2, SEQ)
        d_v = carve(2, SEQ)
        d_z = carve(2, SEQ)
        d_gcR = carve(2, SEQ)
        d_o = d_gcR
        d_bR = carve(2, SEQ)
        d_ET = carve(2, SEQ)
        d_LT = carve(2, SEQ)
        d_Lm = carve(2, 2, SEQ)
        d_T = carve(2, SEQ)
        d_U = carve(2, SEQ)
        d_Y = carve(2, SEQ)
        d_QK = carve(2, SEQ)
        d_kend = carve(2, SEQ)
        d_V = carve(2, SEQ)
        d_qE = carve(2, SEQ)
        d_S = carve(2, P)
        d_r = carve(2, P)
        d_vn = carve(2, P)
        d_out = carve(GDN_H, SEQ)
        at[0] = 0
        r_tab = carve(6, SEQ)
        r_raw = carve(2, 2, SEQ)
        r_sqr = r_raw.rearrange("p a b n -> p (a b) n")
        r_tmp = carve(2, SEQ)
        r_rot = carve(2, 2, SEQ)
        r_v = carve(LT, RET_DV)
        r_gate = carve(4, SEQ)
        r_s = carve(LT, SEQ)
        r_o = carve(4, SEQ)
        r_out = carve(16, SEQ)

        mod_w = [a.rearrange("p (k n) -> p k n", k=MOD_K)
                 for a in (tab[:, 0:512], tab[:, 512:1024], tab[:, 1024:1536], rstd[:, 0:512])]
        mod_acc = tab[:, 1536:2048].rearrange("p (s v n) -> p s v n", s=2, v=2)
        mod_psum = sc[:, 1, 1, :]

        rot2, dup, rotdup = tab[:, 0:P], tab[0:64, P:2 * P], tab[0:64, 2 * P:3 * P]
        rcos, rsin = tab[:, 384:384 + SEQ], tab[:, 896:896 + SEQ]
        keep64, tri_fb = tab[:, 0:T], tab[:, T:T + 2 * P]
        lvl_mask = [tab[:, l * P:(l + 1) * P] for l in range(7)]
        causal, last_row, keep128 = tab[:, 896:1024], tab[:, 1024:1152], tab[:, 1152:1664]

        const_in = sem("const_in")
        x_in = sem("x_in")
        gate1_in, ab_in = sem("gate1_in"), sem("ab_in")
        tab_in, rtab_in = sem("tab_in"), sem("rtab_in")
        gate2_in = sem("gate2_in")
        out_done = sem("out_done")
        w_loaded = [sem(f"w_loaded{s}") for s in range(2)]
        w_used = sem("w_used")
        acc_ready = sem("acc_ready")
        acc_free = [sem(f"acc_free{s}") for s in range(2)]
        dve_step, act_step = sem("dve_step"), sem("act_step")
        vec_turned, cols_ready = sem("vec_turned"), sem("cols_ready")
        x_turned, x_moved = sem("x_turned"), sem("x_moved")
        c_ready, e_ready = sem("c_ready"), sem("e_ready")
        ada_done, mod_ready = sem("ada_done"), sem("mod_ready")
        mod_loaded = [sem(f"mod_loaded{s}") for s in range(MOD_SLOTS)]
        mod_used = [sem(f"mod_used{s}") for s in range(MOD_SLOTS)]
        mod_summed = sem("mod_summed")
        x_ready = sem("x_ready")
        n_sq, n_used = sem("n_sq"), sem("n_used")
        n_std = sem("n_std")
        n_mul, h_ready = sem("n_mul"), sem("h_ready")
        n_mean, n_cent = sem("n_mean"), sem("n_cent")
        lat_ready, krope_ready = sem("lat_ready"), sem("krope_ready")
        qrope_ready, s_ready = sem("qrope_ready"), sem("s_ready")
        p_max, p_exp, p_ready = sem("p_max"), sem("p_exp"), sem("p_ready")
        relu_free = sem("relu_free")
        gl_ready, gG_ready, gE_ready = sem("gl_ready"), sem("gG_ready"), sem("gE_ready")
        gk_ready, gsq_ready = sem("gk_ready"), sem("gsq_ready")
        gr_ready, gss_ready, gdev_ready = sem("gr_ready"), sem("gss_ready"), sem("gdev_ready")
        g_done = sem("g_done")
        d_rows, d_cols, d_ga, d_gc = sem("d_rows"), sem("d_cols"), sem("d_ga"), sem("d_gc")
        d_masked, d_conv, d_silu = sem("d_masked"), sem("d_conv"), sem("d_silu")
        d_sq, d_std, d_norm, d_diff = sem("d_sq"), sem("d_std"), sem("d_norm"), sem("d_diff")
        d_exp, d_lt, d_lm, d_qe = sem("d_exp"), sem("d_lt"), sem("d_lm"), sem("d_qe")
        d_init, d_rr, d_done, d_glr = sem("d_init"), sem("d_rr"), sem("d_done"), sem("d_glr")
        f_conv, f_silu = sem("f_conv"), sem("f_silu")
        r_rotd, r_cent, r_sq, r_done = sem("r_rotd"), sem("r_cent"), sem("r_sq"), sem("r_done")
        o_turned, o_moved = sem("o_turned"), sem("o_moved")

        def unit(stage, j):
            return acc[:, (UNIT0[stage] + j) % 2]

        def flat(a):
            return a.rearrange("p a n -> p (a n)")

        def halves(a):
            return a.rearrange("p (h n) -> p h n", h=2)

        def chunks(a):
            return a.rearrange("p e (c n) -> p (e c) n", n=P)

        def loaded(eng, stage, it, j):
            g = GROUP0[stage] + j
            eng.wait_ge(w_loaded[g % 2], 16 * (g // 2 + 1) + it * (8 * GROUPS[stage]))
            return g % 2

        def finished(eng, stage, it, j):
            eng.wait_ge(acc_ready, UNIT0[stage] + j + 1 + it * UNITS[stage])

        def emptied(eng, stage, it, j):
            u = UNIT0[stage] + j
            eng.wait_ge(acc_free[u % 2], u // 2 + 1 + it * (UNITS[stage] // 2))

        def claim(eng, stage, it, j):
            u = UNIT0[stage] + j
            if u >= 2:
                eng.wait_ge(acc_free[u % 2], u // 2 + it * (UNITS[stage] // 2))

        def free(ins, stage, j):
            ins.then_inc(acc_free[(UNIT0[stage] + j) % 2], 1)

        def col(name, i):
            t, r, _ = VEC[name]
            return cols[:, t, r + i:r + i + 1]

        def vec(name, i, n):
            t, r, _ = VEC[name]
            return cols[:, t, r + i:r + i + n]

        def dyncol(name, i):
            t, r, _ = VEC[name]
            return cols[:, t, bass.ds(i + r, 1)]

        def mod_slot(i, q):
            return (MOD_Q * i + q) % MOD_SLOTS

        def piece(phase, it, i, by=1):
            a = MOD_SLOTS // MOD_Q
            return by * ((MOD_CHUNKS * phase + i) // a + 1) + it * (by * MOD_IT // a)

        rows = lambda a: a.rearrange("(r p) -> r p", p=P)
        rows2 = lambda a: a.rearrange("l (r p) -> (l r) p", p=P)
        rows3 = lambda a: a.rearrange("l i (r p) -> (l i r) p", p=P)
        vec_sources = [
            ("ada_b", rows2(A["ada_b"])), ("c", rows2(A["c"])), ("c_ctx", rows(A["c_ctx"])), ("c_2", rows2(A["c_2"])),
            ("cond_b", rows(A["cond_b_2"])), ("ada_b_2", rows2(A["ada_b_2"])), ("ln_g_2", rows3(A["ln_g_2"])),
            ("norm_g", rows3(A["norm_g"])), ("ln_b_2", rows3(A["ln_b_2"])), ("mla_g_q", rows2(A["mla_g_q"])),
            ("mla_g_kv", rows2(A["mla_g_kv"])), ("gla_b_gate", rows3(A["gla_b_gate"])), ("gla_g_o", rows2(A["gla_g_o"])),
            ("gdn_norm_w", rows(A["gdn_norm_w_2"])), ("conv_w0", rows2(A["ffn_conv_w_2"][0])),
            ("conv_b", rows2(A["ffn_conv_b_2"])), ("conv_w1", rows2(A["ffn_conv_w_2"][1])),
            ("gdn_conv_w", rows2(A["gdn_conv_w_2"])),
        ]
        consts = 16 * (1 + len(vec_sources))
        vec_rows = [max(VEC[n][1] + VEC[n][2] for n, _ in vec_sources if VEC[n][0] == t) for t in range(VEC_TILES)]

        block = ctx.enter_context(nc.Block())

        @block.sync
        def _(sp):
            def slot_free(stage, it, j):
                g = GROUP0[stage] + j
                if g >= 2:
                    sp.wait_ge(w_used, g + it * GROUPS[stage])
                return g % 2

            def load(stage, it, j, src, k, n):
                s = slot_free(stage, it, j)
                dst = wring[s][:, 0:k * n].rearrange("p (k n) -> p k n", k=k)
                sp.dma_start(dst, src).then_inc(w_loaded[s], 16)

            def blocks(w):
                return w.rearrange("(k p) n -> p k n", p=P)

            aw = [blocks(A["ada_w" if l < 2 else "ada_w_2"][l % 2]) for l in range(4)]
            for j in range(4):
                load("ada", 0, j, aw[0][:, :, j * 512:(j + 1) * 512], DB, 512)

            def in_columns(stage, w, n, k):
                wv, its = blocks(w), w.shape[1] // n // 2
                if dict((s, i) for s, i, _, _ in STAGES)[stage] == 1:
                    for j in range(2 * its):
                        load(stage, 0, j, wv[:, :, j * n:(j + 1) * n], k, n)
                    return
                with sp.Fori(0, its) as it:
                    for j in range(2):
                        load(stage, it, j, wv[:, :, bass.ds(it * (2 * n) + j * n, n)], k, n)

            def down(stage, w, k, phase=None):
                wv = blocks(w)
                if phase is not None:
                    sp.wait_ge(n_mul, (16, 32, 40)[phase])
                with sp.Fori(0, 4) as it:
                    for j in range(2):
                        load(stage, it, j, wv[:, :, bass.ds(it * (2 * P) + j * P, P)], k, P)
                        if phase is None:
                            continue
                        for i in range(j * MOD_UNIT, (j + 1) * MOD_UNIT):
                            for q in range(MOD_Q):
                                s = mod_slot(i, q)
                                sp.wait_ge(mod_used[s], piece(phase, it, i))
                                sp.dma_start(mod_w[s], aw[phase + 1][:, MOD_K * q:MOD_K * (q + 1), bass.ds(
                                    it * (MOD_IT * P) + i * P, P)]).then_inc(mod_loaded[s], 16)

            load("mla_in", 0, 0, blocks(A["mla_w_dq"][0]), DB, Q_RANK)
            load("mla_in", 0, 1, blocks(A["mla_w_dkv"][0]), DB, KV_RANK + ROPE)
            cw = blocks(A["cond_w_2"])
            uq, ukv = blocks(A["mla_w_uq"][0]), blocks(A["mla_w_ukv"][0])
            with sp.Fori(0, MLA_H // 2) as it:
                load("mla_pair", it, 0, uq[:, :, bass.ds(it * 384, 384)], 3, 384)
                load("mla_pair", it, 1, ukv[:, :, bass.ds(it * 512, 512)], 2, 512)
                for j in range(2):
                    load("mla_pair", it, 2 + j, aw[0][:, :, bass.ds(it * 1024 + 2 * D + j * 512, 512)], DB, 512)
                for j in range(2):
                    load("mla_pair", it, 4 + j, cw[:, :, bass.ds(it * 256 + j * P, P)], DB, P)
            in_columns("mla_out", A["mla_w_o"][0], 512, DB)
            in_columns("mlp0_up", A["mlp_w1"][0], 512, DB)
            down("mlp0_down", A["mlp_w2"][0], FFB, 0)
            gq, gk, gv, gr = (blocks(A[n][0]) for n in ("gla_w_q", "gla_w_k", "gla_w_v", "gla_w_r"))
            w2 = A["gla_w_gate2"][0].rearrange("d r n -> r d n")
            with sp.Fori(0, GLA_H) as it:
                sp.wait_ge(acc_ready, UNIT0["gla_head"] - UNITS["gla_head"] + 2 + it * UNITS["gla_head"])
                sp.dma_start(gate2[:, :, :], w2[:, :, bass.ds(it * P, P)]).then_inc(gate2_in, 16)
                load("gla_head", it, 0, gq[:, :, bass.ds(it * P, P)], DB, P)
                load("gla_head", it, 1, gk[:, :, bass.ds(it * P, P)], DB, P)
                load("gla_head", it, 2, gv[:, :, bass.ds(it * GLA_DV, GLA_DV)], DB, GLA_DV)
                load("gla_head", it, 3, gr[:, :, bass.ds(it * GLA_DV, GLA_DV)], DB, GLA_DV)
            in_columns("gla_out", A["gla_w_o"][0], 512, DB)
            in_columns("mlp1_up", A["mlp_w1"][1], 512, DB)
            sp.wait_ge(g_done, GLA_H + 1)
            down("mlp1_down", A["mlp_w2"][1], FFB, 1)
            gi = blocks(A["gdn_w_in_2"])
            with sp.Fori(0, GDN_H // 2) as it:
                for j in range(4):
                    load("gdn_pair", it, j, gi[:, :, bass.ds(it * 256 + j * D, 256)], DB, 256)
            in_columns("gdn_out", A["gdn_w_out_2"], 512, DB)

            def ffn(i):
                up = blocks(A["ffn_up_2"][i])
                with sp.Fori(0, HIDB // 2) as it:
                    for j in range(2):
                        load(f"ffn{i}_up", it, j, up[:, :, bass.ds(it * 256 + j * HID, 256)], DB, 256)
                if i == 0:
                    sp.wait_ge(d_done, GDN_H // 2 + 1)
                down(f"ffn{i}_down", A["ffn_down_2"][i], HIDB, 2 if i == 0 else None)

            ffn(0)
            ri = blocks(A["ret_w_in_2"])
            with sp.Fori(0, RET_H) as it:
                load("ret_head", it, 0, ri[:, :, bass.ds(it * 256, 256)], DB, 256)
                load("ret_head", it, 1, ri[:, :, bass.ds(it * 256 + D, 256)], DB, 256)
                load("ret_head", it, 2, ri[:, :, bass.ds(it * 512 + 2 * D, 512)], DB, 512)
                load("ret_head", it, 3, ri[:, :, bass.ds(it * 512 + 4 * D, 512)], DB, 512)
            ro = blocks(A["ret_w_out_2"])
            for j in range(4):
                load("ret_out", 0, j, ro[:, :, j * 256:(j + 1) * 256], 16, 256)
            ffn(1)
            for t in range(LT):
                sp.wait_ge(o_moved, t + 1)
                sp.dma_start(out[0, t * P:(t + 1) * P, :], o_tok[:, t, :]).then_inc(out_done, 16)
            sp.wait_ge(out_done, 16 * LT)

        @block.tensor
        def _(pe):
            def group(stage, it, j, k, n):
                s = loaded(pe, stage, it, j)
                begun[0] = True
                return wring[s][:, 0:k * n].rearrange("p (k n) -> p k n", k=k)

            begun = [False]

            def mm(o, lhsT, rhs, start, stop):
                ins = pe.matmul(o, lhsT, rhs, start=start, stop=stop)
                if begun[0]:
                    ins.then_inc(w_used, 1)
                    begun[0] = False
                return ins

            def linear(u, w, m, x, n, nk, rows=P, at=0):
                for k in range(nk):
                    if n == T:
                        for h in range(2):
                            last = mm(u[at:at + rows, h, 0:HALF], w[:, k, m:m + rows],
                                      x(k)[:, h * HALF:(h + 1) * HALF], k == 0, k == nk - 1)
                    else:
                        last = mm(u[at:at + rows, 0, 0:n], w[:, k, m:m + rows], x(k), k == 0, k == nk - 1)
                return last

            def square_sum(name, n):
                _, b0, nb = NORMS[name]
                for b in range(nb):
                    pe.wait_ge(n_sq, b0 + b + 1)
                    s = sq[:, (b0 + b) % 2]
                    if n == T:
                        for h in range(2):
                            last = pe.matmul(sc[:, 0, h, 0:HALF], ones, s[:, h * HALF:(h + 1) * HALF],
                                             start=b == 0, stop=b == nb - 1)
                    else:
                        last = pe.matmul(sc[:, 0, 0, 0:n], ones, s[:, 0:n], start=b == 0, stop=b == nb - 1)
                    last.then_inc(n_used, 1)

            def mean_sum(stage):
                for b in range(DB):
                    emptied(pe, stage, *divmod(b, UNITS[stage]))
                    last = pe.matmul(sc[:, 0, 1, :], ones, xT[:, b, CTX:T], start=b == 0, stop=b == DB - 1)
                last.then_inc(n_mean, 1)

            seq_h = lambda k: hT[:, k, CTX:T]
            all_h = lambda k: hT[:, k, :]

            pe.wait_ge(const_in, consts)
            for t in range(VEC_TILES):
                n = vec_rows[t]
                last = pe.transpose(flat(acc[:, 0])[:, t * P:t * P + n], vrow[0:n, t, :], ident[0:n, 0:n])
            last.then_inc(vec_turned, 1)
            pe.wait_ge(x_in, 32)
            for b in range(DB):
                if b >= 2:
                    pe.wait_ge(x_moved, b - 1)
                for t in range(QT):
                    last = pe.transpose(flat(sc[:, b % 2])[:, t * P:(t + 1) * P],
                                        x_tok[:, t, b * P:(b + 1) * P], ident)
                last.then_inc(x_turned, 1)
            square_sum("h0", T)
            pe.wait_ge(c_ready, 1)

            def modulation(w, m, o, x):
                for k in range(DB):
                    last = mm(o, w[:, k, m * P:(m + 1) * P], x(k), k == 0, k == DB - 1)
                return last

            for j in range(4):
                w = group("ada", 0, j, DB, 512)
                for m in range(4):
                    c = MOD_AT + (4 * j + m) * 2
                    last = modulation(w, m, mod_psum[:, c:c + 2], lambda k: cs[:, k, 0:2])
            last.then_inc(ada_done, 1)

            def mod_sum(phase, it, i, nv):
                pe.wait_ge(mod_used[mod_slot(i, MOD_Q - 1)], piece(phase, it, i) + 1)
                for v in range(nv):
                    last = pe.matmul(mod_psum[:, bass.ds(it * (MOD_IT * nv) + (MOD_AT + i * nv + v), 1)],
                                     mod_acc[:, i % 2, v, :], ones[:, 0:1], start=True, stop=True)
                last.then_inc(mod_summed, 1)

            def down(stage, n, h, nk, phase=None, nv=1):
                with pe.Fori(0, 4) as it:
                    for j in range(2):
                        w = group(stage, it, j, nk, P)
                        claim(pe, stage, it, j)
                        for k in range(nk):
                            if n == T:
                                for s in range(2):
                                    last = mm(unit(stage, j)[:, s, 0:HALF], w[:, k, :], h(k)[:, s * HALF:(s + 1) * HALF],
                                              k == 0, k == nk - 1)
                            else:
                                last = mm(unit(stage, j)[:, 0, 0:n], w[:, k, :], h(k), k == 0, k == nk - 1)
                            ahead, rest = divmod(nk - 1 - k, nk // (MOD_UNIT + 1))
                            if phase is not None and rest == 0 and ahead < MOD_UNIT:
                                mod_sum(phase, it, (j + 1) * MOD_UNIT - 1 - ahead, nv)
                        last.then_inc(acc_ready, 1)

            pe.wait_ge(h_ready, 8)
            w = group("mla_in", 0, 0, DB, Q_RANK)
            for j in range(6):
                if j == 3:
                    w = group("mla_in", 0, 1, DB, KV_RANK + ROPE)
                claim(pe, "mla_in", 0, j)
                linear(unit("mla_in", j), w, (j % 3) * P, all_h, T, DB,
                       rows=P if j < 5 else ROPE).then_inc(acc_ready, 1)
            emptied(pe, "mla_in", 0, 5)
            pe.wait_ge(tab_in, 16)
            claim(pe, "mla_rope", 0, 0)
            for h in range(2):
                last = pe.matmul(unit("mla_rope", 0)[:, h, 0:HALF], dup, kraw[0:64, h * HALF:(h + 1) * HALF],
                                 start=True, stop=True)
            last.then_inc(acc_ready, 1)
            claim(pe, "mla_rope", 0, 1)
            pe.matmul(unit("mla_rope", 1)[:, 0, :], rotdup, kraw[0:64, CTX:T], start=True,
                      stop=True).then_inc(acc_ready, 1)
            square_sum("cq", T)
            square_sum("ckv", T)
            pe.wait_ge(lat_ready, 5)
            pe.wait_ge(krope_ready, 2)
            S = "mla_pair"
            columns = [None]
            with pe.Fori(0, MLA_H // 2) as it:
                wq = group(S, it, 0, 3, 384)
                for j, m in ((0, 0), (1, 192)):
                    claim(pe, S, it, j)
                    linear(unit(S, j), wq, m, lambda k: cq[:, k, :], T, 3).then_inc(acc_ready, 1)
                claim(pe, S, it, 2)
                linear(unit(S, 2), wq, 128, lambda k: cq[:, k, :], T, 3, rows=64)
                linear(unit(S, 2), wq, 320, lambda k: cq[:, k, :], T, 3, rows=64, at=64).then_inc(acc_ready, 1)
                wkv = group(S, it, 1, 2, 512)
                for j, m in ((3, 0), (4, 256)):
                    claim(pe, S, it, j)
                    linear(unit(S, j), wkv, m, lambda k: ckv[:, k, :], T, 2).then_inc(acc_ready, 1)
                wv = wkv.rearrange("p k (h s n) -> p k h s n", h=2, s=2)
                for j in range(3):
                    claim(pe, S, it, 5 + j)
                    for i in range(2):
                        t = 2 * j + i
                        for k in range(2):
                            last = mm(unit(S, 5 + j)[:, i, 0:256], ckv[:, k, t * P:(t + 1) * P],
                                      wv[:, k, :, 1, :], k == 0, k == 1)
                    last.then_inc(acc_ready, 1)
                emptied(pe, S, it, 2)
                for j in range(2):
                    claim(pe, S, it, 8 + j)
                    pe.matmul(unit(S, 8 + j)[:, 0, 0:256], rot2, qraw[:, CTX + 256 * j:CTX + 256 * (j + 1)],
                              start=True, stop=True).then_inc(acc_ready, 1)
                pe.wait_ge(qrope_ready, it * 1 + 1)

                def scores(n):
                    e, t = n // QT, n % QT
                    spans = [(0, 0, CTX)] if t < 2 else [(h, h * HALF, HALF) for h in range(2)]
                    for h, k0, w in spans:
                        pe.matmul(sc[:, n % 2, h, 0:w], qn[:, e, t * P:(t + 1) * P], kn[:, e, k0:k0 + w],
                                  start=True, stop=False)
                        last = pe.matmul(sc[:, n % 2, h, 0:w], qr[:, t * P:(t + 1) * P], krope[:, e, k0:k0 + w],
                                         start=False, stop=True)
                    last.then_inc(s_ready, 1)

                def weigh(n):
                    e, t = n // QT, n % QT
                    nk = 2 if t < 2 else KT
                    pe.wait_ge(p_ready, it * 12 + n + 1)
                    claim(pe, S, it, 10 + 2 * n)
                    for k in range(nk):
                        last = pe.transpose(flat(unit(S, 10 + 2 * n))[:, k * P:(k + 1) * P],
                                            prob[:, n % 2, k * P:(k + 1) * P], ident)
                    last.then_inc(acc_ready, 1)
                    claim(pe, S, it, 11 + 2 * n)
                    if n < 8:
                        if n % 4 == 0:
                            columns[0] = group(S, it, 2 + n // 4, DB, 512)
                        modulation(columns[0], n % 4, unit(S, 11 + 2 * n)[:, 1, 0:2], lambda k: cs[:, k, 0:2])
                    elif n < 10:
                        columns[0] = group(S, it, 4 + n - 8, DB, P)
                        modulation(columns[0], 0, unit(S, 11 + 2 * n)[:, 1, 0:1], lambda k: vec("c_2", k, 1))
                    emptied(pe, S, it, 10 + 2 * n)
                    for k in range(nk):
                        last = pe.matmul(unit(S, 11 + 2 * n)[:, 0, 0:P], vtok[:, k, e * P:(e + 1) * P],
                                         probT[:, n % 2, k * P:(k + 1) * P], start=k == 0, stop=k == nk - 1)
                    last.then_inc(acc_ready, 1)

                scores(0)
                for n in range(2 * QT):
                    if n + 1 < 2 * QT:
                        scores(n + 1)
                    weigh(n)

            def out_proj(stage, x, n, nk, per):
                for j in range(8):
                    if j % per == 0:
                        w = group(stage, 0, j // per, nk, per * P)
                    claim(pe, stage, 0, j)
                    linear(unit(stage, j), w, (j % per) * P, x, n, nk).then_inc(acc_ready, 1)

            emptied(pe, "mla_pair", 3, 33)
            out_proj("mla_out", lambda k: attn[:, k, :], T, DB, 4)

            def mlp(i, n, x, h):
                up = f"mlp{i}_up"
                with pe.Fori(0, 4) as it:
                    for j in range(8):
                        if j % 4 == 0:
                            w = group(up, it, j // 4, DB, 512)
                        claim(pe, up, it, j)
                        linear(unit(up, j), w, (j % 4) * P, x, n, DB).then_inc(acc_ready, 1)
                pe.wait_ge(relu_free, 32 * (i + 1) + 2)
                if i == 0:
                    pe.wait_ge(mod_ready, 2)
                    pe.wait_ge(e_ready, 1)
                down(f"mlp{i}_down", n, h, FFB, i, 2 - i)

            square_sum("y0", T)
            square_sum("h0m", T)
            pe.wait_ge(h_ready, 16)
            mlp(0, T, all_h, lambda k: hid[:, k, :])
            square_sum("y0m", T)

            square_sum("h1", T)
            pe.wait_ge(h_ready, 24)
            pe.wait_ge(gate1_in, 16 * 2)
            for d in range(2):
                claim(pe, "gla_gate", 0, d)
                linear(unit("gla_gate", d), gate1[:, :, d, :], 0, all_h, T, DB,
                       rows=GATE_RANK).then_inc(acc_ready, 1)
            emptied(pe, "gla_gate", 0, 1)
            S = "gla_head"
            with pe.Fori(0, GLA_H) as it:
                pe.wait_ge(gate2_in, it * 16 + 16)
                for d in range(2):
                    claim(pe, S, it, d)
                    for h in range(2):
                        last = pe.matmul(unit(S, d)[:, h, 0:HALF], gate2[:, d, :],
                                         hgate[0:GATE_RANK, d, h * HALF:(h + 1) * HALF], start=True, stop=True)
                    last.then_inc(acc_ready, 1)
                w = group(S, it, 0, DB, P)
                claim(pe, S, it, 2)
                linear(unit(S, 2), w, 0, seq_h, SEQ, DB).then_inc(acc_ready, 1)
                w = group(S, it, 1, DB, P)
                claim(pe, S, it, 3)
                linear(unit(S, 3), w, 0, all_h, T, DB).then_inc(acc_ready, 1)
                w = group(S, it, 2, DB, GLA_DV)
                for j in range(3):
                    claim(pe, S, it, 4 + j)
                    for i in range(2):
                        t = 2 * j + i
                        for k in range(DB):
                            last = mm(unit(S, 4 + j)[:, i, 0:GLA_DV], hT[:, k, t * P:(t + 1) * P], w[:, k, :],
                                      k == 0, k == DB - 1)
                    last.then_inc(acc_ready, 1)
                order = ([0, 1, 2, 3, 4], [1, 0, 5, 4, 3])
                for d in range(2):
                    pe.wait_ge(gk_ready, it * 2 + d + 1)
                    claim(pe, S, it, 7 + d)
                    for i, t in enumerate(order[d]):
                        last = pe.transpose(flat(unit(S, 7 + d))[:, i * P:(i + 1) * P],
                                            g_kE[:, d, t * P:(t + 1) * P], ident)
                    last.then_inc(acc_ready, 1)
                claim(pe, S, it, 9)
                for d in range(2):
                    u = unit(S, 9)[:, d, :]
                    for t in range(LT):
                        a, b = t * P, t * P + 64
                        pe.matmul(u[:, a:a + P], g_kt[:, d, a:a + P], g_qt[:, d, a:a + P], start=True, stop=True)
                        src, dst = (a, b) if d == 0 else (b, a)
                        last = pe.matmul(u[64 * d:64 * d + 64, dst:dst + 64], g_ke[:, d, CTX + src:CTX + src + 64],
                                         g_qt[:, d, dst:dst + 64], start=True, stop=True)
                last.then_inc(acc_ready, 1)
                for d in range(2):
                    emptied(pe, S, it, 7 + d)
                    if d == 0:
                        emptied(pe, S, it, 6)
                    for i, t in enumerate(order[d]):
                        if i in (0, 4):
                            claim(pe, S, it, 10 + 2 * d + i // 4)
                        u = unit(S, 10 + 2 * d + i // 4)
                        last = pe.matmul(u[:, (i % 4) // 2, (i % 2) * 256:(i % 2) * 256 + 256],
                                         g_kEt[:, d, i * P:(i + 1) * P], g_v[:, t, :], start=True, stop=True)
                        if i in (3, 4):
                            last.then_inc(acc_ready, 1)
                w = group(S, it, 3, DB, GLA_DV)
                for b in range(2):
                    for k in range(DB):
                        last = mm(sc[:, 0, b, :], w[:, k, b * P:(b + 1) * P], seq_h(k), k == 0, k == DB - 1)
                last.then_inc(gr_ready, 1)
                emptied(pe, S, it, 13)
                for b in range(2):
                    claim(pe, S, it, 14 + b)
                    for t in range(LT):
                        o = unit(S, 14 + b)[:, 0, t * P:(t + 1) * P]
                        v = slice(b * P, (b + 1) * P)
                        tok = slice(t * P, (t + 1) * P)
                        pe.matmul(o, g_v[:, 2 + t, v], g_AT[:, 0, tok], start=True, stop=False)
                        pe.matmul(o, g_v[:, 2 + t, v], g_AT[:, 1, tok], start=False, stop=False)
                        pe.matmul(o, g_S[:, 0, 1 + t, v], g_qS[:, 0, tok], start=False, stop=False)
                        last = pe.matmul(o, g_S[:, 1, 4 - t, v], g_qS[:, 1, tok], start=False, stop=True)
                    last.then_inc(acc_ready, 1)
                pe.wait_ge(gsq_ready, it * 1 + 1)
                for b in range(2):
                    last = pe.matmul(sc[:, 1, 0, :], ones, sq[:, b, 0:SEQ], start=b == 0, stop=b == 1)
                last.then_inc(gss_ready, 1)
            pe.wait_ge(g_done, GLA_H + 1)
            out_proj("gla_out", lambda k: g_out[:, k, :], SEQ, DB, 4)
            square_sum("y1", SEQ)
            square_sum("h1m", SEQ)
            pe.wait_ge(h_ready, 32)
            mlp(1, SEQ, seq_h, lambda k: hid[:, k, 0:SEQ])
            square_sum("y1m", SEQ)

            pe.wait_ge(h_ready, 40)
            pe.wait_ge(ab_in, 48)
            for j in range(2):
                claim(pe, "gdn_gate", 0, j)
                linear(unit("gdn_gate", j), w_ab, 8 * j, seq_h, SEQ, DB, rows=GDN_H).then_inc(acc_ready, 1)
            pe.wait_ge(tab_in, 48)
            pe.wait_ge(d_rows, 2)
            for r in range(2):
                for c in range(LT):
                    last = pe.transpose(sc[:, 1, 0, (r * LT + c) * 8:(r * LT + c) * 8 + 8],
                                        d_row[:, r, c * P:(c + 1) * P], ident[0:GDN_H, 0:GDN_H])
            last.then_inc(d_cols, 1)
            pe.wait_ge(d_gc, 1)
            pe.matmul(sc[:, 1, 1, 0:32], last_row, d_col[:, 1].rearrange("p c h -> p (c h)"), start=True,
                      stop=True).then_inc(d_cols, 1)
            S = "gdn_pair"
            tiles = [(e, c) for e in range(2) for c in range(LT)]
            with pe.Fori(0, GDN_H // 2) as it:
                for j in range(3):
                    w = group(S, it, j, DB, 256)
                    claim(pe, S, it, j)
                    for e in range(2):
                        for k in range(DB):
                            last = mm(unit(S, j)[:, e, :], w[:, k, e * P:(e + 1) * P], seq_h(k), k == 0, k == DB - 1)
                    last.then_inc(acc_ready, 1)
                w = group(S, it, 3, DB, 256)
                for e in range(2):
                    claim(pe, S, it, 3 + e)
                    linear(unit(S, 3 + e), w, e * P, seq_h, SEQ, DB).then_inc(acc_ready, 1)
                for r in range(2):
                    pe.wait_ge(d_masked, it * 2 + r + 1)
                    claim(pe, S, it, 5 + r)
                    for e in range(2):
                        last = pe.matmul(unit(S, 5 + r)[:, e, :], ones[0:GDN_H, :], sq[0:GDN_H, e, 0:SEQ],
                                         start=True, stop=True)
                    last.then_inc(acc_ready, 1)
                for r in range(2):
                    pe.wait_ge(d_sq, it * 3 + r + 1)
                    claim(pe, S, it, 7 + r)
                    for e in range(2):
                        last = pe.matmul(unit(S, 7 + r)[:, e, :], ones, sq[:, e, 0:SEQ], start=True, stop=True)
                    last.then_inc(acc_ready, 1)

                def products(j, left, right, wait=None):
                    claim(pe, S, it, j)
                    for e, c in tiles:
                        t = slice(c * P, (c + 1) * P)
                        last = pe.matmul(unit(S, j)[:, e, t], left[:, e, t], right[:, e, t], start=True, stop=True)
                    last.then_inc(acc_ready, 1)

                pe.wait_ge(d_norm, it * 2 + 2)
                products(9, d_k, d_k)
                products(10, d_k, d_q)
                for j, x in ((11, d_k), (12, d_v)):
                    if j == 12:
                        pe.wait_ge(d_silu, it * 3 + 3)
                    claim(pe, S, it, j)
                    for e, c in tiles:
                        t = slice(c * P, (c + 1) * P)
                        last = pe.transpose(unit(S, j)[:, e, t], x[:, e, t], ident)
                    last.then_inc(acc_ready, 1)
                pe.wait_ge(d_init, it * 1 + 1)
                for l in range(7):
                    j = 13 + 3 * l
                    pe.wait_ge(d_lm, it * 7 + l + 1)
                    if l:
                        emptied(pe, S, it, j - 2)
                    products(j, d_Lm[:, l % 2], d_T)
                    emptied(pe, S, it, j)
                    if l:
                        emptied(pe, S, it, j - 1)
                    if l < 6:
                        products(j + 1, d_U, d_Y)
                    products(j + 2 if l < 6 else j + 1, d_Y, d_U)
                emptied(pe, S, it, 32)
                pe.wait_ge(d_qe, it * 1 + 1)
                for c in range(LT):
                    t, j = slice(c * P, (c + 1) * P), 33 + 4 * c
                    if c:
                        emptied(pe, S, it, j - 1)
                    claim(pe, S, it, j)
                    for e in range(2):
                        last = pe.matmul(unit(S, j)[:, e, 0:P], d_k[:, e, t], d_S[:, e, :], start=True, stop=True)
                    last.then_inc(acc_ready, 1)
                    pe.wait_ge(d_rr, it * LT + c + 1)
                    claim(pe, S, it, j + 1)
                    for e in range(2):
                        last = pe.matmul(unit(S, j + 1)[:, e, 0:P], d_U[:, e, t], d_r[:, e, :], start=True, stop=True)
                    last.then_inc(acc_ready, 1)
                    claim(pe, S, it, j + 2)
                    for e in range(2):
                        pe.matmul(unit(S, j + 2)[:, e, 0:P], d_S[:, e, :], d_qE[:, e, t], start=True, stop=False)
                        if e == 0:
                            emptied(pe, S, it, j + 1)
                        last = pe.matmul(unit(S, j + 2)[:, e, 0:P], d_vn[:, e, :], d_QK[:, e, t], start=False, stop=True)
                    last.then_inc(acc_ready, 1)
                    claim(pe, S, it, j + 3)
                    for e in range(2):
                        last = pe.matmul(unit(S, j + 3)[:, e, 0:P], d_kend[:, e, t], d_vn[:, e, :], start=True, stop=True)
                    last.then_inc(acc_ready, 1)
                pe.wait_ge(d_sq, it * 3 + 3)
                claim(pe, S, it, 49)
                for e in range(2):
                    last = pe.matmul(unit(S, 49)[:, e, :], ones, sq[:, e, 0:SEQ], start=True, stop=True)
                last.then_inc(acc_ready, 1)
            pe.wait_ge(d_done, GDN_H // 2 + 1)
            out_proj("gdn_out", lambda k: d_out[:, k, :], SEQ, DB, 4)

            def ffn(i):
                up = f"ffn{i}_up"
                with pe.Fori(0, HIDB // 2) as it:
                    for j in range(2):
                        w = group(up, it, j, DB, 256)
                        claim(pe, up, it, j)
                        for b in range(2):
                            for k in range(DB):
                                last = mm(unit(up, j)[:, b, :], w[:, k, b * P:(b + 1) * P], seq_h(k), k == 0, k == DB - 1)
                        last.then_inc(acc_ready, 1)
                emptied(pe, up, HIDB // 2 - 1, 1)
                down(f"ffn{i}_down", SEQ, lambda k: hid2[:, k, :], HIDB, 2 if i == 0 else None)

            mean_sum("gdn_out")
            square_sum("ln0", SEQ)
            pe.wait_ge(h_ready, 48)
            ffn(0)
            mean_sum("ffn0_down")
            square_sum("ln0f", SEQ)

            pe.wait_ge(h_ready, 56)
            S = "ret_head"
            with pe.Fori(0, RET_H) as it:
                for j in range(2):
                    w = group(S, it, j, DB, 256)
                    claim(pe, S, it, j)
                    for b in range(2):
                        for k in range(DB):
                            last = mm(unit(S, j)[:, b, :], w[:, k, b * P:(b + 1) * P], seq_h(k), k == 0, k == DB - 1)
                    last.then_inc(acc_ready, 1)
                w = group(S, it, 2, DB, 512)
                for j in range(2):
                    claim(pe, S, it, 2 + j)
                    for i in range(2):
                        t = CTX + (2 * j + i) * P
                        for k in range(DB):
                            last = mm(unit(S, 2 + j)[:, i, :], hT[:, k, t:t + P], w[:, k, :], k == 0, k == DB - 1)
                    last.then_inc(acc_ready, 1)
                w = group(S, it, 3, DB, 512)
                for j in range(2):
                    claim(pe, S, it, 4 + j)
                    for i in range(2):
                        for k in range(DB):
                            m = (2 * j + i) * P
                            last = mm(unit(S, 4 + j)[:, i, :], w[:, k, m:m + P], seq_h(k), k == 0, k == DB - 1)
                    last.then_inc(acc_ready, 1)
                pe.wait_ge(r_rotd, it * 2 + 2)
                for j in range(2):
                    claim(pe, S, it, 6 + j)
                    for i in range(2):
                        t = (2 * j + i) * P
                        for b in range(2):
                            last = pe.matmul(unit(S, 6 + j)[:, i, 0:SEQ - t], r_rot[:, 1, b, t:t + P],
                                             r_rot[:, 0, b, t:SEQ], start=b == 0, stop=b == 1)
                    last.then_inc(acc_ready, 1)
                emptied(pe, S, it, 6)
                emptied(pe, S, it, 7)
                for j in range(2):
                    claim(pe, S, it, 8 + j)
                    for i in range(2):
                        m = (2 * j + i) * P
                        for t in range(LT):
                            last = pe.matmul(unit(S, 8 + j)[:, i, t * P:SEQ], r_v[:, t, m:m + P],
                                             r_s[:, t, 0:SEQ - t * P], start=t == 0, stop=t == LT - 1)
                    last.then_inc(acc_ready, 1)
                emptied(pe, S, it, 8)
                emptied(pe, S, it, 9)
                claim(pe, S, it, 10)
                for b in range(4):
                    last = pe.matmul(unit(S, 10)[:, 0, :], ones, r_o[:, b, :], start=b == 0, stop=b == 3)
                last.then_inc(acc_ready, 1)
                claim(pe, S, it, 11)
                for b in range(4):
                    pe.wait_ge(r_sq, it * 4 + b + 1)
                    last = pe.matmul(unit(S, 11)[:, 0, :], ones, r_sqr[:, b, :], start=b == 0, stop=b == 3)
                last.then_inc(acc_ready, 1)
            pe.wait_ge(r_done, RET_H + 1)
            out_proj("ret_out", lambda k: r_out[:, k, :], SEQ, 16, 2)
            mean_sum("ret_out")
            square_sum("ln1", SEQ)
            pe.wait_ge(h_ready, 64)
            ffn(1)
            mean_sum("ffn1_down")
            square_sum("ln1f", SEQ)
            pe.wait_ge(x_ready, 64)
            for t in range(LT):
                if t >= 2:
                    pe.wait_ge(o_moved, t - 1)
                for b in range(DB):
                    last = pe.transpose(flat(sc[:, t % 2])[:, b * P:(b + 1) * P],
                                        xT[:, b, CTX + t * P:CTX + (t + 1) * P], ident)
                last.then_inc(o_turned, 1)

        @block.scalar
        def _(act):
            st = Steps(act, act_step)
            f = act.activation

            def squares(name, src, n, ready=None):
                _, b0, nb = NORMS[name]
                for b in range(nb):
                    if ready is not None:
                        ready(b)
                    if b0 + b >= 2:
                        act.wait_ge(n_used, b0 + b - 1)
                    f(sq[:, (b0 + b) % 2, 0:n], src(b), ACT.Square).then_inc(n_sq, 1)

            def deviation(name, n, width, e=0):
                k, b0, nb = NORMS[name]
                act.wait_ge(n_used, b0 + nb)
                i, o = (sc[:, 0, :, 0:HALF], halves(rstd)) if n == T else (sc[:, 0, 0, 0:n], rstd[:, 0:n])
                f(o, i, ACT.Sqrt, scale=1.0 / width, bias=eps[:, e:e + 1]).then_inc(n_std, 1)

            def affine(l, q, n, mul0):
                for b in range(DB):
                    act.wait_ge(n_mul, mul0 + b + 1)
                    if n == T:
                        f(hT[:, b, 0:CTX], hT[:, b, 0:CTX], ACT.Identity, scale=dcol[:, l, q, b, 1:2],
                          bias=mod[:, l, 24 * (q // 2) + b, 1:2])
                    f(hT[:, b, CTX:T], hT[:, b, CTX:T], ACT.Identity, scale=dcol[:, l, q, b, 0:1],
                      bias=mod[:, l, 24 * (q // 2) + b, 0:1]).then_inc(h_ready, 1)

            def modulate(l, q, x0):
                for b in range(DB):
                    act.wait_ge(x_ready, x0 + b + 1)
                    f(hT[:, b, CTX:T], xT[:, b, CTX:T], ACT.Identity, scale=dcol[:, l, q, b, 0:1],
                      bias=mod[:, l, 24 * (q // 2) + b, 0:1]).then_inc(h_ready, 1)

            def layer_norm_out(l, i, mul0):
                for b in range(DB):
                    act.wait_ge(n_mul, mul0 + b + 1)
                    f(xT[:, b, CTX:T], xT[:, b, CTX:T], ACT.Identity, scale=col("ln_g_2", (2 * l + i) * DB + b),
                      bias=col("ln_b_2", (2 * l + i) * DB + b)).then_inc(x_ready, 1)

            def x_at(b0, seq=False):
                return lambda b: act.wait_ge(x_ready, b0 + b + 1)

            def y_at(stage):
                return lambda b: emptied(act, stage, *divmod(b, UNITS[stage]))

            def const(dst, src, s):
                act.dma_start(dst, src).then_inc(s, 16)

            const(base_tab[:, :], A["tab_base"], const_in)
            for name, src in vec_sources:
                t, r, rows = VEC[name]
                const(vrow[r:r + rows, t, :], src, const_in)
            const(x_tok[:, 0:2, :], A["ctx"][0].rearrange("(t p) d -> p t d", p=P), x_in)
            const(x_tok[:, 2:QT, :], A["x"][0].rearrange("(t p) d -> p t d", p=P), x_in)
            const(tab[:, 0:1408], A["tab_mla"], tab_in)
            for d in range(2):
                const(gate1[:, :, d, :], A["gla_w_gate1"][0, d].rearrange("(k p) r -> p k r", p=P), gate1_in)
            const(w_ab[:, :, :], A["gdn_w_in_2"][:, 4 * D:4 * D + 16].rearrange("(k p) n -> p k n", p=P), ab_in)
            const(a_dt[:, 0:1], A["gdn_a_log_2"].rearrange("(h a) -> h a", a=1), ab_in)
            const(a_dt[:, 1:2], A["gdn_dt_bias_2"].rearrange("(h a) -> h a", a=1), ab_in)
            act.wait_ge(cols_ready, 1)
            f(cs[:, :, 0], vec("c", 0, DB), ACT.Silu)
            f(cs[:, :, 1], vec("c_ctx", 0, DB), ACT.Silu).then_inc(c_ready, 1)
            for b in range(DB):
                act.wait_ge(x_turned, b + 1)
                f(xT[:, b, :], flat(sc[:, b % 2])[:, 0:T], ACT.Copy).then_inc(x_moved, 1)
            act.wait_ge(relu_free, 2)
            act.wait_ge(x_moved, DB)
            squares("h0", lambda b: xT[:, b, :], T)
            deviation("h0", T, D)
            act.wait_ge(mod_ready, 1)
            affine(0, 0, T, 0)
            squares("cq", lambda b: cq[:, b, :], T, lambda b: emptied(act, "mla_in", 0, b))
            deviation("cq", T, Q_RANK)
            squares("ckv", lambda b: ckv[:, b, :], T, lambda b: emptied(act, "mla_in", 0, 3 + b))
            act.wait_ge(lat_ready, 3)
            deviation("ckv", T, KV_RANK)
            scale = (NOPE + ROPE) ** -0.5
            with act.Fori(0, MLA_H // 2) as it:
                for n in range(2 * QT):
                    act.wait_ge(p_max, it * 12 + n + 1)
                    if n % QT < 2:
                        i, o = sc[:, n % 2, 0, 0:CTX], prob[:, n % 2, 0:CTX]
                    else:
                        i, o = sc[:, n % 2, :, 0:HALF], halves(prob[:, n % 2, :])
                    f(o, i, ACT.Exp, bias=small[:, n % 2, 1:2], scale=scale,
                      accum_out=small[:, n % 2, 2:3]).then_inc(p_exp, 1)

            def mlp(i, n):
                up = f"mlp{i}_up"
                with act.Fori(0, 4) as it:
                    for j in range(8):
                        finished(act, up, it, j)
                        act.wait_ge(relu_free, it * 8 + (32 * i + j + 1))
                        u = unit(up, j)
                        if n == T:
                            ins = f(halves(relu[:, j % 2, :]), u[:, :, 0:HALF], ACT.Relu)
                        else:
                            ins = f(relu[:, j % 2, 0:n], u[:, 0, 0:n], ACT.Relu)
                        free(ins, up, j)

            emptied(act, "mla_pair", MLA_H // 2 - 1, 33)
            for k in range(DB):
                last = f(cs[:, k, 2:3], cs[:, k, 2:3], ACT.Silu, bias=col("cond_b", k))
            last.then_inc(e_ready, 1)
            y_all = lambda b: hT[:, b, :]
            y_seq = lambda b: hT[:, b, CTX:T]
            x_all = lambda b: xT[:, b, :]
            x_seq = lambda b: xT[:, b, CTX:T]
            squares("y0", y_all, T, y_at("mla_out"))
            deviation("y0", T, D)
            squares("h0m", x_all, T, x_at(0))
            deviation("h0m", T, D)
            act.wait_ge(mod_ready, 2)
            affine(0, 2, T, 8)
            mlp(0, T)
            squares("y0m", y_all, T, y_at("mlp0_down"))
            act.wait_ge(mod_summed, 2 + MOD_CHUNKS)
            deviation("y0m", T, D)
            const(tab[:, 0:1024], A["tab_gla"], tab_in)

            squares("h1", x_all, T, x_at(8))
            deviation("h1", T, D)
            act.wait_ge(mod_ready, 3)
            affine(1, 0, T, 16)
            S = "gla_head"
            with act.Fori(0, GLA_H) as it:
                st.enter(it, 4)
                for d in range(2):
                    emptied(act, S, it, d)
                    st.did(f(g_l, g_z[:, d, :], ACT.Abs))
                    st.settle()
                    st.did(f(g_l, g_l, ACT.Exp, scale=-1.0))
                    st.settle()
                    f(g_l, g_l, ACT.Ln, bias=1.0).then_inc(gl_ready, 1)
                    finished(act, S, it, 2 + d)
                    if d == 0:
                        free(f(g_q, unit(S, 2)[:, 0, :], ACT.Copy, scale=P ** -0.5), S, 2)
                    else:
                        free(f(halves(g_k), unit(S, 3)[:, :, 0:HALF], ACT.Copy), S, 3)
                    act.wait_ge(gG_ready, it * 2 + d + 1)
                    f(g_qt[:, d, :], g_G[:, CTX:T], ACT.Exp, scale=1 / 16)
                    f(g_kt[:, d, :], g_G[:, CTX:T], ACT.Exp, scale=-1 / 16)
                    f(g_ke[:, d, :], g_z[:, d, :], ACT.Exp, scale=1 / 16)
                    f(g_et[:, d, :], g_tot[:, d, :], ACT.Exp, scale=1 / 16).then_inc(gE_ready, 1)
                for d in range(2):
                    finished(act, S, it, 7 + d)
                    free(f(g_kEt[:, d, :], flat(unit(S, 7 + d))[:, 0:5 * P], ACT.Copy), S, 7 + d)
                act.wait_ge(g_done, it * 1 + 1)
                act.wait_ge(gr_ready, it * 1 + 1)
                f(g_r, sc[:, 0], ACT.Silu)
                emptied(act, S, it, 14)
                emptied(act, S, it, 15)
                f(sq[:, :, 0:SEQ], g_o, ACT.Square).then_inc(gsq_ready, 1)
                act.wait_ge(gss_ready, it * 1 + 1)
                f(rstd[:, 0:SEQ], sc[:, 1, 0, :], ACT.Sqrt, scale=1.0 / GLA_DV, bias=eps[:, 0:1]).then_inc(gdev_ready, 1)
            st.leave(GLA_H)
            squares("y1", y_seq, SEQ, y_at("gla_out"))
            deviation("y1", SEQ, D)
            squares("h1m", x_seq, SEQ, x_at(16))
            deviation("h1m", SEQ, D)
            affine(1, 2, SEQ, 24)
            mlp(1, SEQ)
            squares("y1m", y_seq, SEQ, y_at("mlp1_down"))
            act.wait_ge(mod_summed, 2 + 2 * MOD_CHUNKS)
            deviation("y1m", SEQ, D)
            const(tab[:, 0:1664], A["tab_gdn"], tab_in)

            act.wait_ge(mod_ready, 4)
            modulate(2, 0, 24)
            act.wait_ge(ab_in, 48)
            f(a_dt[:, 2:3], a_dt[:, 0:1], ACT.Exp).then_inc(d_ga, 1)
            finished(act, "gdn_gate", 0, 1)
            free(f(d_row[:, 0, :], unit("gdn_gate", 1)[0:GDN_H, 0, :], ACT.Sigmoid), "gdn_gate", 1)
            emptied(act, "gdn_gate", 0, 0)
            st.did(f(sq[0:GDN_H, 0, 0:SEQ], rstd[0:GDN_H, 0:SEQ], ACT.Abs))
            st.settle()
            st.did(f(sq[0:GDN_H, 0, 0:SEQ], sq[0:GDN_H, 0, 0:SEQ], ACT.Exp, scale=-1.0))
            st.settle()
            f(sq[0:GDN_H, 0, 0:SEQ], sq[0:GDN_H, 0, 0:SEQ], ACT.Ln, bias=1.0).then_inc(d_ga, 1)
            act.wait_ge(d_glr, 1)
            f(d_col[:, 2], d_col[:, 1], ACT.Exp)
            f(d_col[:, 4], d_col[:, 4], ACT.Exp)
            f(d_col[:, 3], d_col[:, 3], ACT.Exp).then_inc(d_ga, 1)
            S = "gdn_pair"
            with act.Fori(0, GDN_H // 2) as it:
                for j in range(3):
                    finished(act, S, it, j)
                    act.wait_ge(d_conv, it * 3 + max(2, j + 1))
                    free(f(d_cp[:, j % 2, :, 3:SEQ + 3], unit(S, j), ACT.Copy), S, j)
                act.wait_ge(d_done, it * 1 + 1)
                for e in range(2):
                    finished(act, S, it, 3 + e)
                    free(f(d_z[:, e, :], unit(S, 3 + e)[:, 0, :], ACT.Silu), S, 3 + e)
                for j, x in enumerate((d_q, d_k, d_v)):
                    act.wait_ge(d_conv, it * 3 + j + 3)
                    f(x, x, ACT.Silu).then_inc(d_silu, 1)
                for r, x in enumerate((d_gcR, d_bR)):
                    finished(act, S, it, 5 + r)
                    free(f(x, unit(S, 5 + r), ACT.Copy), S, 5 + r)
                for r, (x, y) in enumerate(((d_q, d_Y), (d_k, d_U))):
                    act.wait_ge(d_silu, it * 3 + r + 1)
                    if r:
                        finished(act, S, it, 7)
                    f(sq[:, :, 0:SEQ], x, ACT.Square).then_inc(d_sq, 1)
                    finished(act, S, it, 7 + r)
                    free(f(y, unit(S, 7 + r), ACT.Sqrt, bias=eps[:, 0:1]), S, 7 + r)
                act.wait_ge(d_diff, it * 1 + 1)
                f(d_ET, d_ET, ACT.Exp).then_inc(d_exp, 1)
                finished(act, S, it, 12)
                f(d_v, d_gcR, ACT.Exp).then_inc(d_exp, 1)
                for l in range(7):
                    finished(act, S, it, 13 + 3 * l)
                    free(f(d_Y, unit(S, 13 + 3 * l), ACT.Copy), S, 13 + 3 * l)
                for c in range(LT):
                    t, j = slice(c * P, (c + 1) * P), 33 + 4 * c
                    finished(act, S, it, j + 1)
                    free(f(d_vn, unit(S, j + 1)[:, :, 0:P], ACT.Copy), S, j + 1)
                    finished(act, S, it, j + 2)
                    free(f(d_o[:, :, t], unit(S, j + 2)[:, :, 0:P], ACT.Copy), S, j + 2)
                emptied(act, S, it, 47)
                f(sq[:, :, 0:SEQ], d_o, ACT.Square).then_inc(d_sq, 1)
                finished(act, S, it, 49)
                free(f(d_Y, unit(S, 49), ACT.Sqrt, scale=1.0 / P, bias=eps[:, 0:1]), S, 49)

            def layer_norm(stage, name, l, i, x0, mul0):
                squares(name, x_seq, SEQ, lambda b: act.wait_ge(n_cent, x0 - 32 + b + 1))
                deviation(name, SEQ, D, 1)
                layer_norm_out(l, i, mul0)

            def ffn(i):
                up = f"ffn{i}_up"
                with act.Fori(0, HIDB // 2) as it:
                    finished(act, up, it, 0)
                    act.wait_ge(f_conv, it * 1 + (HIDB // 2 * i + i + 1))
                    free(f(gpad[:, :, 2:SEQ + 2], unit(up, 0), ACT.Copy), up, 0)
                    act.wait_ge(f_conv, it * 1 + (HIDB // 2 * i + i + 2))
                    f(gsilu, gconv, ACT.Silu).then_inc(f_silu, 1)

            layer_norm("gdn_out", "ln0", 0, 0, 32, 32)
            modulate(2, 2, 32)
            ffn(0)
            layer_norm("ffn0_down", "ln0f", 0, 1, 40, 40)

            const(r_tab[:, :, :], A["tab_ret"].rearrange("p (a n) -> p a n", a=6), rtab_in)
            act.wait_ge(mod_ready, 5)
            modulate(3, 0, 40)
            S = "ret_head"
            with act.Fori(0, RET_H) as it:
                finished(act, S, it, 0)
                free(f(r_raw[:, 0], unit(S, 0), ACT.Copy), S, 0)
                finished(act, S, it, 1)
                free(f(r_raw[:, 1], unit(S, 1), ACT.Copy, scale=1 / 16), S, 1)
                act.wait_ge(r_done, it * 1 + 1)
                for j in range(2):
                    finished(act, S, it, 4 + j)
                    free(f(r_gate[:, 2 * j:2 * j + 2, :], unit(S, 4 + j), ACT.Silu), S, 4 + j)
                for b in range(4):
                    if b < 3:
                        act.wait_ge(r_cent, it * 3 + b + 1)
                    else:
                        emptied(act, S, it, 10)
                    f(r_sqr[:, b, :], r_o[:, b, :], ACT.Square).then_inc(r_sq, 1)
                finished(act, S, it, 11)
                free(f(rstd[:, 0:SEQ], unit(S, 11)[:, 0, :], ACT.Sqrt, scale=1.0 / RET_DV, bias=eps[:, 0:1]), S, 11)
            layer_norm("ret_out", "ln1", 1, 0, 48, 48)
            modulate(3, 2, 48)
            ffn(1)
            layer_norm("ffn1_down", "ln1f", 1, 1, 56, 56)

        @block.vector
        def _(dve):
            st = Steps(dve, dve_step)
            tt, ts, stt, cp = dve.tensor_tensor, dve.tensor_scalar, dve.scalar_tensor_tensor, dve.tensor_copy
            MUL, ADD, SUB, MIN, MAX = ALU.mult, ALU.add, ALU.subtract, ALU.min, ALU.max

            def reciprocal_of(name, n):
                k, _, _ = NORMS[name]
                dve.wait_ge(n_std, k + 1)
                st.did(dve.reciprocal(rstd[:, 0:n], rstd[:, 0:n]))
                st.settle()

            def normed(name, n):
                reciprocal_of(name, n)
                for b in range(DB):
                    tt(hT[:, b, T - n:T], xT[:, b, T - n:T], rstd[:, 0:n], MUL).then_inc(n_mul, 1)

            def residual(name, n, l, q):
                reciprocal_of(name, n)
                for b in range(DB):
                    st.did(tt(hT[:, b, T - n:T], hT[:, b, T - n:T], rstd[:, 0:n], MUL))
                st.settle()
                for b in range(DB):
                    if n == T:
                        stt(xT[:, b, 0:CTX], hT[:, b, 0:CTX], dcol[:, l, q, b, 1:2], xT[:, b, 0:CTX], MUL, ADD)
                    stt(xT[:, b, CTX:T], hT[:, b, CTX:T], dcol[:, l, q, b, 0:1], xT[:, b, CTX:T],
                        MUL, ADD).then_inc(x_ready, 1)

            dve.memset(eps[:, 0:1], 1e-6).then_inc(relu_free, 1)
            dve.memset(eps[:, 1:2], 1e-5 / ALPHA ** 2).then_inc(relu_free, 1)
            dve.wait_ge(vec_turned, 1)
            for t in range(VEC_TILES):
                n = vec_rows[t]
                last = cp(cols[:, t, 0:n], flat(acc[:, 0])[:, t * P:t * P + n])
            last.then_inc(cols_ready, 1)
            dve.wait_ge(cols_ready, 1)

            def modulation(l, i0, i1, nv, src=None):
                if src is None:
                    src = mod_psum[:, MOD_AT:MOD_AT + 48 * nv].rearrange("p (i v) -> p i v", v=nv)
                o = src[:, i0 * DB:i1 * DB]
                for v in range(nv):
                    b = vec("ada_b" if l < 2 else "ada_b_2", 48 * (l % 2) + i0 * DB, (i1 - i0) * DB)
                    st.did(tt(mod[:, l, i0 * DB:i1 * DB, v], o[:, :, v], b, ADD))
                st.settle()
                for q, (m, plus) in enumerate(((1, 1.0), (2, 0.0), (4, 1.0), (5, 0.0))):
                    if not i0 <= m < i1:
                        continue
                    for v in range(nv):
                        src = mod[:, l, m * DB:(m + 1) * DB, v]
                        if l < 2:
                            last = stt(dcol[:, l, q, :, v], src, plus, vec("norm_g", (4 * l + q) * DB, DB), ADD, MUL)
                        else:
                            last = ts(dcol[:, l, q, :, v], src, 1.0, 1.0 if plus else 1.0 / ALPHA, ADD, MUL)
                last.then_inc(mod_ready, 1)

            def mod_chunk(phase, it, i, vs):
                dve.wait_ge(mod_summed, MOD_CHUNKS * phase + i + 1 + it * MOD_IT)
                for q in range(MOD_Q):
                    s = mod_slot(i, q)
                    dve.wait_ge(mod_loaded[s], piece(phase, it, i, 16))
                    for kk in range(MOD_K):
                        for j, v in enumerate(vs):
                            k = MOD_K * q + kk
                            a, w = mod_acc[:, i % 2, j, :], mod_w[s][:, kk, :]
                            if k == 0:
                                ins = ts(a, w, cs[:, k, v:v + 1], None, MUL)
                            else:
                                ins = stt(a, w, cs[:, k, v:v + 1], a, MUL, ADD)
                        if kk == MOD_K - 1:
                            ins.then_inc(mod_used[s], 1)
                            dve.wait_ge(mod_used[s], piece(phase, it, i) + 1)
                        else:
                            st.did(ins)
                            st.settle()

            normed("h0", T)
            dve.memset(krope[:, :, :], 0.0).then_inc(krope_ready, 1)
            dve.wait_ge(krope_ready, 1)
            dve.wait_ge(ada_done, 1)
            modulation(0, 0, 2, 2)
            for j in range(5):
                finished(dve, "mla_in", 0, j)
                free(cp(halves(cq[:, j, :] if j < 3 else ckv[:, j - 3, :]), unit("mla_in", j)[:, :, 0:HALF]), "mla_in", j)
            finished(dve, "mla_in", 0, 5)
            free(cp(halves(kraw[0:64]), unit("mla_in", 5)[0:64, :, 0:HALF]), "mla_in", 5)
            finished(dve, "mla_rope", 0, 0)
            free(cp(halves(qraw), unit("mla_rope", 0)[:, :, 0:HALF]), "mla_rope", 0)
            finished(dve, "mla_rope", 0, 1)
            free(tt(ktmp, unit("mla_rope", 1)[:, 0, :], rsin, MUL), "mla_rope", 1)
            emptied(dve, "mla_rope", 0, 0)
            emptied(dve, "mla_rope", 0, 1)
            st.did(tt(qr[:, CTX:T], qraw[:, CTX:T], rcos, MUL))
            st.settle()
            for e in range(2):
                h = slice(64 * e, 64 * e + 64)
                cp(krope[h, e, 0:CTX], qraw[h, 0:CTX])
                last = tt(krope[h, e, CTX:T], qr[h, CTX:T], ktmp[h, :], ADD)
            last.then_inc(krope_ready, 1)
            for name, x, nb, g in (("cq", cq, 3, "mla_g_q"), ("ckv", ckv, 2, "mla_g_kv")):
                reciprocal_of(name, T)
                for b in range(nb):
                    stt(x[:, b, :], x[:, b, :], col(g, b), rstd[:, :], MUL, MUL).then_inc(lat_ready, 1)
            S = "mla_pair"
            scale = (NOPE + ROPE) ** -0.5
            with dve.Fori(0, MLA_H // 2) as it:
                st.enter(it, 1 + 12 * 2)
                for j, o in ((0, qn[:, 0]), (1, qn[:, 1]), (2, qraw), (3, kn[:, 0]), (4, kn[:, 1])):
                    finished(dve, S, it, j)
                    free(cp(halves(o), unit(S, j)[:, :, 0:HALF]), S, j)
                for j in range(3):
                    finished(dve, S, it, 5 + j)
                    free(cp(vtok[:, 2 * j:2 * j + 2, :], unit(S, 5 + j)[:, :, 0:256]), S, 5 + j)
                emptied(dve, S, it, 2)
                cp(qr[:, 0:CTX], qraw[:, 0:CTX])
                st.did(tt(qr[:, CTX:T], qraw[:, CTX:T], rcos, MUL))
                for j in range(2):
                    finished(dve, S, it, 8 + j)
                    free(tt(ktmp[:, 256 * j:256 * j + 256], unit(S, 8 + j)[:, 0, 0:256],
                            rsin[:, 256 * j:256 * j + 256], MUL), S, 8 + j)
                emptied(dve, S, it, 8)
                emptied(dve, S, it, 9)
                st.settle()
                tt(qr[:, CTX:T], qr[:, CTX:T], ktmp, ADD).then_inc(qrope_ready, 1)
                for n in range(2 * QT + 1):
                    e, t, s = n // QT, n % QT, n % 2
                    if n < 2 * QT:
                        dve.wait_ge(s_ready, it * 12 + n + 1)
                        i = sc[:, s, 0:1, 0:CTX] if t < 2 else sc[:, s, :, 0:HALF]
                        st.did(dve.tensor_reduce(small[:, s, 0:1], i, XY, MAX))
                        st.settle()
                        ts(small[:, s, 1:2], small[:, s, 0:1], -scale, None, MUL).then_inc(p_max, 1)
                    if n:
                        nk = 2 if (n - 1) % QT < 2 else KT
                        u = 10 + 2 * (n - 1)
                        finished(dve, S, it, u)
                        free(cp(probT[:, (n - 1) % 2, 0:nk * P], flat(unit(S, u))[:, 0:nk * P]), S, u)
                    if n < 2 * QT:
                        w = CTX if t < 2 else T
                        dve.wait_ge(p_exp, it * 12 + n + 1)
                        st.did(dve.reciprocal(small[:, s, 3:4], small[:, s, 2:3]))
                        st.settle()
                        ts(prob[:, s, 0:w], prob[:, s, 0:w], small[:, s, 3:4], None, MUL).then_inc(p_ready, 1)
                    if n:
                        m, u = n - 1, 11 + 2 * (n - 1)
                        finished(dve, S, it, u)
                        if m < 8:
                            cp(mod[:, 0, bass.ds(it * 8 + (2 * DB + m), 1), :], unit(S, u)[:, 1:2, 0:2])
                        elif m < 10:
                            cp(cs[:, bass.ds(it * 2 + (m - 8), 1), 2:3], unit(S, u)[:, 1:2, 0:1])
                        free(cp(attn[:, bass.ds(it * 2 + m // QT, 1), (m % QT) * P:(m % QT) * P + P],
                                unit(S, u)[:, 0:1, 0:P]), S, u)
            st.leave(MLA_H // 2)
            emptied(dve, S, MLA_H // 2 - 1, 33)
            modulation(0, 2, 6, 2, mod[:, 0])
            dve.wait_ge(mod_ready, 2)
            for s in range(MOD_SLOTS):
                dve.memset(mod_w[s % 3][:, s // 3, 0:1], 0.0).then_inc(mod_used[s], 1)
            for s in range(2):
                dve.memset(mod_acc[:, s, 0, 0:1], 0.0).then_inc(mod_summed, 1)

            def out_y(stage, n):
                for j in range(8):
                    finished(dve, stage, 0, j)
                    if n == T:
                        ins = cp(halves(hT[:, j, :]), unit(stage, j)[:, :, 0:HALF])
                    else:
                        ins = cp(hT[:, j, CTX:T], unit(stage, j)[:, 0, :])
                    free(ins, stage, j)

            def mlp(i, n):
                up, down = f"mlp{i}_up", f"mlp{i}_down"
                with dve.Fori(0, 4) as it:
                    for j in range(8):
                        emptied(dve, up, it, j)
                        r = relu[:, j % 2:j % 2 + 1, 0:n]
                        tt(hid[:, bass.ds(it * 8 + j, 1), 0:n], r, r, MUL).then_inc(relu_free, 1)
                dve.wait_ge(e_ready, 1)
                with dve.Fori(0, 4) as it:
                    st.enter(it, MOD_IT * MOD_Q * (MOD_K - 1))
                    for j in range(2):
                        for c in range(j * MOD_UNIT, (j + 1) * MOD_UNIT):
                            mod_chunk(i, it, c, ((0, 1), (2,))[i])
                        finished(dve, down, it, j)
                        if n == T:
                            ins = cp(hT[:, bass.ds(it * 2 + j, 1), :].rearrange("p a (h n) -> p (a h) n", h=2),
                                     unit(down, j)[:, :, 0:HALF])
                        else:
                            ins = cp(hT[:, bass.ds(it * 2 + j, 1), CTX:T], unit(down, j)[:, 0:1, :])
                        free(ins, down, j)
                st.leave(4)
                dve.wait_ge(mod_summed, 2 + MOD_CHUNKS * (i + 1))
                modulation(i + 1, 0, 6, 2 - i)
                dve.wait_ge(mod_ready, 3 + i)

            out_y("mla_out", T)
            residual("y0", T, 0, 1)
            normed("h0m", T)
            mlp(0, T)
            residual("y0m", T, 0, 3)

            normed("h1", T)
            for d in range(2):
                finished(dve, "gla_gate", 0, d)
                free(cp(halves(hgate[0:GATE_RANK, d, :]), unit("gla_gate", d)[0:GATE_RANK, :, 0:HALF]), "gla_gate", d)
            dve.memset(g_AT[:, :, :], 0.0).then_inc(g_done, 1)
            dve.wait_ge(g_done, 1)
            dve.wait_ge(tab_in, 32)
            S = "gla_head"
            c64 = lambda a: a.rearrange("p (c n) -> p c n", n=64)
            with dve.Fori(0, GLA_H) as it:
                st.enter(it, 19)
                dve.wait_ge(g_done, it * 1 + 1)
                for d in range(2):
                    finished(dve, S, it, d)
                    free(ts(halves(g_z[:, d, :]), unit(S, d)[:, :, 0:HALF], dyncol("gla_b_gate", it * 1 + 4 * d), None, ADD), S, d)
                for d in range(2):
                    emptied(dve, S, it, d)
                    dve.wait_ge(gl_ready, it * 2 + d + 1)
                    st.did(stt(g_g, g_z[:, d, :], 0.0, g_l, MIN, SUB))
                    st.settle()
                    if d == 1:
                        dve.wait_ge(gE_ready, it * 2 + 1)
                    st.did(dve.tensor_tensor_scan(g_G, keep64, g_g, 0.0, MUL, ADD))
                    st.settle()
                    st.did(cp(g_tot[:, d, :], c64(g_G)[:, :, 63]))
                    if d == 1:
                        st.did(tt(g_g, g_G, g_g, SUB))
                        st.settle()
                        st.did(tt(c64(g_G), g_tot[:, 1, :].unsqueeze(2).to_broadcast([P, 12, 64]), c64(g_g), SUB))
                    st.settle()
                    tt(c64(g_z[:, d, :]), g_tot[:, d, :].unsqueeze(2).to_broadcast([P, 12, 64]), c64(g_G), SUB).then_inc(gG_ready, 1)

                def values(j):
                    finished(dve, S, it, 4 + j)
                    free(cp(g_v[:, 2 * j:2 * j + 2, :], unit(S, 4 + j)[:, :, 0:GLA_DV]), S, 4 + j)

                for d in range(2):
                    dve.wait_ge(gE_ready, it * 2 + d + 1)
                    emptied(dve, S, it, 2)
                    emptied(dve, S, it, 3)
                    tt(g_qt[:, d, :], g_qt[:, d, :], g_q, MUL)
                    tt(g_kt[:, d, :], g_kt[:, d, :], g_k[:, CTX:T], MUL)
                    st.did(tt(g_ke[:, d, :], g_ke[:, d, :], g_k, MUL))
                    st.settle()
                    q4, s4 = (x[:, d, :].rearrange("p (t a n) -> p t a n", a=2, n=64) for x in (g_qt, g_qS))
                    e4, k4 = (x[:, d, :].rearrange("p (t a n) -> p t a n", a=2, n=64) for x in (g_ke, g_kE))
                    et = g_et[:, d, :].rearrange("p (t a) -> p t a", a=2)
                    near, far = (0, 1) if d == 0 else (1, 0)
                    cp(s4[:, :, near], q4[:, :, near])
                    tt(s4[:, :, far], q4[:, :, far], et[:, 2:QT, near].unsqueeze(2).to_broadcast([P, LT, 64]), MUL)
                    cp(k4[:, :, far], e4[:, :, far])
                    tt(k4[:, :, near], e4[:, :, near], et[:, :, far].unsqueeze(2).to_broadcast([P, QT, 64]), MUL)
                    tt(g_dec[:, d, :], et[:, :, 0], et[:, :, 1], MUL).then_inc(gk_ready, 1)
                    if d == 0:
                        values(0)
                values(1)
                values(2)
                tri = tri_fb.bitcast(U32).rearrange("p (d n) -> p d n", d=2).unsqueeze(2).to_broadcast([P, 2, LT, P])
                order = ([0, 1, 2, 3, 4], [1, 0, 5, 4, 3])
                for d in range(2):
                    for i, t in enumerate(order[d]):
                        if i in (0, 4):
                            finished(dve, S, it, 10 + 2 * d + i // 4)
                        p = unit(S, 10 + 2 * d + i // 4)[:, (i % 4) // 2, (i % 2) * 256:(i % 2) * 256 + 256]
                        if i == 0:
                            ins = cp(g_S[:, d, 0, :], p)
                        else:
                            ins = stt(g_S[:, d, i, :], g_S[:, d, i - 1, :], g_dec[:, d, t:t + 1], p, MUL, ADD)
                        if i == 3:
                            free(ins, S, 10 + 2 * d)
                            emptied(dve, S, it, 10 + 2 * d)
                        elif i == 4:
                            free(ins, S, 11 + 2 * d)
                        else:
                            st.did(ins)
                            if d == 0 and i == 0:
                                free(dve.copy_predicated(g_AT.rearrange("p d (t n) -> p d t n", n=P), tri,
                                                         unit(S, 9).rearrange("p d (t n) -> p d t n", n=P)), S, 9)
                            st.settle()
                for b in range(2):
                    finished(dve, S, it, 14 + b)
                    free(cp(g_o[:, b, :], unit(S, 14 + b)[:, 0, :]), S, 14 + b)
                dve.wait_ge(gdev_ready, it * 1 + 1)
                st.did(dve.reciprocal(rstd[:, 0:SEQ], rstd[:, 0:SEQ]))
                st.settle()
                for b in range(2):
                    st.did(stt(g_o[:, b, :], g_o[:, b, :], col("gla_g_o", b), rstd[:, 0:SEQ], MUL, MUL))
                st.settle()
                tt(g_out[:, bass.ds(it * 2, 2), :], g_o, g_r, MUL).then_inc(g_done, 1)
            st.leave(GLA_H)
            out_y("gla_out", SEQ)
            residual("y1", SEQ, 1, 1)
            normed("h1m", SEQ)
            mlp(1, SEQ)
            residual("y1m", SEQ, 1, 3)

            finished(dve, "gdn_gate", 0, 0)
            dve.wait_ge(d_ga, 1)
            free(ts(rstd[0:GDN_H, 0:SEQ], unit("gdn_gate", 0)[0:GDN_H, 0, :], a_dt[:, 1:2], None, ADD), "gdn_gate", 0)
            dve.wait_ge(d_ga, 2)
            st.did(stt(rstd[0:GDN_H, 0:SEQ], rstd[0:GDN_H, 0:SEQ], 0.0, sq[0:GDN_H, 0, 0:SEQ], MAX, ADD))
            st.settle()
            st.did(ts(rstd[0:GDN_H, 0:SEQ], rstd[0:GDN_H, 0:SEQ], a_dt[:, 2:3], -1.0, MUL, MUL))
            st.settle()
            dve.wait_ge(tab_in, 48)
            dve.tensor_tensor_scan(d_row[:, 1, :], keep128[0:GDN_H, :], rstd[0:GDN_H, 0:SEQ], 0.0, MUL, ADD).then_inc(d_rows, 1)
            emptied(dve, "gdn_gate", 0, 1)
            dve.memset(d_S[:, :, :], 0.0).then_inc(d_rows, 1)
            dve.wait_ge(d_cols, 1)
            cp(d_col[:, 0:2].rearrange("p r c h -> p (r c h)"), sc[:, 1, 0, 0:64]).then_inc(d_gc, 1)
            dve.wait_ge(d_gc, 1)
            dve.wait_ge(d_cols, 2)
            gl = sc[:, 1, 1, 0:32].rearrange("p (c h) -> p c h", c=LT)
            cp(d_col[:, 4], gl)
            tt(d_col[:, 3], gl, d_col[:, 1], SUB).then_inc(d_glr, 1)
            dve.wait_ge(d_ga, 3)
            st.did(ts(d_col[:, 2], d_col[:, 2], -1.0, None, MUL))
            st.settle()
            for j in range(2):
                dve.memset(d_cp[:, j, :, 0:3], 0.0).then_inc(d_conv, 1)
            dve.memset(d_r[:, :, :], 0.0).then_inc(d_done, 1)
            dve.wait_ge(d_done, 1)
            dve.wait_ge(d_conv, 2)
            S = "gdn_pair"
            colh = lambda r, c, it, e: d_col[:, r, c, bass.ds(it * 2 + e, 1)]
            with dve.Fori(0, GDN_H // 2) as it:
                st.enter(it, 31)
                for j, x in enumerate((d_q, d_k, d_v)):
                    emptied(dve, S, it, j)
                    for tap in (3, 0, 1, 2):
                        for e in range(2):
                            w = dyncol("gdn_conv_w", it * 2 + (24 * tap + 8 * j + e))
                            s = d_cp[:, j % 2, e, tap:tap + SEQ]
                            if tap == 3:
                                ins = ts(x[:, e, :], s, w, None, MUL)
                            else:
                                ins = stt(x[:, e, :], s, w, x[:, e, :], MUL, ADD)
                            if tap == 2 and e == 1:
                                ins.then_inc(d_conv, 1)
                            else:
                                st.did(ins)
                        if tap != 2:
                            st.settle()
                for r in range(2):
                    if r:
                        finished(dve, S, it, 5)
                    for e in range(2):
                        ins = ts(sq[0:GDN_H, e, 0:SEQ], d_row[:, 1 - r, :], ident[0:GDN_H, bass.ds(it * 2 + e, 1)], None, MUL)
                    ins.then_inc(d_masked, 1)
                emptied(dve, S, it, 7)
                st.did(dve.reciprocal(d_Y, d_Y))
                st.settle()
                stt(d_q, d_q, P ** -0.5, d_Y, MUL, MUL).then_inc(d_norm, 1)
                emptied(dve, S, it, 5)
                for e in range(2):
                    for c in range(LT):
                        t = slice(c * P, (c + 1) * P)
                        last = ts(d_ET[:, e, t], d_gcR[:, e, t], colh(1, c, it, e), 0.0, SUB, MIN)
                last.then_inc(d_diff, 1)
                emptied(dve, S, it, 8)
                st.did(dve.reciprocal(d_U, d_U))
                st.settle()
                tt(d_k, d_k, d_U, MUL).then_inc(d_norm, 1)
                dve.wait_ge(d_exp, it * 2 + 1)
                emptied(dve, S, it, 6)
                st.did(tt(d_LT, d_ET, d_bR, MUL))
                st.settle()
                finished(dve, S, it, 9)
                free(tt(d_LT, d_LT, unit(S, 9), MUL), S, 9)
                emptied(dve, S, it, 9)
                c8 = lambda m: m.unsqueeze(1).to_broadcast([P, 2 * LT, P])
                cp(chunks(d_T), c8(ident))
                cp(chunks(d_U), c8(ident)).then_inc(d_init, 1)

                def level_mask(l):
                    tt(chunks(d_Lm[:, l % 2]), chunks(d_LT), c8(lvl_mask[l]), MUL).then_inc(d_lm, 1)

                level_mask(0)
                level_mask(1)
                st.did(tt(chunks(d_ET), chunks(d_ET), c8(causal), MUL))
                st.settle()
                finished(dve, S, it, 10)
                free(tt(d_QK, d_ET, unit(S, 10), MUL), S, 10)
                finished(dve, S, it, 11)
                for e in range(2):
                    for c in range(LT):
                        t = slice(c * P, (c + 1) * P)
                        last = ts(d_kend[:, e, t], unit(S, 11)[:, e, t], colh(3, c, it, e), None, MUL)
                free(last, S, 11)
                finished(dve, S, it, 12)
                free(cp(d_V, unit(S, 12)), S, 12)
                for l in range(7):
                    j = 13 + 3 * l
                    if l < 6:
                        finished(dve, S, it, j + 1)
                        free(tt(d_T, d_T, unit(S, j + 1), SUB), S, j + 1)
                    k = j + 2 if l < 6 else j + 1
                    finished(dve, S, it, k)
                    free(tt(d_U, d_U, unit(S, k), SUB), S, k)
                    emptied(dve, S, it, k)
                    if l < 6:
                        emptied(dve, S, it, j + 1)
                    if l + 2 < 7:
                        level_mask(l + 2)
                    if l == 0:
                        dve.wait_ge(d_exp, it * 2 + 2)
                        tt(d_qE, d_q, d_v, MUL)
                        dve.memset(d_S[:, :, :], 0.0).then_inc(d_qe, 1)
                for c in range(LT):
                    t, j = slice(c * P, (c + 1) * P), 33 + 4 * c
                    finished(dve, S, it, j)
                    for e in range(2):
                        ins = stt(d_r[:, e, :], unit(S, j)[:, e, 0:P], colh(2, c, it, e), d_V[:, e, t], MUL, ADD)
                        if e:
                            free(ins, S, j)
                        else:
                            st.did(ins)
                    emptied(dve, S, it, j)
                    st.settle()
                    for e in range(2):
                        ins = ts(d_r[:, e, :], d_r[:, e, :], colh(0, c, it, e), None, MUL)
                    ins.then_inc(d_rr, 1)
                    finished(dve, S, it, j + 3)
                    for e in range(2):
                        ins = stt(d_S[:, e, :], d_S[:, e, :], colh(4, c, it, e), unit(S, j + 3)[:, e, 0:P], MUL, ADD)
                    free(ins, S, j + 3)
                    emptied(dve, S, it, j + 3)
                emptied(dve, S, it, 49)
                st.did(dve.reciprocal(d_Y, d_Y))
                st.settle()
                st.did(stt(d_o, d_o, col("gdn_norm_w", 0), d_Y, MUL, MUL))
                st.settle()
                tt(d_out[:, bass.ds(it * 2, 2), :], d_o, d_z, MUL).then_inc(d_done, 1)
            st.leave(GDN_H // 2)

            def add_residual(stage, l, q, loop, phase=None):
                if not loop:
                    for j in range(8):
                        finished(dve, stage, 0, j)
                        free(stt(xT[:, j, CTX:T], unit(stage, j)[:, 0, :], dcol[:, l, q, j, 0:1], xT[:, j, CTX:T], MUL, ADD), stage, j)
                    return
                with dve.Fori(0, 4) as it:
                    st.enter(it, MOD_IT * MOD_Q * (MOD_K - 1) if phase else 0)
                    for j in range(2):
                        if phase:
                            for c in range(j * MOD_UNIT, (j + 1) * MOD_UNIT):
                                mod_chunk(phase, it, c, (2,))
                        finished(dve, stage, it, j)
                        x = xT[:, bass.ds(it * 2 + j, 1), CTX:T]
                        free(stt(x, unit(stage, j)[:, 0:1, :], dcol[:, l, q, bass.ds(it * 2 + j, 1), 0], x, MUL, ADD), stage, j)
                st.leave(4)
                if phase:
                    dve.wait_ge(mod_summed, 2 + MOD_CHUNKS * (phase + 1))
                    modulation(phase + 1, 0, 6, 1)
                    dve.wait_ge(mod_ready, 3 + phase)

            def layer_norm(name, i):
                dve.wait_ge(n_mean, i + 1)
                for b in range(DB):
                    stt(xT[:, b, CTX:T], sc[:, 0, 1, :], -1.0 / D, xT[:, b, CTX:T], MUL, ADD).then_inc(n_cent, 1)
                reciprocal_of(name, SEQ)
                for b in range(DB):
                    tt(xT[:, b, CTX:T], xT[:, b, CTX:T], rstd[:, 0:SEQ], MUL).then_inc(n_mul, 1)

            def ffn(i):
                up = f"ffn{i}_up"
                dve.memset(gpad[:, :, 0:2], 0.0).then_inc(f_conv, 1)
                with dve.Fori(0, HIDB // 2) as it:
                    st.enter(it, 2 * 2)
                    emptied(dve, up, it, 0)
                    for tap in (2, 0, 1):
                        for b in range(2):
                            w = dyncol(f"conv_w{i}", it * 2 + (HIDB * tap + b))
                            s = gpad[:, b, tap:tap + SEQ]
                            if tap == 2:
                                ins = ts(gconv[:, b, :], s, w, dyncol("conv_b", it * 2 + (HIDB * i + b)), MUL, ADD)
                            else:
                                ins = stt(gconv[:, b, :], s, w, gconv[:, b, :], MUL, ADD)
                            if tap == 1 and b == 1:
                                ins.then_inc(f_conv, 1)
                            elif tap == 1:
                                pass
                            else:
                                st.did(ins)
                        if tap != 1:
                            st.settle()
                    dve.wait_ge(f_silu, it * 1 + (HIDB // 2 * i + 1))
                    finished(dve, up, it, 1)
                    free(tt(hid2[:, bass.ds(it * 2, 2), :], gsilu, unit(up, 1), MUL), up, 1)
                st.leave(HIDB // 2)

            add_residual("gdn_out", 2, 1, False)
            layer_norm("ln0", 0)
            ffn(0)
            add_residual("ffn0_down", 2, 3, True, 2)
            layer_norm("ln0f", 1)

            dve.memset(gpad[:, :, 0:2], 0.0).then_inc(r_done, 1)
            dve.wait_ge(rtab_in, 16)
            tcos, tsin = r_tab[:, 0, :], r_tab[:, 1, :]
            S = "ret_head"
            with dve.Fori(0, RET_H) as it:
                st.enter(it, 10)
                for i in range(2):
                    emptied(dve, S, it, i)
                    a, b = r_raw[:, i, 0, :], r_raw[:, i, 1, :]
                    oa, ob = r_rot[:, i, 0, :], r_rot[:, i, 1, :]
                    st.did(tt(r_tmp[:, 0, :], b, tsin, MUL))
                    st.did(tt(r_tmp[:, 1, :], b, tcos, MUL))
                    st.did(tt(oa, a, tcos, MUL))
                    st.did(tt(ob, a, tsin, MUL))
                    st.settle()
                    tt(oa, oa, r_tmp[:, 0, :], SUB)
                    tt(ob, ob, r_tmp[:, 1, :], ADD).then_inc(r_rotd, 1)
                    dve.wait_ge(r_rotd, it * 2 + i + 1)
                for j in range(2):
                    finished(dve, S, it, 2 + j)
                    free(cp(r_v[:, 2 * j:2 * j + 2, :], unit(S, 2 + j)), S, 2 + j)
                for j in range(2):
                    finished(dve, S, it, 6 + j)
                    for i in range(2):
                        t = 2 * j + i
                        w = SEQ - t * P
                        ins = tt(r_s[:, t:t + 1, 0:w], unit(S, 6 + j)[:, i:i + 1, 0:w],
                                 r_tab[:, bass.ds(it * 1 + 2, 1), 0:w], MUL)
                    free(ins, S, 6 + j)
                for j in range(2):
                    finished(dve, S, it, 8 + j)
                    free(cp(r_o[:, 2 * j:2 * j + 2, :], unit(S, 8 + j)), S, 8 + j)
                emptied(dve, S, it, 8)
                emptied(dve, S, it, 9)
                finished(dve, S, it, 10)
                for b in range(4):
                    ins = stt(r_o[:, b, :], unit(S, 10)[:, 0, :], -1.0 / RET_DV, r_o[:, b, :], MUL, ADD)
                    if b < 3:
                        ins.then_inc(r_cent, 1)
                    else:
                        free(ins, S, 10)
                emptied(dve, S, it, 11)
                st.did(dve.reciprocal(rstd[:, 0:SEQ], rstd[:, 0:SEQ]))
                st.settle()
                st.did(tt(r_o, r_o, rstd[:, 0:SEQ].unsqueeze(1).to_broadcast([P, 4, SEQ]), MUL))
                st.settle()
                tt(r_out[:, bass.ds(it * 4, 4), :], r_o, r_gate, MUL).then_inc(r_done, 1)
            st.leave(RET_H)
            add_residual("ret_out", 3, 1, False)
            layer_norm("ln1", 2)
            ffn(1)
            add_residual("ffn1_down", 3, 3, True)
            layer_norm("ln1f", 3)
            for t in range(LT):
                dve.wait_ge(o_turned, t + 1)
                cp(o_tok[:, t, :], flat(sc[:, t % 2])).then_inc(o_moved, 1)


def tables():
    f = np.float32
    eye = np.eye(P, dtype=f)
    base = np.concatenate([eye, np.ones((P, P), f)], 1)
    i, j = np.arange(P)[None, :], np.arange(P)[:, None]
    swap = np.zeros((64, 64), f)
    for g in (0, 32):
        for a in range(16):
            swap[g + a, g + 16 + a], swap[g + 16 + a, g + a] = -1.0, 1.0
    rot2 = np.kron(np.eye(2, dtype=f), swap).T
    pad = np.zeros((64, P), f)
    dup = np.concatenate([np.concatenate([np.eye(64, dtype=f)] * 2, 1), pad], 0)
    rotdup = np.concatenate([np.concatenate([swap.T] * 2, 1), pad], 0)
    tok = np.arange(SEQ)
    inv = (f(10000.0) ** (-np.arange(0, 32, 2, dtype=f) / f(32))).astype(f)
    ang = np.concatenate([inv[:, None] * (tok // 64).astype(f)] * 2 + [inv[:, None] * (tok % 64).astype(f)] * 2, 0)
    ang = np.concatenate([ang, ang], 0).astype(f)
    mla = np.concatenate([rot2, dup, rotdup, np.cos(ang), np.sin(ang)], 1)
    keep = np.ones((P, T), f)
    keep[:, ::64] = 0.0
    gla = np.concatenate([keep, j <= i, j >= i], 1)
    lv = [((i // (2 * s)) == (j // (2 * s))) & ((i // s) % 2 == 1) & ((j // s) % 2 == 0) for s in LEVELS]
    last = np.zeros((P, P), f)
    last[P - 1] = 1.0
    keep = np.ones((P, SEQ), f)
    keep[:, ::P] = 0.0
    gdn = np.concatenate(lv + [j <= i, last, keep], 1)
    inv = (f(10000.0) ** (-np.linspace(0.0, 1.0, P, dtype=f))).astype(f)
    ang = (inv[:, None] * tok.astype(f)[None, :]).astype(f)
    rel = np.arange(SEQ, dtype=f)[None, :] - np.arange(P, dtype=f)[:, None]
    lg = np.log(f(1.0) - np.power(f(2.0), f(-5.0) - np.arange(RET_H, dtype=f))).astype(f)
    dec = [np.where(rel >= 0, np.exp(np.maximum(rel, f(0)) * g), f(0)) for g in lg]
    ret = np.concatenate([np.cos(ang), np.sin(ang)] + dec, 1)
    return {n: np.ascontiguousarray(a, dtype=f) for n, a in
            (("tab_base", base), ("tab_mla", mla), ("tab_gla", gla), ("tab_gdn", gdn), ("tab_ret", ret))}


INPUTS = ["x", "c", "ctx", "c_ctx", "ada_w", "ada_b", "norm_g", "mlp_w1", "mlp_w2", "mla_w_dq", "mla_g_q", "mla_w_uq",
          "mla_w_dkv", "mla_g_kv", "mla_w_ukv", "mla_w_o", "gla_w_q", "gla_w_k", "gla_w_v", "gla_w_r", "gla_w_gate1",
          "gla_w_gate2", "gla_b_gate", "gla_g_o", "gla_w_o", "c_2", "cond_w_2", "cond_b_2", "ada_w_2", "ada_b_2",
          "ln_g_2", "ln_b_2", "ffn_up_2", "ffn_conv_w_2", "ffn_conv_b_2", "ffn_down_2", "gdn_w_in_2", "gdn_conv_w_2",
          "gdn_a_log_2", "gdn_dt_bias_2", "gdn_norm_w_2", "gdn_w_out_2", "ret_w_in_2", "ret_w_out_2"]


def kernel(**inputs):
    import numpy as _np
    import concourse.bacc as _bacc
    from concourse import mybir as _mybir
    from concourse.bass_utils import run_bass_kernel_spmd as _run

    nc = _bacc.Bacc("TRN2", target_bir_lowering=False, num_devices=1)
    given = {n: _np.ascontiguousarray(inputs[n]) for n in INPUTS}
    given.update(tables())
    arrays, A = {}, {}
    for name, a in given.items():
        arrays[f"in_{name}"] = a
        A[name] = nc.dram_tensor(f"in_{name}", a.shape, _mybir.dt.from_np(a.dtype), kind="ExternalInput").ap()
    out = nc.dram_tensor("out_0", (1, SEQ, D), _mybir.dt.float32, kind="ExternalOutput").ap()
    first_and_second_block(nc, A, out)
    r = _run(nc, [arrays], core_ids=[0])
    return r.results[0]["out_0"]
```

```python
import numpy as np
import concourse.bass as bass
from concourse import mybir
from contextlib import ExitStack

ACT = mybir.ActivationFunctionType
ALU = mybir.AluOpType
F32 = mybir.dt.float32
F32R = mybir.dt.float32r
U32 = mybir.dt.uint32
XY = mybir.AxisListType.XY

P = 128
D = 1024
DB = D // P
CTX, SEQ = 256, 512
T = CTX + SEQ
HALF = T // 2
FF = 4096
FFB = FF // P
HID = 2816
HIDB = HID // P
MLA_H, NOPE, ROPE, Q_RANK, KV_RANK = 8, 128, 64, 384, 256
GLA_H, GLA_DV, GATE_RANK = 4, 256, 16
GDN_H = 8
RET_H, RET_DK, RET_DV = 4, 256, 512
ALPHA = (2.0 * 2) ** 0.25
QT, KT = T // P, T // P
LT = SEQ // P
LEVELS = [1, 2, 4, 8, 16, 32, 64]

VEC = {}
_rows = 0
for _name, _n in [
    ("ada_b", 96), ("c", 8), ("c_ctx", 8), ("c_2", 8), ("cond_b", 8),
    ("ada_b_2", 96), ("ln_g_2", 32),
    ("norm_g", 64), ("ln_b_2", 32), ("mla_g_q", 3), ("mla_g_kv", 2), ("gla_b_gate", 8), ("gla_g_o", 2),
    ("gdn_norm_w", 1), ("pad", 16),
    ("conv_w0", 66), ("conv_b", 44), ("pad2", 18),
    ("conv_w1", 66), ("pad3", 62),
    ("gdn_conv_w", 96), ("pad4", 32),
]:
    VEC[_name] = (_rows // P, _rows % P, _n)
    _rows += _n
VEC_TILES = _rows // P

STAGES = [
    ("ada", 1, 4, 0),
    ("mla_in", 1, 2, 6), ("mla_rope", 1, 0, 2), ("mla_pair", 4, 6, 34), ("mla_out", 1, 2, 8),
    ("mlp0", 4, 8, 16),
    ("gla_gate", 1, 0, 2), ("gla_head", 4, 4, 16), ("gla_out", 1, 2, 8),
    ("mlp1", 4, 8, 16),
    ("gdn_gate", 1, 2, 2), ("gdn_pair", 4, 4, 48), ("gdn_out", 1, 2, 8),
    ("ffn0_up", 11, 2, 2), ("ffn0_down", 4, 2, 2),
    ("ret_head", 4, 6, 12), ("ret_out", 1, 4, 8),
    ("ffn1_up", 11, 2, 2), ("ffn1_down", 4, 2, 2),
]
SPLIT = ("mlp0", "mlp1", "ffn0_up", "ret_head", "ffn1_up")
GROUP0, UNIT0, GROUPS, UNITS, SPLIT0 = {}, {}, {}, {}, {}
_g = _u = _w = 0
for _s, _n, _gi, _ui in STAGES:
    GROUP0[_s], UNIT0[_s], GROUPS[_s], UNITS[_s] = _g, _u, _gi, _ui
    _g, _u = _g + _n * _gi, _u + _n * _ui
    if _s in SPLIT:
        SPLIT0[_s], _w = _w, _w + _n * _gi
    assert _gi % 2 == 0 and _ui % 2 == 0
    if _s == "gdn_pair":
        _g -= 2

MOD_SLOTS, MOD_Q = 4, 2
MOD_K = DB // MOD_Q
MOD_CHUNKS = 6 * DB
MOD_IT, MOD_UNIT = MOD_CHUNKS // 4, MOD_CHUNKS // 8
MOD_BESIDE = {g: (2 * n, 2 * n + 1) for n, g in enumerate((1, 2, 3, 5, 6, 7))}
MOD_AT = 512 - 96

NORMS = {}
_b = 0
for _k, (_s, _n) in enumerate([
    ("h0", 8), ("cq", 3), ("ckv", 2), ("y0", 8), ("h0m", 8), ("y0m", 8),
    ("h1", 8), ("y1", 8), ("h1m", 8), ("y1m", 8),
    ("ln0", 8), ("ln0f", 8), ("ln1", 8), ("ln1f", 8),
]):
    NORMS[_s] = (_k, _b, _n)
    _b += _n


class Steps:

    def __init__(self, eng, sem):
        self.eng, self.sem, self.n, self.it, self.per, self.local = eng, sem, 0, None, 0, 0

    def did(self, ins):
        ins.then_inc(self.sem, 1)
        if self.it is None:
            self.n += 1
        else:
            self.local += 1

    def settle(self):
        v = self.n if self.it is None else self.it * self.per + (self.n + self.local)
        self.eng.wait_ge(self.sem, v)

    def enter(self, it, per):
        self.it, self.per, self.local = it, per, 0

    def leave(self, iterations):
        assert self.local == self.per, (self.local, self.per)
        self.n, self.it = self.n + iterations * self.per, None


def first_and_second_block(nc, A, out):
    ctx = ExitStack()
    with ctx:
        def sb(name, shape, dt=F32):
            return ctx.enter_context(nc.sbuf_tensor(name, shape, dt))

        def sem(name):
            return ctx.enter_context(nc.semaphore(name))

        xT = sb("xT", [P, DB, T])
        base_tab = sb("base_tab", [P, 2 * P])
        ident, ones = base_tab[:, 0:P], base_tab[:, P:2 * P]
        tab = sb("tab", [P, 2048])
        cols = sb("cols", [P, VEC_TILES, P])
        cs = sb("cs", [P, DB, 3])
        mod = sb("mod", [P, 4, 48, 2])
        dcol = sb("dcol", [P, 4, 4, DB, 2])
        ln_col = sb("ln_col", [P, 3, 2, DB])
        eps = sb("eps", [P, 2])
        sq = sb("sq", [P, 2, T])
        rstd = sb("rstd", [P, T])
        gate1 = sb("gate1", [P, DB, 2, GATE_RANK])
        gate2 = sb("gate2", [GATE_RANK, 2, P])
        w_ab = sb("w_ab", [P, DB, 16])
        a_dt = sb("a_dt", [GDN_H, 3])
        d_row = sb("d_row", [GDN_H, 2, SEQ])
        d_col = sb("d_col", [P, 5, LT, GDN_H])
        with ExitStack() as plain:
            def first(name, shape, dt=F32):
                return plain.enter_context(nc.sbuf_tensor(name, shape, dt))

            hT = first("hT", [P, DB, T])
            arena = first("arena", [P, FFB * T])
            wring = [first(f"wring{s}", [P, 4096]) for s in range(2)]
        with ExitStack() as plain:
            first("hT_", [P, DB, T])
            first("before_x_hi", [P, 2 * DB * T])
            x_hi_seq = first("x_hi_seq", [P, DB, SEQ], F32R)
        x_lo = sb("x_lo", [P, DB, T], F32R)
        hid_hi, hid_lo = sb("hid_hi", [P, DB, T], F32R), sb("hid_lo", [P, DB, T], F32R)
        x_hi = sb("x_hi", [P, DB, T], F32R)
        sb("others", [P, DB, T])
        w_lo, w_hi = [None, None], [None, None]
        for s in range(2):
            w_lo[s], w_hi[s] = sb(f"w_lo{s}", [P, 2048], F32R), sb(f"w_hi{s}", [P, 2048], F32R)
        acc = ctx.enter_context(nc.psum_tensor("acc", [P, 2, 2, 512], F32))
        sc = ctx.enter_context(nc.psum_tensor("sc", [P, 2, 2, 512], F32))

        at = [0]

        def carve(*shape):
            n = int(np.prod(shape))
            a = arena[:, at[0]:at[0] + n]
            at[0] += n
            assert at[0] <= FFB * T, at[0]
            if len(shape) == 1:
                return a
            names = " ".join(f"a{i}" for i in range(len(shape)))
            return a.rearrange(f"p ({names}) -> p {names}", **{f"a{i}": s for i, s in enumerate(shape)})

        x_tok = carve(QT, D)
        vrow = carve(VEC_TILES, P)
        ada_row = carve(4, 512)
        at[0] = 0
        o_tok = carve(LT, D)
        at[0] = 0
        split_parts = carve(3, DB, T)
        y_mlp = carve(DB, T)
        relu = sq
        at[0] = 0
        hid2 = carve(HIDB, SEQ)
        at[0] = 3 * DB * T
        gpad = carve(2, SEQ + 2)
        gconv = carve(2, SEQ)
        gsilu = carve(2, SEQ)
        at[0] = 0
        cq = carve(3, T)
        ckv = carve(2, T)
        krope = carve(2, T)
        kraw = carve(T)
        ktmp = carve(SEQ)
        qn = carve(2, T)
        qr = carve(T)
        qraw = carve(T)
        kn = carve(2, T)
        vtok = carve(QT, 256)
        prob = carve(2, T)
        probT = carve(2, T)
        attn = carve(MLA_H, T)
        small = carve(2, 4)
        at[0] = 0
        hgate = carve(2, T)
        g_q = carve(SEQ)
        g_k = carve(T)
        g_v = carve(QT, GLA_DV)
        g_r = carve(2, SEQ)
        g_z = carve(2, T)
        g_l = carve(T)
        g_o = g_z[:, :, 0:SEQ]
        g_g = carve(T)
        g_G = carve(T)
        g_tot = carve(2, 12)
        g_et = carve(2, 12)
        g_dec = carve(2, QT)
        g_qt = carve(2, SEQ)
        g_kt = carve(2, SEQ)
        g_ke = carve(2, T)
        g_qS = carve(2, SEQ)
        g_kE = carve(2, T)
        g_kEt = carve(2, 5 * P)
        g_AT = carve(2, SEQ)
        g_S = carve(2, 5, GLA_DV)
        g_out = carve(DB, SEQ)
        at[0] = 0
        d_cp = carve(2, 2, SEQ + 3)
        d_q = carve(2, SEQ)
        d_k = carve(2, SEQ)
        d_v = carve(2, SEQ)
        d_z = carve(2, SEQ)
        d_gcR = carve(2, SEQ)
        d_o = d_gcR
        d_bR = carve(2, SEQ)
        d_ET = carve(2, SEQ)
        d_LT = carve(2, SEQ)
        d_Lm = carve(2, 2, SEQ)
        d_T = carve(2, SEQ)
        d_U = carve(2, SEQ)
        d_Y = carve(2, SEQ)
        d_QK = carve(2, SEQ)
        d_kend = carve(2, SEQ)
        d_V = carve(2, SEQ)
        d_qE = carve(2, SEQ)
        d_S = carve(2, P)
        d_r = carve(2, P)
        d_vn = carve(2, P)
        d_out = carve(GDN_H, SEQ)
        at[0] = 0
        r_out = carve(16, SEQ)
        r_raw = carve(2, 2, SEQ)
        r_sqr = r_raw.rearrange("p a b n -> p (a b) n")
        r_rot = carve(2, 2, SEQ)
        x_hi_plain = carve(DB, SEQ)
        r_tab = carve(6, SEQ)
        r_s = carve(LT, SEQ)
        r_o = carve(4, SEQ)
        r_tmp = tab[:, 0:2 * SEQ].rearrange("p (a n) -> p a n", a=2)
        r_v = hT[:, :, 0:CTX].rearrange("p (t a) n -> p t a n", a=2)
        r_gate = xT[:, :, 0:CTX].rearrange("p (e a) n -> p e a n", a=2)

        mod_w = [a.rearrange("p (k n) -> p k n", k=MOD_K)
                 for a in (tab[:, 0:512], tab[:, 512:1024], tab[:, 1024:1536], rstd[:, 0:512])]
        mod_acc = tab[:, 1536:2048].rearrange("p (s v n) -> p s v n", s=2, v=2)
        mod_psum = sc[:, 1, 1, :]

        rot2, dup, rotdup = tab[:, 0:P], tab[0:64, P:2 * P], tab[0:64, 2 * P:3 * P]
        rcos, rsin = tab[:, 384:384 + SEQ], tab[:, 896:896 + SEQ]
        keep64, tri_fb = tab[:, 0:T], tab[:, T:T + 2 * P]
        lvl_mask = [tab[:, l * P:(l + 1) * P] for l in range(7)]
        causal, last_row, keep128 = tab[:, 896:1024], tab[:, 1024:1152], tab[:, 1152:1664]

        const_in = sem("const_in")
        x_in = sem("x_in")
        gate1_in, ab_in = sem("gate1_in"), sem("ab_in")
        tab_in, rtab_in = sem("tab_in"), sem("rtab_in")
        gate2_in = sem("gate2_in")
        out_done = sem("out_done")
        w_loaded = [sem(f"w_loaded{s}") for s in range(2)]
        w_high = sem("w_high")
        w_split = sem("w_split")
        x_high, x_split = sem("x_high"), sem("x_split")
        hid_square, hid_high = sem("hid_square"), sem("hid_high")
        ln_cols = sem("ln_cols")
        w_used = sem("w_used")
        acc_ready = sem("acc_ready")
        acc_free = [sem(f"acc_free{s}") for s in range(2)]
        dve_step, act_step = sem("dve_step"), sem("act_step")
        vec_turned, cols_ready = sem("vec_turned"), sem("cols_ready")
        x_turned, x_moved = sem("x_turned"), sem("x_moved")
        c_ready, e_ready = sem("c_ready"), sem("e_ready")
        ada_ready, ada_moved = sem("ada_ready"), sem("ada_moved")
        ada_done, mod_ready = sem("ada_done"), sem("mod_ready")
        mod_loaded = [sem(f"mod_loaded{s}") for s in range(MOD_SLOTS)]
        mod_used = [sem(f"mod_used{s}") for s in range(MOD_SLOTS)]
        mod_summed = sem("mod_summed")
        x_ready = sem("x_ready")
        n_sq, n_used = sem("n_sq"), sem("n_used")
        n_std = sem("n_std")
        n_mul, h_ready = sem("n_mul"), sem("h_ready")
        n_mean, n_cent = sem("n_mean"), sem("n_cent")
        lat_ready, krope_ready = sem("lat_ready"), sem("krope_ready")
        qrope_ready, s_ready = sem("qrope_ready"), sem("s_ready")
        p_max, p_exp, p_ready = sem("p_max"), sem("p_exp"), sem("p_ready")
        relu_free = sem("relu_free")
        gl_ready, gG_ready, gE_ready = sem("gl_ready"), sem("gG_ready"), sem("gE_ready")
        gk_ready, gsq_ready = sem("gk_ready"), sem("gsq_ready")
        gr_ready, gss_ready, gdev_ready = sem("gr_ready"), sem("gss_ready"), sem("gdev_ready")
        g_done = sem("g_done")
        d_rows, d_cols, d_ga, d_gc = sem("d_rows"), sem("d_cols"), sem("d_ga"), sem("d_gc")
        d_masked, d_conv, d_silu = sem("d_masked"), sem("d_conv"), sem("d_silu")
        d_sq, d_len, d_norm, d_diff = sem("d_sq"), sem("d_len"), sem("d_norm"), sem("d_diff")
        d_exp, d_lt, d_lm, d_qe = sem("d_exp"), sem("d_lt"), sem("d_lm"), sem("d_qe")
        d_init, d_rr, d_done, d_glr = sem("d_init"), sem("d_rr"), sem("d_done"), sem("d_glr")
        qk_ready, qk_moved = sem("qk_ready"), sem("qk_moved")
        f_conv, f_silu = sem("f_conv"), sem("f_silu")
        r_rotd, r_cent, r_sq, r_done = sem("r_rotd"), sem("r_cent"), sem("r_sq"), sem("r_done")
        r_dev = sem("r_dev")
        o_turned, o_moved = sem("o_turned"), sem("o_moved")

        def unit(stage, j):
            return acc[:, (UNIT0[stage] + j) % 2]

        def flat(a):
            return a.rearrange("p a n -> p (a n)")

        def halves(a):
            return a.rearrange("p (h n) -> p h n", h=2)

        def chunks(a):
            return a.rearrange("p e (c n) -> p (e c) n", n=P)

        def loaded(eng, stage, it, j):
            g = GROUP0[stage] + j
            eng.wait_ge(w_loaded[g % 2], 16 * (g // 2 + 1) + it * (8 * GROUPS[stage]))
            return g % 2

        def half_group(stage, it, j, h):
            return 2 * (SPLIT0[stage] + j) + h + 1 + it * (2 * GROUPS[stage])

        def parts(s, k, n):
            return [w[s][:, 0:k * n].rearrange("p (k n) -> p k n", k=k) for w in (w_hi, w_lo)]

        def x_parts(n, k):
            if n == T:
                return [(h, HALF, x_hi[:, k, t], x_lo[:, k, t]) for h, t in ((0, slice(0, HALF)), (1, slice(HALF, T)))]
            return [(0, n, x_hi_seq[:, k, :], x_lo[:, k, CTX:T])]

        def finished(eng, stage, it, j):
            eng.wait_ge(acc_ready, UNIT0[stage] + j + 1 + it * UNITS[stage])

        def emptied(eng, stage, it, j):
            u = UNIT0[stage] + j
            eng.wait_ge(acc_free[u % 2], u // 2 + 1 + it * (UNITS[stage] // 2))

        def claim(eng, stage, it, j):
            u = UNIT0[stage] + j
            if u >= 2:
                eng.wait_ge(acc_free[u % 2], u // 2 + it * (UNITS[stage] // 2))

        def free(ins, stage, j):
            ins.then_inc(acc_free[(UNIT0[stage] + j) % 2], 1)

        def col(name, i):
            t, r, _ = VEC[name]
            return cols[:, t, r + i:r + i + 1]

        def vec(name, i, n):
            t, r, _ = VEC[name]
            return cols[:, t, r + i:r + i + n]

        def dyncol(name, i):
            t, r, _ = VEC[name]
            return cols[:, t, bass.ds(i + r, 1)]

        def mod_slot(i, q):
            return (MOD_Q * i + q) % MOD_SLOTS

        def piece(phase, it, i, by=1):
            a = MOD_SLOTS // MOD_Q
            return by * ((MOD_CHUNKS * phase + i) // a + 1) + it * (by * MOD_IT // a)

        rows = lambda a: a.rearrange("(r p) -> r p", p=P)
        rows2 = lambda a: a.rearrange("l (r p) -> (l r) p", p=P)
        rows3 = lambda a: a.rearrange("l i (r p) -> (l i r) p", p=P)
        vec_sources = [
            ("ada_b", rows2(A["ada_b"])), ("c", rows2(A["c"])), ("c_ctx", rows(A["c_ctx"])), ("c_2", rows2(A["c_2"])),
            ("cond_b", rows(A["cond_b_2"])), ("ada_b_2", rows2(A["ada_b_2"])), ("ln_g_2", rows3(A["ln_g_2"])),
            ("norm_g", rows3(A["norm_g"])), ("ln_b_2", rows3(A["ln_b_2"])), ("mla_g_q", rows2(A["mla_g_q"])),
            ("mla_g_kv", rows2(A["mla_g_kv"])), ("gla_b_gate", rows3(A["gla_b_gate"])), ("gla_g_o", rows2(A["gla_g_o"])),
            ("gdn_norm_w", rows(A["gdn_norm_w_2"])), ("conv_w0", rows2(A["ffn_conv_w_2"][0])),
            ("conv_b", rows2(A["ffn_conv_b_2"])), ("conv_w1", rows2(A["ffn_conv_w_2"][1])),
            ("gdn_conv_w", rows2(A["gdn_conv_w_2"])),
        ]
        consts = 16 * (1 + len(vec_sources))
        vec_rows = [max(VEC[n][1] + VEC[n][2] for n, _ in vec_sources if VEC[n][0] == t) for t in range(VEC_TILES)]

        block = ctx.enter_context(nc.Block())

        @block.sync
        def _(sp):
            def slot_free(stage, it, j):
                g = GROUP0[stage] + j
                if g >= 2:
                    sp.wait_ge(w_used, g + it * GROUPS[stage])
                return g % 2

            def load(stage, it, j, src, k, n):
                s = slot_free(stage, it, j)
                dst = wring[s][:, 0:k * n].rearrange("p (k n) -> p k n", k=k)
                sp.dma_start(dst, src).then_inc(w_loaded[s], 16)

            def blocks(w):
                return w.rearrange("(k p) n -> p k n", p=P)

            aw = [blocks(A["ada_w" if l < 2 else "ada_w_2"][l % 2]) for l in range(4)]
            for j in range(4):
                load("ada", 0, j, aw[0][:, :, j * 512:(j + 1) * 512], DB, 512)

            def in_columns(stage, w, n, k):
                wv, its = blocks(w), w.shape[1] // n // 2
                if dict((s, i) for s, i, _, _ in STAGES)[stage] == 1:
                    for j in range(2 * its):
                        load(stage, 0, j, wv[:, :, j * n:(j + 1) * n], k, n)
                    return
                with sp.Fori(0, its) as it:
                    for j in range(2):
                        load(stage, it, j, wv[:, :, bass.ds(it * (2 * n) + j * n, n)], k, n)

            def mod_pieces(phase, it, i):
                for q in range(MOD_Q):
                    s = mod_slot(i, q)
                    sp.wait_ge(mod_used[s], piece(phase, it, i))
                    sp.dma_start(mod_w[s], aw[phase + 1][:, MOD_K * q:MOD_K * (q + 1), bass.ds(
                        it * (MOD_IT * P) + i * P, P)]).then_inc(mod_loaded[s], 16)

            def mlp(i):
                w1, w2 = blocks(A["mlp_w1"][i]), blocks(A["mlp_w2"][i])
                with sp.Fori(0, 4) as it:
                    for g in range(8):
                        if g < 4:
                            load(f"mlp{i}", it, g, w1[:, :, bass.ds(it * D + g * 256, 256)], DB, 256)
                        else:
                            load(f"mlp{i}", it, g, w2[:, bass.ds(it * DB, DB), (g - 4) * 256:(g - 3) * 256], DB, 256)
                        if g == 1:
                            sp.wait_ge(n_mul, 16 + 16 * i)
                        for c in MOD_BESIDE.get(g - 1, ())[1:] + MOD_BESIDE.get(g, ())[:1]:
                            mod_pieces(i, it, c)
                    mod_pieces(i, it, MOD_BESIDE[7][1])

            def down(stage, w, k, phase=None):
                wv = blocks(w)
                if phase is not None:
                    sp.wait_ge(n_mul, 40)
                with sp.Fori(0, 4) as it:
                    for j in range(2):
                        load(stage, it, j, wv[:, :, bass.ds(it * (2 * P) + j * P, P)], k, P)
                        for i in range(j * MOD_UNIT, (j + 1) * MOD_UNIT if phase is not None else 0):
                            mod_pieces(phase, it, i)

            load("mla_in", 0, 0, blocks(A["mla_w_dq"][0]), DB, Q_RANK)
            load("mla_in", 0, 1, blocks(A["mla_w_dkv"][0]), DB, KV_RANK + ROPE)
            cw = blocks(A["cond_w_2"])
            uq, ukv = blocks(A["mla_w_uq"][0]), blocks(A["mla_w_ukv"][0])
            with sp.Fori(0, MLA_H // 2) as it:
                load("mla_pair", it, 0, uq[:, :, bass.ds(it * 384, 384)], 3, 384)
                load("mla_pair", it, 1, ukv[:, :, bass.ds(it * 512, 512)], 2, 512)
                for j in range(2):
                    load("mla_pair", it, 2 + j, aw[0][:, :, bass.ds(it * 1024 + 2 * D + j * 512, 512)], DB, 512)
                for j in range(2):
                    load("mla_pair", it, 4 + j, cw[:, :, bass.ds(it * 256 + j * P, P)], DB, P)
            in_columns("mla_out", A["mla_w_o"][0], 512, DB)
            mlp(0)
            gq, gk, gv, gr = (blocks(A[n][0]) for n in ("gla_w_q", "gla_w_k", "gla_w_v", "gla_w_r"))
            w2 = A["gla_w_gate2"][0].rearrange("d r n -> r d n")
            with sp.Fori(0, GLA_H) as it:
                sp.wait_ge(acc_ready, UNIT0["gla_head"] - UNITS["gla_head"] + 2 + it * UNITS["gla_head"])
                sp.dma_start(gate2[:, :, :], w2[:, :, bass.ds(it * P, P)]).then_inc(gate2_in, 16)
                load("gla_head", it, 0, gq[:, :, bass.ds(it * P, P)], DB, P)
                load("gla_head", it, 1, gk[:, :, bass.ds(it * P, P)], DB, P)
                load("gla_head", it, 2, gv[:, :, bass.ds(it * GLA_DV, GLA_DV)], DB, GLA_DV)
                load("gla_head", it, 3, gr[:, :, bass.ds(it * GLA_DV, GLA_DV)], DB, GLA_DV)
            in_columns("gla_out", A["gla_w_o"][0], 512, DB)
            sp.wait_ge(g_done, GLA_H + 1)
            mlp(1)
            gi = blocks(A["gdn_w_in_2"])
            for j in range(2):
                load("gdn_gate", 0, j, gi[:, :, j * D:j * D + 256], DB, 256)

            def gdn_pair(it, last):
                for j in range(2):
                    load("gdn_pair", it, j, gi[:, :, bass.ds(it * 256 + (2 + j) * D, 256)], DB, 256)
                for j in range(0 if last else 2):
                    load("gdn_pair", it, 2 + j, gi[:, :, bass.ds(it * 256 + (256 + j * D), 256)], DB, 256)

            with sp.Fori(0, GDN_H // 2 - 1) as it:
                gdn_pair(it, False)
            gdn_pair(GDN_H // 2 - 1, True)
            in_columns("gdn_out", A["gdn_w_out_2"], 512, DB)

            def ffn(i):
                up = blocks(A["ffn_up_2"][i])
                with sp.Fori(0, HIDB // 2) as it:
                    for j in range(2):
                        load(f"ffn{i}_up", it, j, up[:, :, bass.ds(it * 256 + j * HID, 256)], DB, 256)
                if i == 0:
                    sp.wait_ge(d_done, GDN_H // 2 + 1)
                down(f"ffn{i}_down", A["ffn_down_2"][i], HIDB, 2 if i == 0 else None)

            ffn(0)
            ri = blocks(A["ret_w_in_2"])
            with sp.Fori(0, RET_H) as it:
                for j in range(2):
                    load("ret_head", it, j, ri[:, :, bass.ds(it * 256 + j * D, 256)], DB, 256)
                for j in range(4):
                    load("ret_head", it, 2 + j, ri[:, :, bass.ds(it * 512 + ((2 + 2 * (j // 2)) * D + j % 2 * 256), 256)], DB, 256)
            ro = blocks(A["ret_w_out_2"])
            for j in range(4):
                load("ret_out", 0, j, ro[:, :, j * 256:(j + 1) * 256], 16, 256)
            ffn(1)
            for t in range(LT):
                sp.wait_ge(o_moved, t + 1)
                sp.dma_start(out[0, t * P:(t + 1) * P, :], o_tok[:, t, :]).then_inc(out_done, 16)
            sp.wait_ge(out_done, 16 * LT)

        @block.tensor
        def _(pe):
            def group(stage, it, j, k, n):
                s = loaded(pe, stage, it, j)
                begun[0] = True
                return wring[s][:, 0:k * n].rearrange("p (k n) -> p k n", k=k)

            begun = [False]

            def mm(o, lhsT, rhs, start, stop):
                ins = pe.matmul(o, lhsT, rhs, start=start, stop=stop)
                if begun[0]:
                    ins.then_inc(w_used, 1)
                    begun[0] = False
                return ins

            def block_ready(k, after):
                if after is not None:
                    pe.wait_ge(h_ready, after + k + 1)

            def linear(u, w, m, x, n, nk, rows=P, at=0, after=None):
                for k in range(nk):
                    block_ready(k, after)
                    if n == T:
                        for h in range(2):
                            last = mm(u[at:at + rows, h, 0:HALF], w[:, k, m:m + rows],
                                      x(k)[:, h * HALF:(h + 1) * HALF], k == 0, k == nk - 1)
                    else:
                        last = mm(u[at:at + rows, 0, 0:n], w[:, k, m:m + rows], x(k), k == 0, k == nk - 1)
                return last

            def square_sum(name, n):
                _, b0, nb = NORMS[name]
                for b in range(nb):
                    pe.wait_ge(n_sq, b0 + b + 1)
                    s = sq[:, (b0 + b) % 2]
                    if n == T:
                        for h in range(2):
                            last = pe.matmul(sc[:, 0, h, 0:HALF], ones, s[:, h * HALF:(h + 1) * HALF],
                                             start=b == 0, stop=b == nb - 1)
                    else:
                        last = pe.matmul(sc[:, 0, 0, 0:n], ones, s[:, 0:n], start=b == 0, stop=b == nb - 1)
                    last.then_inc(n_used, 1)

            def mean_sum(stage):
                for b in range(DB):
                    emptied(pe, stage, *divmod(b, UNITS[stage]))
                    last = pe.matmul(sc[:, 0, 1, :], ones, xT[:, b, CTX:T], start=b == 0, stop=b == DB - 1)
                last.then_inc(n_mean, 1)

            seq_h = lambda k: hT[:, k, CTX:T]
            all_h = lambda k: hT[:, k, :]

            pe.wait_ge(const_in, consts)
            for t in range(VEC_TILES):
                n = vec_rows[t]
                last = pe.transpose(flat(acc[:, 0])[:, t * P:t * P + n], vrow[0:n, t, :], ident[0:n, 0:n])
            last.then_inc(vec_turned, 1)
            pe.wait_ge(x_in, 32)
            for b in range(DB):
                if b >= 2:
                    pe.wait_ge(x_moved, b - 1)
                for t in range(QT):
                    last = pe.transpose(flat(sc[:, b % 2])[:, t * P:(t + 1) * P],
                                        x_tok[:, t, b * P:(b + 1) * P], ident)
                last.then_inc(x_turned, 1)
            square_sum("h0", T)
            pe.wait_ge(c_ready, 1)

            for j in range(4):
                w = group("ada", 0, j, DB, 512)
                for k in range(DB):
                    last = mm(acc[0:2, j // 2, j % 2, :], cs[:, k, 0:2], w[:, k, :], k == 0, k == DB - 1)
                last.then_inc(ada_ready, 1)
            for j in range(4):
                pe.wait_ge(ada_moved, j + 1)
                for m in range(4):
                    c = MOD_AT + (4 * j + m) * 2
                    last = pe.transpose(mod_psum[:, c:c + 2], ada_row[0:2, j, m * P:(m + 1) * P], ident[0:2, 0:2])
            last.then_inc(ada_done, 1)

            def modulation(w, m, o, x):
                for k in range(DB):
                    last = mm(o, w[:, k, m * P:(m + 1) * P], x(k), k == 0, k == DB - 1)
                return last

            def mod_sum(phase, it, i, nv):
                pe.wait_ge(mod_used[mod_slot(i, MOD_Q - 1)], piece(phase, it, i) + 1)
                for v in range(nv):
                    last = pe.matmul(mod_psum[:, bass.ds(it * (MOD_IT * nv) + (MOD_AT + i * nv + v), 1)],
                                     mod_acc[:, i % 2, v, :], ones[:, 0:1], start=True, stop=True)
                last.then_inc(mod_summed, 1)

            def down(stage, n, h, nk, phase=None, nv=1):
                with pe.Fori(0, 4) as it:
                    for j in range(2):
                        w = group(stage, it, j, nk, P)
                        claim(pe, stage, it, j)
                        for k in range(nk):
                            if n == T:
                                for s in range(2):
                                    last = mm(unit(stage, j)[:, s, 0:HALF], w[:, k, :], h(k)[:, s * HALF:(s + 1) * HALF],
                                              k == 0, k == nk - 1)
                            else:
                                last = mm(unit(stage, j)[:, 0, 0:n], w[:, k, :], h(k), k == 0, k == nk - 1)
                            ahead, rest = divmod(nk - 1 - k, nk // (MOD_UNIT + 1))
                            if phase is not None and rest == 0 and ahead < MOD_UNIT:
                                mod_sum(phase, it, (j + 1) * MOD_UNIT - 1 - ahead, nv)
                        last.then_inc(acc_ready, 1)

            w = group("mla_in", 0, 0, DB, Q_RANK)
            for j in range(6):
                if j == 3:
                    w = group("mla_in", 0, 1, DB, KV_RANK + ROPE)
                claim(pe, "mla_in", 0, j)
                linear(unit("mla_in", j), w, (j % 3) * P, all_h, T, DB,
                       rows=P if j < 5 else ROPE, after=0 if j == 0 else None).then_inc(acc_ready, 1)
            emptied(pe, "mla_in", 0, 5)
            pe.wait_ge(tab_in, 16)
            claim(pe, "mla_rope", 0, 0)
            for h in range(2):
                last = pe.matmul(unit("mla_rope", 0)[:, h, 0:HALF], dup, kraw[0:64, h * HALF:(h + 1) * HALF],
                                 start=True, stop=True)
            last.then_inc(acc_ready, 1)
            claim(pe, "mla_rope", 0, 1)
            pe.matmul(unit("mla_rope", 1)[:, 0, :], rotdup, kraw[0:64, CTX:T], start=True,
                      stop=True).then_inc(acc_ready, 1)
            square_sum("cq", T)
            square_sum("ckv", T)
            pe.wait_ge(lat_ready, 5)
            pe.wait_ge(krope_ready, 2)
            S = "mla_pair"
            columns = [None]
            with pe.Fori(0, MLA_H // 2) as it:
                wq = group(S, it, 0, 3, 384)
                for j, m in ((0, 0), (1, 192)):
                    claim(pe, S, it, j)
                    linear(unit(S, j), wq, m, lambda k: cq[:, k, :], T, 3).then_inc(acc_ready, 1)
                claim(pe, S, it, 2)
                linear(unit(S, 2), wq, 128, lambda k: cq[:, k, :], T, 3, rows=64)
                linear(unit(S, 2), wq, 320, lambda k: cq[:, k, :], T, 3, rows=64, at=64).then_inc(acc_ready, 1)
                wkv = group(S, it, 1, 2, 512)
                for j, m in ((3, 0), (4, 256)):
                    claim(pe, S, it, j)
                    linear(unit(S, j), wkv, m, lambda k: ckv[:, k, :], T, 2).then_inc(acc_ready, 1)
                wv = wkv.rearrange("p k (h s n) -> p k h s n", h=2, s=2)
                for j in range(3):
                    claim(pe, S, it, 5 + j)
                    for i in range(2):
                        t = 2 * j + i
                        for k in range(2):
                            last = mm(unit(S, 5 + j)[:, i, 0:256], ckv[:, k, t * P:(t + 1) * P],
                                      wv[:, k, :, 1, :], k == 0, k == 1)
                    last.then_inc(acc_ready, 1)
                emptied(pe, S, it, 2)
                for j in range(2):
                    claim(pe, S, it, 8 + j)
                    pe.matmul(unit(S, 8 + j)[:, 0, 0:256], rot2, qraw[:, CTX + 256 * j:CTX + 256 * (j + 1)],
                              start=True, stop=True).then_inc(acc_ready, 1)
                pe.wait_ge(qrope_ready, it * 1 + 1)

                def scores(n):
                    e, t = n // QT, n % QT
                    spans = [(0, 0, CTX)] if t < 2 else [(h, h * HALF, HALF) for h in range(2)]
                    for h, k0, w in spans:
                        pe.matmul(sc[:, n % 2, h, 0:w], qn[:, e, t * P:(t + 1) * P], kn[:, e, k0:k0 + w],
                                  start=True, stop=False)
                        last = pe.matmul(sc[:, n % 2, h, 0:w], qr[:, t * P:(t + 1) * P], krope[:, e, k0:k0 + w],
                                         start=False, stop=True)
                    last.then_inc(s_ready, 1)

                def weigh(n):
                    e, t = n // QT, n % QT
                    nk = 2 if t < 2 else KT
                    pe.wait_ge(p_ready, it * 12 + n + 1)
                    claim(pe, S, it, 10 + 2 * n)
                    for k in range(nk):
                        last = pe.transpose(flat(unit(S, 10 + 2 * n))[:, k * P:(k + 1) * P],
                                            prob[:, n % 2, k * P:(k + 1) * P], ident)
                    last.then_inc(acc_ready, 1)
                    claim(pe, S, it, 11 + 2 * n)
                    if n < 8:
                        if n % 4 == 0:
                            columns[0] = group(S, it, 2 + n // 4, DB, 512)
                        modulation(columns[0], n % 4, unit(S, 11 + 2 * n)[:, 1, 0:2], lambda k: cs[:, k, 0:2])
                    elif n < 10:
                        columns[0] = group(S, it, 4 + n - 8, DB, P)
                        modulation(columns[0], 0, unit(S, 11 + 2 * n)[:, 1, 0:1], lambda k: vec("c_2", k, 1))
                    emptied(pe, S, it, 10 + 2 * n)
                    for k in range(nk):
                        last = pe.matmul(unit(S, 11 + 2 * n)[:, 0, 0:P], vtok[:, k, e * P:(e + 1) * P],
                                         probT[:, n % 2, k * P:(k + 1) * P], start=k == 0, stop=k == nk - 1)
                    last.then_inc(acc_ready, 1)

                scores(0)
                for n in range(2 * QT):
                    if n + 1 < 2 * QT:
                        scores(n + 1)
                    weigh(n)

            def out_proj(stage, x, n, nk, per):
                for j in range(8):
                    if j % per == 0:
                        w = group(stage, 0, j // per, nk, per * P)
                    claim(pe, stage, 0, j)
                    linear(unit(stage, j), w, (j % per) * P, x, n, nk).then_inc(acc_ready, 1)

            emptied(pe, "mla_pair", 3, 33)
            out_proj("mla_out", lambda k: attn[:, k, :], T, DB, 4)

            def split_group(stage, it, j, k, n):
                g = GROUP0[stage] + j
                pe.wait_ge(w_split, half_group(stage, it, j, 0))
                begun[0] = True
                return parts(g % 2, k, n)

            def second_half(stage, it, j):
                pe.wait_ge(w_split, half_group(stage, it, j, 1))

            def split_product(u, w, m, k, x, start, stop):
                for h, n, hi, lo in x:
                    for i, (a, b) in enumerate(((0, hi), (0, lo), (1, hi))):
                        last = mm(u[:, h, 0:n], w[a][:, k, m:m + P], b, start and i == 0, stop and i == 2)
                return last

            def input_split(k, before):
                pe.wait_ge(x_split, before + k + 1)

            def mlp(i, n):
                S = f"mlp{i}"
                if n == T:
                    spans = [(h, HALF, slice(h * HALF, (h + 1) * HALF)) for h in range(2)]
                else:
                    spans = [(0, n, slice(0, n))]
                with pe.Fori(0, 4) as it:
                    for u in range(16):
                        if u % 2 == 0:
                            w = split_group(S, it, u // 2, DB, 256)
                        claim(pe, S, it, u)
                        for k in range(DB):
                            if u == 0:
                                input_split(k, DB * i)
                            if u % 2 == 0 and k == DB // 2:
                                second_half(S, it, u // 2)
                            if u == 8:
                                pe.wait_ge(relu_free, it * DB + (4 * DB * i + k + 3))
                            x = x_parts(n, k) if u < 8 else [(h, w_, hid_hi[:, k, t], hid_lo[:, k, t]) for h, w_, t in spans]
                            last = split_product(unit(S, u), w, (u % 2) * P, k, x, k == 0, k == DB - 1)
                        last.then_inc(acc_ready, 1)
                        if u % 2 and u // 2 in MOD_BESIDE:
                            mod_sum(i, it, MOD_BESIDE[u // 2][0], 2 - i)
                        if u % 2 == 0 and u // 2 - 1 in MOD_BESIDE:
                            mod_sum(i, it, MOD_BESIDE[u // 2 - 1][1], 2 - i)
                    mod_sum(i, it, MOD_BESIDE[7][1], 2 - i)

            square_sum("y0", T)
            square_sum("h0m", T)
            pe.wait_ge(mod_ready, 2)
            mlp(0, T)
            square_sum("y0m", T)

            square_sum("h1", T)
            pe.wait_ge(gate1_in, 16 * 2)
            for d in range(2):
                claim(pe, "gla_gate", 0, d)
                linear(unit("gla_gate", d), gate1[:, :, d, :], 0, all_h, T, DB,
                       rows=GATE_RANK, after=16 if d == 0 else None).then_inc(acc_ready, 1)
            emptied(pe, "gla_gate", 0, 1)
            S = "gla_head"
            with pe.Fori(0, GLA_H) as it:
                pe.wait_ge(gate2_in, it * 16 + 16)
                for d in range(2):
                    claim(pe, S, it, d)
                    for h in range(2):
                        last = pe.matmul(unit(S, d)[:, h, 0:HALF], gate2[:, d, :],
                                         hgate[0:GATE_RANK, d, h * HALF:(h + 1) * HALF], start=True, stop=True)
                    last.then_inc(acc_ready, 1)
                w = group(S, it, 0, DB, P)
                claim(pe, S, it, 2)
                linear(unit(S, 2), w, 0, seq_h, SEQ, DB).then_inc(acc_ready, 1)
                w = group(S, it, 1, DB, P)
                claim(pe, S, it, 3)
                linear(unit(S, 3), w, 0, all_h, T, DB).then_inc(acc_ready, 1)
                w = group(S, it, 2, DB, GLA_DV)
                for j in range(3):
                    claim(pe, S, it, 4 + j)
                    for i in range(2):
                        t = 2 * j + i
                        for k in range(DB):
                            last = mm(unit(S, 4 + j)[:, i, 0:GLA_DV], hT[:, k, t * P:(t + 1) * P], w[:, k, :],
                                      k == 0, k == DB - 1)
                    last.then_inc(acc_ready, 1)
                order = ([0, 1, 2, 3, 4], [1, 0, 5, 4, 3])
                for d in range(2):
                    pe.wait_ge(gk_ready, it * 2 + d + 1)
                    claim(pe, S, it, 7 + d)
                    for i, t in enumerate(order[d]):
                        last = pe.transpose(flat(unit(S, 7 + d))[:, i * P:(i + 1) * P],
                                            g_kE[:, d, t * P:(t + 1) * P], ident)
                    last.then_inc(acc_ready, 1)
                claim(pe, S, it, 9)
                for d in range(2):
                    u = unit(S, 9)[:, d, :]
                    for t in range(LT):
                        a, b = t * P, t * P + 64
                        pe.matmul(u[:, a:a + P], g_kt[:, d, a:a + P], g_qt[:, d, a:a + P], start=True, stop=True)
                        src, dst = (a, b) if d == 0 else (b, a)
                        last = pe.matmul(u[64 * d:64 * d + 64, dst:dst + 64], g_ke[:, d, CTX + src:CTX + src + 64],
                                         g_qt[:, d, dst:dst + 64], start=True, stop=True)
                last.then_inc(acc_ready, 1)
                for d in range(2):
                    emptied(pe, S, it, 7 + d)
                    if d == 0:
                        emptied(pe, S, it, 6)
                    for i, t in enumerate(order[d]):
                        if i in (0, 4):
                            claim(pe, S, it, 10 + 2 * d + i // 4)
                        u = unit(S, 10 + 2 * d + i // 4)
                        last = pe.matmul(u[:, (i % 4) // 2, (i % 2) * 256:(i % 2) * 256 + 256],
                                         g_kEt[:, d, i * P:(i + 1) * P], g_v[:, t, :], start=True, stop=True)
                        if i in (3, 4):
                            last.then_inc(acc_ready, 1)
                w = group(S, it, 3, DB, GLA_DV)
                for b in range(2):
                    for k in range(DB):
                        last = mm(sc[:, 0, b, :], w[:, k, b * P:(b + 1) * P], seq_h(k), k == 0, k == DB - 1)
                last.then_inc(gr_ready, 1)
                emptied(pe, S, it, 13)
                for b in range(2):
                    claim(pe, S, it, 14 + b)
                    for t in range(LT):
                        o = unit(S, 14 + b)[:, 0, t * P:(t + 1) * P]
                        v = slice(b * P, (b + 1) * P)
                        tok = slice(t * P, (t + 1) * P)
                        pe.matmul(o, g_v[:, 2 + t, v], g_AT[:, 0, tok], start=True, stop=False)
                        pe.matmul(o, g_v[:, 2 + t, v], g_AT[:, 1, tok], start=False, stop=False)
                        pe.matmul(o, g_S[:, 0, 1 + t, v], g_qS[:, 0, tok], start=False, stop=False)
                        last = pe.matmul(o, g_S[:, 1, 4 - t, v], g_qS[:, 1, tok], start=False, stop=True)
                    last.then_inc(acc_ready, 1)
                pe.wait_ge(gsq_ready, it * 1 + 1)
                for b in range(2):
                    last = pe.matmul(sc[:, 1, 0, :], ones, sq[:, b, 0:SEQ], start=b == 0, stop=b == 1)
                last.then_inc(gss_ready, 1)
            pe.wait_ge(g_done, GLA_H + 1)
            out_proj("gla_out", lambda k: g_out[:, k, :], SEQ, DB, 4)
            square_sum("y1", SEQ)
            square_sum("h1m", SEQ)
            mlp(1, SEQ)
            square_sum("y1m", SEQ)

            pe.wait_ge(ab_in, 48)
            for j in range(2):
                claim(pe, "gdn_gate", 0, j)
                linear(unit("gdn_gate", j), w_ab, 8 * j, seq_h, SEQ, DB, rows=GDN_H,
                       after=32 if j == 0 else None).then_inc(acc_ready, 1)

            def project(o, w, parts):
                for i in parts:
                    e, k = divmod(i, DB)
                    last = mm(o[:, e, :], w[:, k, e * P:(e + 1) * P], seq_h(k), k == 0, k == DB - 1)
                if 2 * DB - 1 in parts:
                    last.then_inc(qk_ready, 1)

            every = range(2 * DB)
            w = group("gdn_gate", 0, 0, DB, 256)
            project(sc[:, 0], w, every)
            pe.wait_ge(tab_in, 48)
            pe.wait_ge(d_rows, 2)
            for r in range(2):
                for c in range(LT):
                    last = pe.transpose(sc[:, 1, 0, (r * LT + c) * 8:(r * LT + c) * 8 + 8],
                                        d_row[:, r, c * P:(c + 1) * P], ident[0:GDN_H, 0:GDN_H])
            last.then_inc(d_cols, 1)
            pe.wait_ge(d_gc, 1)
            pe.matmul(sc[:, 1, 1, 0:32], last_row, d_col[:, 1].rearrange("p c h -> p (c h)"), start=True,
                      stop=True).then_inc(d_cols, 1)
            pe.wait_ge(d_glr, 1)
            w = group("gdn_gate", 0, 1, DB, 256)
            project(sc[:, 1], w, every)
            S = "gdn_pair"
            tiles = [(e, c) for e in range(2) for c in range(LT)]

            def gdn_pair(it, final):
                w = group(S, it, 0, DB, 256)
                claim(pe, S, it, 0)
                for e in range(2):
                    for k in range(DB):
                        last = mm(unit(S, 0)[:, e, :], w[:, k, e * P:(e + 1) * P], seq_h(k), k == 0, k == DB - 1)
                last.then_inc(acc_ready, 1)
                for r, x in enumerate((sq[0:GDN_H, :, 0:SEQ], d_ET[0:GDN_H])):
                    pe.wait_ge(d_masked, it * 2 + r + 1)
                    claim(pe, S, it, 1 + r)
                    for e in range(2):
                        last = pe.matmul(unit(S, 1 + r)[:, e, :], ones[0:GDN_H, :], x[:, e, :], start=True, stop=True)
                    last.then_inc(acc_ready, 1)
                w = group(S, it, 1, DB, 256)
                for r in range(2):
                    claim(pe, S, it, 3 + 2 * r)
                    linear(unit(S, 3 + 2 * r), w, r * P, seq_h, SEQ, DB).then_inc(acc_ready, 1)
                    pe.wait_ge(d_sq, it * 3 + r + 1)
                    claim(pe, S, it, 4 + 2 * r)
                    for e in range(2):
                        last = pe.matmul(unit(S, 4 + 2 * r)[:, e, :], ones, sq[:, e, 0:SEQ], start=True, stop=True)
                    last.then_inc(acc_ready, 1)

                def products(j, left, right):
                    claim(pe, S, it, j)
                    for e, c in tiles:
                        t = slice(c * P, (c + 1) * P)
                        last = pe.matmul(unit(S, j)[:, e, t], left[:, e, t], right[:, e, t], start=True, stop=True)
                    last.then_inc(acc_ready, 1)

                pe.wait_ge(d_norm, it * 2 + 2)
                products(7, d_k, d_k)
                products(8, d_k, d_q)
                for j, x in ((9, d_k), (10, d_v)):
                    if j == 10:
                        pe.wait_ge(d_silu, it * 3 + 3)
                    claim(pe, S, it, j)
                    for e, c in tiles:
                        t = slice(c * P, (c + 1) * P)
                        last = pe.transpose(unit(S, j)[:, e, t], x[:, e, t], ident)
                    last.then_inc(acc_ready, 1)
                pe.wait_ge(d_init, it * 1 + 1)
                for l in range(7):
                    j = 11 + 3 * l
                    pe.wait_ge(d_lm, it * 7 + l + 1)
                    if l:
                        emptied(pe, S, it, j - 2)
                    products(j, d_Lm[:, l % 2], d_T)
                    emptied(pe, S, it, j)
                    if l:
                        emptied(pe, S, it, j - 1)
                    if l < 6:
                        products(j + 1, d_U, d_Y)
                    products(j + 2 if l < 6 else j + 1, d_Y, d_U)
                emptied(pe, S, it, 30)
                pe.wait_ge(d_qe, it * 1 + 1)
                for c in range(LT):
                    t, j = slice(c * P, (c + 1) * P), 31 + 4 * c
                    ahead = [range(0)] * 3
                    if not final:
                        if c % 2 == 0:
                            w = group(S, it, 2 + c // 2, DB, 256)
                            pe.wait_ge(qk_moved, it * 2 + (c // 2 + 1))
                        n = DB * (c % 2)
                        ahead = range(n, n + 3), range(n + 3, n + 6), range(n + 6, n + 8)
                    if c:
                        emptied(pe, S, it, j - 1)
                    claim(pe, S, it, j)
                    for e in range(2):
                        last = pe.matmul(unit(S, j)[:, e, 0:P], d_k[:, e, t], d_S[:, e, :], start=True, stop=True)
                    last.then_inc(acc_ready, 1)
                    project(sc[:, c // 2], w, ahead[0])
                    pe.wait_ge(d_rr, it * LT + c + 1)
                    claim(pe, S, it, j + 1)
                    for e in range(2):
                        last = pe.matmul(unit(S, j + 1)[:, e, 0:P], d_U[:, e, t], d_r[:, e, :], start=True, stop=True)
                    last.then_inc(acc_ready, 1)
                    project(sc[:, c // 2], w, ahead[1])
                    claim(pe, S, it, j + 2)
                    for e in range(2):
                        pe.matmul(unit(S, j + 2)[:, e, 0:P], d_S[:, e, :], d_qE[:, e, t], start=True, stop=False)
                        if e == 0:
                            emptied(pe, S, it, j + 1)
                        last = pe.matmul(unit(S, j + 2)[:, e, 0:P], d_vn[:, e, :], d_QK[:, e, t], start=False, stop=True)
                    last.then_inc(acc_ready, 1)
                    claim(pe, S, it, j + 3)
                    for e in range(2):
                        last = pe.matmul(unit(S, j + 3)[:, e, 0:P], d_kend[:, e, t], d_vn[:, e, :], start=True, stop=True)
                    last.then_inc(acc_ready, 1)
                    project(sc[:, c // 2], w, ahead[2])
                pe.wait_ge(d_sq, it * 3 + 3)
                claim(pe, S, it, 47)
                for e in range(2):
                    last = pe.matmul(unit(S, 47)[:, e, :], ones, sq[:, e, 0:SEQ], start=True, stop=True)
                last.then_inc(acc_ready, 1)

            with pe.Fori(0, GDN_H // 2 - 1) as it:
                gdn_pair(it, False)
            gdn_pair(GDN_H // 2 - 1, True)
            pe.wait_ge(d_done, GDN_H // 2 + 1)
            out_proj("gdn_out", lambda k: d_out[:, k, :], SEQ, DB, 4)

            def ffn(i):
                up = f"ffn{i}_up"
                with pe.Fori(0, HIDB // 2) as it:
                    for j in range(2):
                        w = split_group(up, it, j, DB, 256)
                        claim(pe, up, it, j)
                        for b in range(2):
                            for k in range(DB):
                                if b == 0 and k == DB // 2:
                                    second_half(up, it, j)
                                if j == b == 0:
                                    input_split(k, DB * (2 + 2 * i))
                                last = split_product(unit(up, j)[:, b:b + 1], w, b * P, k, x_parts(SEQ, k), k == 0, k == DB - 1)
                        last.then_inc(acc_ready, 1)
                emptied(pe, up, HIDB // 2 - 1, 1)
                down(f"ffn{i}_down", SEQ, lambda k: hid2[:, k, :], HIDB, 2 if i == 0 else None)

            mean_sum("gdn_out")
            square_sum("ln0", SEQ)
            ffn(0)
            mean_sum("ffn0_down")
            square_sum("ln0f", SEQ)

            S = "ret_head"
            with pe.Fori(0, RET_H) as it:
                def columns_of(j, u, first=False):
                    w = split_group(S, it, j, DB, 256)
                    claim(pe, S, it, u)
                    for b in range(2):
                        for k in range(DB):
                            if b == 0 and k == DB // 2:
                                second_half(S, it, j)
                            if first and b == 0:
                                input_split(k, DB * 3)
                            last = split_product(unit(S, u)[:, b:b + 1], w, b * P, k, x_parts(SEQ, k), k == 0, k == DB - 1)
                    last.then_inc(acc_ready, 1)

                columns_of(0, 0, True)
                columns_of(1, 1)
                for g in range(2):
                    w = split_group(S, it, 2 + g, DB, 256)
                    for t in range(LT):
                        j, i = divmod(t, 2)
                        if g == i == 0:
                            claim(pe, S, it, 2 + j)
                        o = unit(S, 2 + j)[:, i, g * 256:(g + 1) * 256]
                        tok = slice(t * P, (t + 1) * P)
                        for k in range(DB):
                            if t == 0 and k == DB // 2:
                                second_half(S, it, 2 + g)
                            hi, lo = x_hi_seq[:, k, tok], x_lo[:, k, CTX + t * P:CTX + (t + 1) * P]
                            for n, (x, a) in enumerate(((hi, 0), (lo, 0), (hi, 1))):
                                last = mm(o, x, w[a][:, k, :], k == n == 0, k == DB - 1 and n == 2)
                        if g == i == 1:
                            last.then_inc(acc_ready, 1)
                columns_of(4, 4)
                columns_of(5, 5)
                pe.wait_ge(r_rotd, it * 2 + 2)
                for j in range(2):
                    claim(pe, S, it, 6 + j)
                    for i in range(2):
                        t = (2 * j + i) * P
                        for b in range(2):
                            last = pe.matmul(unit(S, 6 + j)[:, i, 0:SEQ - t], r_rot[:, 1, b, t:t + P],
                                             r_rot[:, 0, b, t:SEQ], start=b == 0, stop=b == 1)
                    last.then_inc(acc_ready, 1)
                emptied(pe, S, it, 6)
                emptied(pe, S, it, 7)
                for j in range(2):
                    claim(pe, S, it, 8 + j)
                    for i in range(2):
                        m = (2 * j + i) * P
                        for t in range(LT):
                            last = pe.matmul(unit(S, 8 + j)[:, i, t * P:SEQ], r_v[:, t, m // CTX, m % CTX:m % CTX + P],
                                             r_s[:, t, 0:SEQ - t * P], start=t == 0, stop=t == LT - 1)
                    last.then_inc(acc_ready, 1)
                emptied(pe, S, it, 8)
                emptied(pe, S, it, 9)
                claim(pe, S, it, 10)
                for b in range(4):
                    last = pe.matmul(unit(S, 10)[:, 0, :], ones, r_o[:, b, :], start=b == 0, stop=b == 3)
                last.then_inc(acc_ready, 1)
                claim(pe, S, it, 11)
                for b in range(4):
                    pe.wait_ge(r_sq, it * 4 + b + 1)
                    last = pe.matmul(unit(S, 11)[:, 0, :], ones, r_sqr[:, b, :], start=b == 0, stop=b == 3)
                last.then_inc(acc_ready, 1)
            pe.wait_ge(r_done, RET_H + 1)
            out_proj("ret_out", lambda k: r_out[:, k, :], SEQ, 16, 2)
            mean_sum("ret_out")
            square_sum("ln1", SEQ)
            ffn(1)
            mean_sum("ffn1_down")
            square_sum("ln1f", SEQ)
            pe.wait_ge(x_ready, 64)
            for t in range(LT):
                if t >= 2:
                    pe.wait_ge(o_moved, t - 1)
                for b in range(DB):
                    last = pe.transpose(flat(sc[:, t % 2])[:, b * P:(b + 1) * P],
                                        xT[:, b, CTX + t * P:CTX + (t + 1) * P], ident)
                last.then_inc(o_turned, 1)

        @block.scalar
        def _(act):
            st = Steps(act, act_step)
            f = act.activation

            def squares(name, src, n, ready=None):
                _, b0, nb = NORMS[name]
                for b in range(nb):
                    if ready is not None:
                        ready(b)
                    if b0 + b >= 2:
                        act.wait_ge(n_used, b0 + b - 1)
                    f(sq[:, (b0 + b) % 2, 0:n], src(b), ACT.Square).then_inc(n_sq, 1)

            def deviation(name, n, width, e=0):
                k, b0, nb = NORMS[name]
                act.wait_ge(n_used, b0 + nb)
                i, o = (sc[:, 0, :, 0:HALF], halves(rstd)) if n == T else (sc[:, 0, 0, 0:n], rstd[:, 0:n])
                st.did(f(o, i, ACT.Ln, scale=1.0 / width, bias=eps[:, e:e + 1]))
                st.settle()
                f(o, o, ACT.Exp, scale=-0.5).then_inc(n_std, 1)

            def high_input(n, b, h0):
                act.wait_ge(h_ready, h0 + b + 1)
                f(x_hi[:, b, :] if n == T else x_hi_seq[:, b, :], hT[:, b, T - n:T], ACT.Copy).then_inc(x_high, 1)

            def affine(l, q, n, mul0, split=False):
                for b in range(DB):
                    act.wait_ge(n_mul, mul0 + b + 1)
                    if n == T:
                        f(hT[:, b, 0:CTX], hT[:, b, 0:CTX], ACT.Identity, scale=dcol[:, l, q, b, 1:2],
                          bias=mod[:, l, 24 * (q // 2) + b, 1:2])
                    f(hT[:, b, CTX:T], hT[:, b, CTX:T], ACT.Identity, scale=dcol[:, l, q, b, 0:1],
                      bias=mod[:, l, 24 * (q // 2) + b, 0:1]).then_inc(h_ready, 1)
                    if split:
                        high_input(n, b, mul0)

            def modulate(l, q, x0):
                for b in range(DB):
                    act.wait_ge(x_ready, x0 + b + 1)
                    f(hT[:, b, CTX:T], xT[:, b, CTX:T], ACT.Identity, scale=dcol[:, l, q, b, 0:1],
                      bias=mod[:, l, 24 * (q // 2) + b, 0:1]).then_inc(h_ready, 1)

            def modulate_normed(i, mul0, h0):
                for b in range(DB):
                    act.wait_ge(n_mul, mul0 + b + 1)
                    f(hT[:, b, CTX:T], xT[:, b, CTX:T], ACT.Identity, scale=ln_col[:, i, 0, b:b + 1],
                      bias=ln_col[:, i, 1, b:b + 1]).then_inc(h_ready, 1)
                    high_input(SEQ, b, h0)

            def layer_norm_out(l, i, mul0):
                for b in range(DB):
                    act.wait_ge(n_mul, mul0 + b + 1)
                    f(xT[:, b, CTX:T], xT[:, b, CTX:T], ACT.Identity, scale=col("ln_g_2", (2 * l + i) * DB + b),
                      bias=col("ln_b_2", (2 * l + i) * DB + b)).then_inc(x_ready, 1)

            def x_at(b0, seq=False):
                return lambda b: act.wait_ge(x_ready, b0 + b + 1)

            def y_at(stage):
                return lambda b: emptied(act, stage, *divmod(b, UNITS[stage]))

            def const(dst, src, s):
                act.dma_start(dst, src).then_inc(s, 16)

            const(base_tab[:, :], A["tab_base"], const_in)
            for name, src in vec_sources:
                t, r, rows = VEC[name]
                const(vrow[r:r + rows, t, :], src, const_in)
            const(x_tok[:, 0:2, :], A["ctx"][0].rearrange("(t p) d -> p t d", p=P), x_in)
            const(x_tok[:, 2:QT, :], A["x"][0].rearrange("(t p) d -> p t d", p=P), x_in)
            const(tab[:, 0:1408], A["tab_mla"], tab_in)
            for d in range(2):
                const(gate1[:, :, d, :], A["gla_w_gate1"][0, d].rearrange("(k p) r -> p k r", p=P), gate1_in)
            const(w_ab[:, :, :], A["gdn_w_in_2"][:, 4 * D:4 * D + 16].rearrange("(k p) n -> p k n", p=P), ab_in)
            const(a_dt[:, 0:1], A["gdn_a_log_2"].rearrange("(h a) -> h a", a=1), ab_in)
            const(a_dt[:, 1:2], A["gdn_dt_bias_2"].rearrange("(h a) -> h a", a=1), ab_in)
            act.wait_ge(cols_ready, 1)
            f(cs[:, :, 0], vec("c", 0, DB), ACT.Silu)
            f(cs[:, :, 1], vec("c_ctx", 0, DB), ACT.Silu).then_inc(c_ready, 1)
            for b in range(DB):
                act.wait_ge(x_turned, b + 1)
                f(xT[:, b, :], flat(sc[:, b % 2])[:, 0:T], ACT.Copy).then_inc(x_moved, 1)
            act.wait_ge(relu_free, 2)
            act.wait_ge(x_moved, DB)
            squares("h0", lambda b: xT[:, b, :], T)
            deviation("h0", T, D)
            act.wait_ge(mod_ready, 1)
            affine(0, 0, T, 0)
            squares("cq", lambda b: cq[:, b, :], T, lambda b: emptied(act, "mla_in", 0, b))
            deviation("cq", T, Q_RANK)
            squares("ckv", lambda b: ckv[:, b, :], T, lambda b: emptied(act, "mla_in", 0, 3 + b))
            act.wait_ge(lat_ready, 3)
            deviation("ckv", T, KV_RANK)
            scale = (NOPE + ROPE) ** -0.5
            with act.Fori(0, MLA_H // 2) as it:
                for n in range(2 * QT):
                    act.wait_ge(p_max, it * 12 + n + 1)
                    if n % QT < 2:
                        i, o = sc[:, n % 2, 0, 0:CTX], prob[:, n % 2, 0:CTX]
                    else:
                        i, o = sc[:, n % 2, :, 0:HALF], halves(prob[:, n % 2, :])
                    f(o, i, ACT.Exp, bias=small[:, n % 2, 1:2], scale=scale,
                      accum_out=small[:, n % 2, 2:3]).then_inc(p_exp, 1)

            def high_weights(stage, it, j):
                s = loaded(act, stage, it, j)
                for h in range(2):
                    c = slice(h * 1024, (h + 1) * 1024)
                    f(w_hi[s][:, c], wring[s][:, c], ACT.Copy).then_inc(w_high, 1)

            def mlp(i, n):
                S = f"mlp{i}"

                def quarter(it, final):
                    for u in range(16):
                        if u % 2 == 0 and u < 14:
                            high_weights(S, it, u // 2 + 1)
                        elif u == 14 and not final:
                            high_weights(S, it + 1, 0)
                        if u < 8:
                            finished(act, S, it, u)
                            act.wait_ge(relu_free, it * 8 + (32 * i + u + 1))
                            r = relu[:, u % 2, 0:n]
                            if n == T:
                                free(f(halves(r), unit(S, u)[:, :, 0:HALF], ACT.Relu), S, u)
                            else:
                                free(f(r, unit(S, u)[:, 0, 0:n], ACT.Relu), S, u)
                            emptied(act, S, it, u)
                            f(r, r, ACT.Square).then_inc(hid_square, 1)
                            act.wait_ge(hid_square, it * 8 + (32 * i + u + 1))
                            f(hid_hi[:, u, 0:n], r, ACT.Copy).then_inc(hid_high, 1)

                with act.Fori(0, 3) as it:
                    quarter(it, False)
                quarter(3, True)

            emptied(act, "mla_pair", MLA_H // 2 - 1, 33)
            for k in range(DB):
                last = f(cs[:, k, 2:3], cs[:, k, 2:3], ACT.Silu, bias=col("cond_b", k))
            last.then_inc(e_ready, 1)
            y_all = lambda b: hT[:, b, :]
            y_seq = lambda b: hT[:, b, CTX:T]
            x_all = lambda b: xT[:, b, :]
            x_seq = lambda b: xT[:, b, CTX:T]
            squares("y0", y_all, T, y_at("mla_out"))
            deviation("y0", T, D)
            high_weights("mlp0", 0, 0)
            squares("h0m", x_all, T, x_at(0))
            deviation("h0m", T, D)
            act.wait_ge(mod_ready, 2)
            affine(0, 2, T, 8, True)
            mlp(0, T)
            squares("y0m", lambda b: y_mlp[:, b, :], T, lambda b: emptied(act, "mlp0", 3, 8 + b))
            act.wait_ge(mod_summed, 2 + MOD_CHUNKS)
            deviation("y0m", T, D)
            const(tab[:, 0:1024], A["tab_gla"], tab_in)

            squares("h1", x_all, T, x_at(8))
            deviation("h1", T, D)
            act.wait_ge(mod_ready, 3)
            affine(1, 0, T, 16)
            S = "gla_head"
            with act.Fori(0, GLA_H) as it:
                st.enter(it, 5)
                for d in range(2):
                    emptied(act, S, it, d)
                    st.did(f(g_l, g_z[:, d, :], ACT.Abs))
                    st.settle()
                    st.did(f(g_l, g_l, ACT.Exp, scale=-1.0))
                    st.settle()
                    f(g_l, g_l, ACT.Ln, bias=1.0).then_inc(gl_ready, 1)
                    finished(act, S, it, 2 + d)
                    if d == 0:
                        free(f(g_q, unit(S, 2)[:, 0, :], ACT.Copy, scale=P ** -0.5), S, 2)
                    else:
                        free(f(halves(g_k), unit(S, 3)[:, :, 0:HALF], ACT.Copy), S, 3)
                    act.wait_ge(gG_ready, it * 2 + d + 1)
                    f(g_qt[:, d, :], g_G[:, CTX:T], ACT.Exp, scale=1 / 16)
                    f(g_kt[:, d, :], g_G[:, CTX:T], ACT.Exp, scale=-1 / 16)
                    f(g_ke[:, d, :], g_z[:, d, :], ACT.Exp, scale=1 / 16)
                    f(g_et[:, d, :], g_tot[:, d, :], ACT.Exp, scale=1 / 16).then_inc(gE_ready, 1)
                for d in range(2):
                    finished(act, S, it, 7 + d)
                    free(f(g_kEt[:, d, :], flat(unit(S, 7 + d))[:, 0:5 * P], ACT.Copy), S, 7 + d)
                act.wait_ge(g_done, it * 1 + 1)
                act.wait_ge(gr_ready, it * 1 + 1)
                f(g_r, sc[:, 0], ACT.Silu)
                emptied(act, S, it, 14)
                emptied(act, S, it, 15)
                f(sq[:, :, 0:SEQ], g_o, ACT.Square).then_inc(gsq_ready, 1)
                act.wait_ge(gss_ready, it * 1 + 1)
                st.did(f(rstd[:, 0:SEQ], sc[:, 1, 0, :], ACT.Ln, scale=1.0 / GLA_DV, bias=eps[:, 0:1]))
                st.settle()
                f(rstd[:, 0:SEQ], rstd[:, 0:SEQ], ACT.Exp, scale=-0.5).then_inc(gdev_ready, 1)
            st.leave(GLA_H)
            squares("y1", y_seq, SEQ, y_at("gla_out"))
            deviation("y1", SEQ, D)
            high_weights("mlp1", 0, 0)
            squares("h1m", x_seq, SEQ, x_at(16))
            deviation("h1m", SEQ, D)
            affine(1, 2, SEQ, 24, True)
            mlp(1, SEQ)
            squares("y1m", lambda b: y_mlp[:, b, 0:SEQ], SEQ, lambda b: emptied(act, "mlp1", 3, 8 + b))
            act.wait_ge(mod_summed, 2 + 2 * MOD_CHUNKS)
            deviation("y1m", SEQ, D)
            const(tab[:, 0:1664], A["tab_gdn"], tab_in)

            act.wait_ge(mod_ready, 4)
            modulate(2, 0, 24)
            act.wait_ge(ab_in, 48)
            f(a_dt[:, 2:3], a_dt[:, 0:1], ACT.Exp).then_inc(d_ga, 1)
            finished(act, "gdn_gate", 0, 1)
            free(f(d_row[:, 0, :], unit("gdn_gate", 1)[0:GDN_H, 0, :], ACT.Sigmoid), "gdn_gate", 1)
            emptied(act, "gdn_gate", 0, 0)
            st.did(f(sq[0:GDN_H, 0, 0:SEQ], rstd[0:GDN_H, 0:SEQ], ACT.Abs))
            st.settle()
            st.did(f(sq[0:GDN_H, 0, 0:SEQ], sq[0:GDN_H, 0, 0:SEQ], ACT.Exp, scale=-1.0))
            st.settle()
            f(sq[0:GDN_H, 0, 0:SEQ], sq[0:GDN_H, 0, 0:SEQ], ACT.Ln, bias=1.0).then_inc(d_ga, 1)
            act.wait_ge(d_glr, 1)
            f(d_col[:, 2], d_col[:, 1], ACT.Exp)
            f(d_col[:, 4], d_col[:, 4], ACT.Exp)
            f(d_col[:, 3], d_col[:, 3], ACT.Exp).then_inc(d_ga, 1)
            S = "gdn_pair"
            with act.Fori(0, GDN_H // 2) as it:
                for j in range(3):
                    act.wait_ge(d_conv, it * 3 + max(2, j + 1))
                    if j < 2:
                        act.wait_ge(qk_ready, it * 2 + j + 1)
                        f(d_cp[:, j, :, 3:SEQ + 3], sc[:, j], ACT.Copy).then_inc(qk_moved, 1)
                    else:
                        finished(act, S, it, 0)
                        free(f(d_cp[:, 0, :, 3:SEQ + 3], unit(S, 0), ACT.Copy), S, 0)
                act.wait_ge(d_done, it * 1 + 1)
                for r, x in enumerate((d_gcR, d_bR)):
                    finished(act, S, it, 1 + r)
                    free(f(x, unit(S, 1 + r), ACT.Copy), S, 1 + r)
                for r, (x, y) in enumerate(((d_q, d_Y), (d_k, d_U))):
                    act.wait_ge(d_conv, it * 3 + r + 3)
                    f(x, x, ACT.Silu).then_inc(d_silu, 1)
                    act.wait_ge(d_silu, it * 3 + r + 1)
                    if r:
                        finished(act, S, it, 4)
                    f(sq[:, :, 0:SEQ], x, ACT.Square).then_inc(d_sq, 1)
                    finished(act, S, it, 3 + 2 * r)
                    free(f(d_z[:, r, :], unit(S, 3 + 2 * r)[:, 0, :], ACT.Silu), S, 3 + 2 * r)
                    finished(act, S, it, 4 + 2 * r)
                    free(f(y, unit(S, 4 + 2 * r), ACT.Ln, bias=eps[:, 0:1]), S, 4 + 2 * r)
                    emptied(act, S, it, 4 + 2 * r)
                    f(y, y, ACT.Exp, scale=-0.5).then_inc(d_len, 1)
                act.wait_ge(d_diff, it * 1 + 1)
                f(d_ET, d_ET, ACT.Exp).then_inc(d_exp, 1)
                act.wait_ge(d_conv, it * 3 + 5)
                f(d_v, d_v, ACT.Silu).then_inc(d_silu, 1)
                finished(act, S, it, 10)
                f(d_v, d_gcR, ACT.Exp).then_inc(d_exp, 1)
                for l in range(7):
                    finished(act, S, it, 11 + 3 * l)
                    free(f(d_Y, unit(S, 11 + 3 * l), ACT.Copy), S, 11 + 3 * l)
                for c in range(LT):
                    t, j = slice(c * P, (c + 1) * P), 31 + 4 * c
                    finished(act, S, it, j + 1)
                    free(f(d_vn, unit(S, j + 1)[:, :, 0:P], ACT.Copy), S, j + 1)
                    finished(act, S, it, j + 2)
                    free(f(d_o[:, :, t], unit(S, j + 2)[:, :, 0:P], ACT.Copy), S, j + 2)
                emptied(act, S, it, 45)
                f(sq[:, :, 0:SEQ], d_o, ACT.Square).then_inc(d_sq, 1)
                finished(act, S, it, 47)
                free(f(d_Y, unit(S, 47), ACT.Ln, scale=1.0 / P, bias=eps[:, 0:1]), S, 47)
                emptied(act, S, it, 47)
                f(d_Y, d_Y, ACT.Exp, scale=-0.5).then_inc(d_len, 1)

            def layer_norm(name, x0):
                squares(name, x_seq, SEQ, lambda b: act.wait_ge(n_cent, x0 - 32 + b + 1))
                deviation(name, SEQ, D, 1)

            def ffn(i):
                up = f"ffn{i}_up"

                def pair(it, final):
                    high_weights(up, it, 1)
                    finished(act, up, it, 0)
                    act.wait_ge(f_conv, it * 1 + (HIDB // 2 * i + i + 1))
                    free(f(gpad[:, :, 2:SEQ + 2], unit(up, 0), ACT.Copy), up, 0)
                    act.wait_ge(f_conv, it * 1 + (HIDB // 2 * i + i + 2))
                    f(gsilu, gconv, ACT.Silu).then_inc(f_silu, 1)
                    if not final:
                        high_weights(up, it + 1, 0)

                with act.Fori(0, HIDB // 2 - 1) as it:
                    pair(it, False)
                pair(HIDB // 2 - 1, True)

            high_weights("ffn0_up", 0, 0)
            layer_norm("ln0", 32)
            act.wait_ge(ln_cols, 1)
            modulate_normed(0, 32, 40)
            ffn(0)
            layer_norm_out(0, 0, 32)
            high_weights("ret_head", 0, 0)
            layer_norm("ln0f", 40)

            const(r_tab[:, :, :], A["tab_ret"].rearrange("p (a n) -> p a n", a=6), rtab_in)
            act.wait_ge(ln_cols, 3)
            modulate_normed(1, 40, 48)
            S = "ret_head"

            def ret_head(it, final):
                for i in range(2):
                    high_weights(S, it, 1 + i)
                    finished(act, S, it, i)
                    free(f(r_raw[:, i], unit(S, i), ACT.Copy, scale=(1.0, RET_DK ** -0.5)[i]), S, i)
                high_weights(S, it, 3)
                high_weights(S, it, 4)
                high_weights(S, it, 5)
                act.wait_ge(r_done, it * 1 + 1)
                for j in range(2):
                    finished(act, S, it, 4 + j)
                    free(f(r_gate[:, 2 * j:2 * j + 2], unit(S, 4 + j).rearrange("p e (a n) -> p e a n", a=2), ACT.Silu), S, 4 + j)
                    if j == 0 and not final:
                        high_weights(S, it + 1, 0)
                for b in range(4):
                    if b < 3:
                        act.wait_ge(r_cent, it * 3 + b + 1)
                    else:
                        emptied(act, S, it, 10)
                    f(r_sqr[:, b, :], r_o[:, b, :], ACT.Square).then_inc(r_sq, 1)
                finished(act, S, it, 11)
                free(f(rstd[:, 0:SEQ], unit(S, 11)[:, 0, :], ACT.Ln, scale=1.0 / RET_DV, bias=eps[:, 0:1]), S, 11)
                emptied(act, S, it, 11)
                f(rstd[:, 0:SEQ], rstd[:, 0:SEQ], ACT.Exp, scale=-0.5).then_inc(r_dev, 1)

            with act.Fori(0, RET_H - 1) as it:
                ret_head(it, False)
            ret_head(RET_H - 1, True)
            layer_norm_out(0, 1, 40)
            high_weights("ffn1_up", 0, 0)
            layer_norm("ln1", 48)
            modulate_normed(2, 48, 56)
            ffn(1)
            layer_norm_out(1, 0, 48)
            layer_norm("ln1f", 56)
            layer_norm_out(1, 1, 56)

        @block.vector
        def _(dve):
            st = Steps(dve, dve_step)
            tt, ts, stt, cp = dve.tensor_tensor, dve.tensor_scalar, dve.scalar_tensor_tensor, dve.tensor_copy
            MUL, ADD, SUB, MIN, MAX = ALU.mult, ALU.add, ALU.subtract, ALU.min, ALU.max

            def deviation_of(name):
                k, _, _ = NORMS[name]
                dve.wait_ge(n_std, k + 1)

            def over_deviation(out, n, x0=None):
                for b in range(DB):
                    tt(out[:, b, T - n:T], xT[:, b, T - n:T], rstd[:, 0:n], MUL).then_inc(n_mul, 1)
                    if x0 is not None and b >= 2:
                        low_input(n, b - 2, x0)
                if x0 is not None:
                    low_input(n, DB - 2, x0)
                    low_input(n, DB - 1, x0)

            def normed(name, n, x0=None):
                deviation_of(name)
                over_deviation(hT, n, x0)

            def residual(name, n, l, q, y):
                deviation_of(name)
                for b in range(DB):
                    st.did(tt(y[:, b], y[:, b], rstd[:, 0:n], MUL))
                st.settle()
                for b in range(DB):
                    if n == T:
                        stt(xT[:, b, 0:CTX], y[:, b, 0:CTX], dcol[:, l, q, b, 1:2], xT[:, b, 0:CTX], MUL, ADD)
                    stt(xT[:, b, CTX:T], y[:, b, n - SEQ:n], dcol[:, l, q, b, 0:1], xT[:, b, CTX:T],
                        MUL, ADD).then_inc(x_ready, 1)

            dve.memset(eps[:, 0:1], 1e-6).then_inc(relu_free, 1)
            dve.memset(eps[:, 1:2], 1e-5 / ALPHA ** 2).then_inc(relu_free, 1)
            dve.wait_ge(vec_turned, 1)
            for t in range(VEC_TILES):
                n = vec_rows[t]
                last = cp(cols[:, t, 0:n], flat(acc[:, 0])[:, t * P:t * P + n])
            last.then_inc(cols_ready, 1)
            dve.wait_ge(cols_ready, 1)

            def modulation(l, i0, i1, nv, src=None):
                if src is None:
                    src = mod_psum[:, MOD_AT:MOD_AT + 48 * nv].rearrange("p (i v) -> p i v", v=nv)
                o = src[:, i0 * DB:i1 * DB]
                for v in range(nv):
                    b = vec("ada_b" if l < 2 else "ada_b_2", 48 * (l % 2) + i0 * DB, (i1 - i0) * DB)
                    st.did(tt(mod[:, l, i0 * DB:i1 * DB, v], o[:, :, v], b, ADD))
                st.settle()
                for q, (m, plus) in enumerate(((1, 1.0), (2, 0.0), (4, 1.0), (5, 0.0))):
                    if not i0 <= m < i1:
                        continue
                    for v in range(nv):
                        src = mod[:, l, m * DB:(m + 1) * DB, v]
                        if l < 2:
                            last = stt(dcol[:, l, q, :, v], src, plus, vec("norm_g", (4 * l + q) * DB, DB), ADD, MUL)
                        else:
                            last = ts(dcol[:, l, q, :, v], src, 1.0, 1.0 if plus else 1.0 / ALPHA, ADD, MUL)
                last.then_inc(mod_ready, 1)
                norms = {2: [(0, 2)], 3: [(1, 0), (2, 2)]}.get(l, [])
                for i, q in norms:
                    dve.wait_ge(mod_ready, l + 2)
                    g, b = (vec(name, i * DB, DB) for name in ("ln_g_2", "ln_b_2"))
                    st.did(tt(ln_col[:, i, 0, :], g, dcol[:, l, q, :, 0], MUL))
                    st.did(tt(ln_col[:, i, 1, :], b, dcol[:, l, q, :, 0], MUL))
                    st.settle()
                    tt(ln_col[:, i, 1, :], ln_col[:, i, 1, :], mod[:, l, 12 * q:12 * q + DB, 0], ADD).then_inc(ln_cols, 1)

            def mod_chunk(phase, it, i, vs):
                dve.wait_ge(mod_summed, MOD_CHUNKS * phase + i + 1 + it * MOD_IT)
                for q in range(MOD_Q):
                    s = mod_slot(i, q)
                    dve.wait_ge(mod_loaded[s], piece(phase, it, i, 16))
                    for kk in range(MOD_K):
                        for j, v in enumerate(vs):
                            k = MOD_K * q + kk
                            a, w = mod_acc[:, i % 2, j, :], mod_w[s][:, kk, :]
                            if k == 0:
                                ins = ts(a, w, cs[:, k, v:v + 1], None, MUL)
                            else:
                                ins = stt(a, w, cs[:, k, v:v + 1], a, MUL, ADD)
                        if kk == MOD_K - 1:
                            ins.then_inc(mod_used[s], 1)
                            dve.wait_ge(mod_used[s], piece(phase, it, i) + 1)
                        else:
                            st.did(ins)
                            st.settle()

            normed("h0", T)
            dve.memset(krope[:, :, :], 0.0).then_inc(krope_ready, 1)
            dve.wait_ge(krope_ready, 1)
            for j in range(4):
                dve.wait_ge(ada_ready, j + 1)
                cp(ada_row[0:2, j, :], acc[0:2, j // 2, j % 2, :]).then_inc(ada_moved, 1)
            dve.wait_ge(ada_done, 1)
            modulation(0, 0, 2, 2)
            for j in range(5):
                finished(dve, "mla_in", 0, j)
                free(cp(halves(cq[:, j, :] if j < 3 else ckv[:, j - 3, :]), unit("mla_in", j)[:, :, 0:HALF]), "mla_in", j)
            finished(dve, "mla_in", 0, 5)
            free(cp(halves(kraw[0:64]), unit("mla_in", 5)[0:64, :, 0:HALF]), "mla_in", 5)
            finished(dve, "mla_rope", 0, 0)
            free(cp(halves(qraw), unit("mla_rope", 0)[:, :, 0:HALF]), "mla_rope", 0)
            finished(dve, "mla_rope", 0, 1)
            free(tt(ktmp, unit("mla_rope", 1)[:, 0, :], rsin, MUL), "mla_rope", 1)
            emptied(dve, "mla_rope", 0, 0)
            emptied(dve, "mla_rope", 0, 1)
            st.did(tt(qr[:, CTX:T], qraw[:, CTX:T], rcos, MUL))
            st.settle()
            for e in range(2):
                h = slice(64 * e, 64 * e + 64)
                cp(krope[h, e, 0:CTX], qraw[h, 0:CTX])
                last = tt(krope[h, e, CTX:T], qr[h, CTX:T], ktmp[h, :], ADD)
            last.then_inc(krope_ready, 1)
            for name, x, nb, g in (("cq", cq, 3, "mla_g_q"), ("ckv", ckv, 2, "mla_g_kv")):
                deviation_of(name)
                for b in range(nb):
                    stt(x[:, b, :], x[:, b, :], col(g, b), rstd[:, :], MUL, MUL).then_inc(lat_ready, 1)
            S = "mla_pair"
            scale = (NOPE + ROPE) ** -0.5
            with dve.Fori(0, MLA_H // 2) as it:
                st.enter(it, 1 + 12 * 2)
                for j, o in ((0, qn[:, 0]), (1, qn[:, 1]), (2, qraw), (3, kn[:, 0]), (4, kn[:, 1])):
                    finished(dve, S, it, j)
                    free(cp(halves(o), unit(S, j)[:, :, 0:HALF]), S, j)
                for j in range(3):
                    finished(dve, S, it, 5 + j)
                    free(cp(vtok[:, 2 * j:2 * j + 2, :], unit(S, 5 + j)[:, :, 0:256]), S, 5 + j)
                emptied(dve, S, it, 2)
                cp(qr[:, 0:CTX], qraw[:, 0:CTX])
                st.did(tt(qr[:, CTX:T], qraw[:, CTX:T], rcos, MUL))
                for j in range(2):
                    finished(dve, S, it, 8 + j)
                    free(tt(ktmp[:, 256 * j:256 * j + 256], unit(S, 8 + j)[:, 0, 0:256],
                            rsin[:, 256 * j:256 * j + 256], MUL), S, 8 + j)
                emptied(dve, S, it, 8)
                emptied(dve, S, it, 9)
                st.settle()
                tt(qr[:, CTX:T], qr[:, CTX:T], ktmp, ADD).then_inc(qrope_ready, 1)
                for n in range(2 * QT + 1):
                    e, t, s = n // QT, n % QT, n % 2
                    if n < 2 * QT:
                        dve.wait_ge(s_ready, it * 12 + n + 1)
                        i = sc[:, s, 0:1, 0:CTX] if t < 2 else sc[:, s, :, 0:HALF]
                        st.did(dve.tensor_reduce(small[:, s, 0:1], i, XY, MAX))
                        st.settle()
                        ts(small[:, s, 1:2], small[:, s, 0:1], -scale, None, MUL).then_inc(p_max, 1)
                    if n:
                        nk = 2 if (n - 1) % QT < 2 else KT
                        u = 10 + 2 * (n - 1)
                        finished(dve, S, it, u)
                        free(cp(probT[:, (n - 1) % 2, 0:nk * P], flat(unit(S, u))[:, 0:nk * P]), S, u)
                    if n < 2 * QT:
                        w = CTX if t < 2 else T
                        dve.wait_ge(p_exp, it * 12 + n + 1)
                        st.did(dve.reciprocal(small[:, s, 3:4], small[:, s, 2:3]))
                        st.settle()
                        ts(prob[:, s, 0:w], prob[:, s, 0:w], small[:, s, 3:4], None, MUL).then_inc(p_ready, 1)
                    if n:
                        m, u = n - 1, 11 + 2 * (n - 1)
                        finished(dve, S, it, u)
                        if m < 8:
                            cp(mod[:, 0, bass.ds(it * 8 + (2 * DB + m), 1), :], unit(S, u)[:, 1:2, 0:2])
                        elif m < 10:
                            cp(cs[:, bass.ds(it * 2 + (m - 8), 1), 2:3], unit(S, u)[:, 1:2, 0:1])
                        free(cp(attn[:, bass.ds(it * 2 + m // QT, 1), (m % QT) * P:(m % QT) * P + P],
                                unit(S, u)[:, 0:1, 0:P]), S, u)
            st.leave(MLA_H // 2)
            emptied(dve, S, MLA_H // 2 - 1, 33)
            modulation(0, 2, 6, 2, mod[:, 0])
            dve.wait_ge(mod_ready, 2)
            for s in range(MOD_SLOTS):
                dve.memset(mod_w[s % 3][:, s // 3, 0:1], 0.0).then_inc(mod_used[s], 1)
            for s in range(2):
                dve.memset(mod_acc[:, s, 0, 0:1], 0.0).then_inc(mod_summed, 1)

            def out_y(stage, n):
                for j in range(8):
                    finished(dve, stage, 0, j)
                    if n == T:
                        ins = cp(halves(hT[:, j, :]), unit(stage, j)[:, :, 0:HALF])
                    else:
                        ins = cp(hT[:, j, CTX:T], unit(stage, j)[:, 0, :])
                    free(ins, stage, j)

            def split_weights(stage, it, j):
                s = (GROUP0[stage] + j) % 2
                for h in range(2):
                    c = slice(h * 1024, (h + 1) * 1024)
                    dve.wait_ge(w_high, half_group(stage, it, j, h))
                    tt(w_lo[s][:, c], wring[s][:, c], w_hi[s][:, c].bitcast(F32), SUB).then_inc(w_split, 1)

            def low_input(n, b, x0):
                dve.wait_ge(x_high, x0 + b + 1)
                hi = x_hi[:, b, :] if n == T else x_hi_seq[:, b, :]
                tt(x_lo[:, b, T - n:T], hT[:, b, T - n:T], hi.bitcast(F32), SUB).then_inc(x_split, 1)

            def mlp(i, n):
                S = f"mlp{i}"
                dve.wait_ge(e_ready, 1)

                def quarter(it, last):
                    for u in range(16):
                        beside = MOD_BESIDE.get(u // 2)
                        if beside and u % 2 == 0:
                            mod_chunk(i, it, beside[0], ((0, 1), (2,))[i])
                        if u % 2 == 0 and u < 14:
                            split_weights(S, it, u // 2 + 1)
                        elif u == 14 and not last:
                            split_weights(S, it + 1, 0)
                        if u < 8:
                            dve.wait_ge(hid_high, it * 8 + (32 * i + u + 1))
                            tt(hid_lo[:, u, 0:n], relu[:, u % 2, 0:n], hid_hi[:, u, 0:n].bitcast(F32),
                               SUB).then_inc(relu_free, 1)
                        else:
                            finished(dve, S, it, u)
                            if n == T:
                                y = halves(y_mlp[:, u - 8, :])
                                ins = tt(y, y, unit(S, u)[:, :, 0:HALF], ADD)
                            else:
                                y = y_mlp[:, u - 8, 0:n]
                                ins = tt(y, y, unit(S, u)[:, 0, 0:n], ADD)
                            free(ins, S, u)
                        if beside and u % 2 == 0:
                            mod_chunk(i, it, beside[1], ((0, 1), (2,))[i])

                per = MOD_IT * MOD_Q * (MOD_K - 1)
                with dve.Fori(0, 3) as it:
                    st.enter(it, per)
                    quarter(it, False)
                st.leave(3)
                quarter(3, True)
                dve.wait_ge(mod_summed, 2 + MOD_CHUNKS * (i + 1))
                modulation(i + 1, 0, 6, 2 - i)
                dve.wait_ge(mod_ready, 3 + i)

            out_y("mla_out", T)
            residual("y0", T, 0, 1, hT)
            dve.memset(y_mlp[:, :, :], 0.0)
            split_weights("mlp0", 0, 0)
            normed("h0m", T, 0)
            mlp(0, T)
            residual("y0m", T, 0, 3, y_mlp)

            normed("h1", T)
            for d in range(2):
                finished(dve, "gla_gate", 0, d)
                free(cp(halves(hgate[0:GATE_RANK, d, :]), unit("gla_gate", d)[0:GATE_RANK, :, 0:HALF]), "gla_gate", d)
            dve.memset(g_AT[:, :, :], 0.0).then_inc(g_done, 1)
            dve.wait_ge(g_done, 1)
            dve.wait_ge(tab_in, 32)
            S = "gla_head"
            c64 = lambda a: a.rearrange("p (c n) -> p c n", n=64)
            with dve.Fori(0, GLA_H) as it:
                st.enter(it, 18)
                dve.wait_ge(g_done, it * 1 + 1)
                for d in range(2):
                    finished(dve, S, it, d)
                    free(ts(halves(g_z[:, d, :]), unit(S, d)[:, :, 0:HALF], dyncol("gla_b_gate", it * 1 + 4 * d), None, ADD), S, d)
                for d in range(2):
                    emptied(dve, S, it, d)
                    dve.wait_ge(gl_ready, it * 2 + d + 1)
                    st.did(stt(g_g, g_z[:, d, :], 0.0, g_l, MIN, SUB))
                    st.settle()
                    if d == 1:
                        dve.wait_ge(gE_ready, it * 2 + 1)
                    st.did(dve.tensor_tensor_scan(g_G, keep64, g_g, 0.0, MUL, ADD))
                    st.settle()
                    st.did(cp(g_tot[:, d, :], c64(g_G)[:, :, 63]))
                    if d == 1:
                        st.did(tt(g_g, g_G, g_g, SUB))
                        st.settle()
                        st.did(tt(c64(g_G), g_tot[:, 1, :].unsqueeze(2).to_broadcast([P, 12, 64]), c64(g_g), SUB))
                    st.settle()
                    tt(c64(g_z[:, d, :]), g_tot[:, d, :].unsqueeze(2).to_broadcast([P, 12, 64]), c64(g_G), SUB).then_inc(gG_ready, 1)

                def values(j):
                    finished(dve, S, it, 4 + j)
                    free(cp(g_v[:, 2 * j:2 * j + 2, :], unit(S, 4 + j)[:, :, 0:GLA_DV]), S, 4 + j)

                for d in range(2):
                    dve.wait_ge(gE_ready, it * 2 + d + 1)
                    emptied(dve, S, it, 2)
                    emptied(dve, S, it, 3)
                    tt(g_qt[:, d, :], g_qt[:, d, :], g_q, MUL)
                    tt(g_kt[:, d, :], g_kt[:, d, :], g_k[:, CTX:T], MUL)
                    st.did(tt(g_ke[:, d, :], g_ke[:, d, :], g_k, MUL))
                    st.settle()
                    q4, s4 = (x[:, d, :].rearrange("p (t a n) -> p t a n", a=2, n=64) for x in (g_qt, g_qS))
                    e4, k4 = (x[:, d, :].rearrange("p (t a n) -> p t a n", a=2, n=64) for x in (g_ke, g_kE))
                    et = g_et[:, d, :].rearrange("p (t a) -> p t a", a=2)
                    near, far = (0, 1) if d == 0 else (1, 0)
                    cp(s4[:, :, near], q4[:, :, near])
                    tt(s4[:, :, far], q4[:, :, far], et[:, 2:QT, near].unsqueeze(2).to_broadcast([P, LT, 64]), MUL)
                    cp(k4[:, :, far], e4[:, :, far])
                    tt(k4[:, :, near], e4[:, :, near], et[:, :, far].unsqueeze(2).to_broadcast([P, QT, 64]), MUL)
                    tt(g_dec[:, d, :], et[:, :, 0], et[:, :, 1], MUL).then_inc(gk_ready, 1)
                    if d == 0:
                        values(0)
                values(1)
                values(2)
                tri = tri_fb.bitcast(U32).rearrange("p (d n) -> p d n", d=2).unsqueeze(2).to_broadcast([P, 2, LT, P])
                order = ([0, 1, 2, 3, 4], [1, 0, 5, 4, 3])
                for d in range(2):
                    for i, t in enumerate(order[d]):
                        if i in (0, 4):
                            finished(dve, S, it, 10 + 2 * d + i // 4)
                        p = unit(S, 10 + 2 * d + i // 4)[:, (i % 4) // 2, (i % 2) * 256:(i % 2) * 256 + 256]
                        if i == 0:
                            ins = cp(g_S[:, d, 0, :], p)
                        else:
                            ins = stt(g_S[:, d, i, :], g_S[:, d, i - 1, :], g_dec[:, d, t:t + 1], p, MUL, ADD)
                        if i == 3:
                            free(ins, S, 10 + 2 * d)
                            emptied(dve, S, it, 10 + 2 * d)
                        elif i == 4:
                            free(ins, S, 11 + 2 * d)
                        else:
                            st.did(ins)
                            if d == 0 and i == 0:
                                free(dve.copy_predicated(g_AT.rearrange("p d (t n) -> p d t n", n=P), tri,
                                                         unit(S, 9).rearrange("p d (t n) -> p d t n", n=P)), S, 9)
                            st.settle()
                for b in range(2):
                    finished(dve, S, it, 14 + b)
                    free(cp(g_o[:, b, :], unit(S, 14 + b)[:, 0, :]), S, 14 + b)
                dve.wait_ge(gdev_ready, it * 1 + 1)
                for b in range(2):
                    st.did(stt(g_o[:, b, :], g_o[:, b, :], col("gla_g_o", b), rstd[:, 0:SEQ], MUL, MUL))
                st.settle()
                tt(g_out[:, bass.ds(it * 2, 2), :], g_o, g_r, MUL).then_inc(g_done, 1)
            st.leave(GLA_H)
            out_y("gla_out", SEQ)
            residual("y1", SEQ, 1, 1, hT[:, :, CTX:T])
            dve.memset(y_mlp[:, :, 0:SEQ], 0.0)
            split_weights("mlp1", 0, 0)
            normed("h1m", SEQ, DB)
            mlp(1, SEQ)
            residual("y1m", SEQ, 1, 3, y_mlp[:, :, 0:SEQ])

            finished(dve, "gdn_gate", 0, 0)
            dve.wait_ge(d_ga, 1)
            free(ts(rstd[0:GDN_H, 0:SEQ], unit("gdn_gate", 0)[0:GDN_H, 0, :], a_dt[:, 1:2], None, ADD), "gdn_gate", 0)
            dve.wait_ge(d_ga, 2)
            st.did(stt(rstd[0:GDN_H, 0:SEQ], rstd[0:GDN_H, 0:SEQ], 0.0, sq[0:GDN_H, 0, 0:SEQ], MAX, ADD))
            st.settle()
            st.did(ts(rstd[0:GDN_H, 0:SEQ], rstd[0:GDN_H, 0:SEQ], a_dt[:, 2:3], -1.0, MUL, MUL))
            st.settle()
            dve.wait_ge(tab_in, 48)
            dve.tensor_tensor_scan(d_row[:, 1, :], keep128[0:GDN_H, :], rstd[0:GDN_H, 0:SEQ], 0.0, MUL, ADD).then_inc(d_rows, 1)
            emptied(dve, "gdn_gate", 0, 1)
            dve.memset(d_S[:, :, :], 0.0).then_inc(d_rows, 1)
            dve.wait_ge(d_cols, 1)
            cp(d_col[:, 0:2].rearrange("p r c h -> p (r c h)"), sc[:, 1, 0, 0:64]).then_inc(d_gc, 1)
            dve.wait_ge(d_gc, 1)
            dve.wait_ge(d_cols, 2)
            gl = sc[:, 1, 1, 0:32].rearrange("p (c h) -> p c h", c=LT)
            cp(d_col[:, 4], gl)
            tt(d_col[:, 3], gl, d_col[:, 1], SUB).then_inc(d_glr, 1)
            dve.wait_ge(d_ga, 3)
            st.did(ts(d_col[:, 2], d_col[:, 2], -1.0, None, MUL))
            st.settle()
            for j in range(2):
                dve.memset(d_cp[:, j, :, 0:3], 0.0).then_inc(d_conv, 1)
            dve.memset(d_r[:, :, :], 0.0).then_inc(d_done, 1)
            dve.wait_ge(d_done, 1)
            dve.wait_ge(d_conv, 2)
            S = "gdn_pair"
            colh = lambda r, c, it, e: d_col[:, r, c, bass.ds(it * 2 + e, 1)]
            with dve.Fori(0, GDN_H // 2) as it:
                st.enter(it, 28)
                for r, x in enumerate((sq[0:GDN_H, :, 0:SEQ], d_ET[0:GDN_H])):
                    for e in range(2):
                        ins = ts(x[:, e, :], d_row[:, 1 - r, :], ident[0:GDN_H, bass.ds(it * 2 + e, 1)], None, MUL)
                    ins.then_inc(d_masked, 1)

                def convolve(j, x):
                    if j < 2:
                        dve.wait_ge(qk_moved, it * 2 + j + 1)
                    else:
                        emptied(dve, S, it, 0)
                    for tap in (3, 0, 1, 2):
                        for e in range(2):
                            w = dyncol("gdn_conv_w", it * 2 + (24 * tap + 8 * j + e))
                            s = d_cp[:, j % 2, e, tap:tap + SEQ]
                            if tap == 3:
                                ins = ts(x[:, e, :], s, w, None, MUL)
                            else:
                                ins = stt(x[:, e, :], s, w, x[:, e, :], MUL, ADD)
                            if tap == 2 and e == 1:
                                ins.then_inc(d_conv, 1)
                            else:
                                st.did(ins)
                        if tap != 2:
                            st.settle()
                convolve(0, d_q)
                convolve(1, d_k)
                convolve(2, d_v)
                emptied(dve, S, it, 1)
                emptied(dve, S, it, 2)
                for e in range(2):
                    for c in range(LT):
                        t = slice(c * P, (c + 1) * P)
                        last = ts(d_ET[:, e, t], d_gcR[:, e, t], colh(1, c, it, e), 0.0, SUB, MIN)
                last.then_inc(d_diff, 1)
                dve.wait_ge(d_len, it * 3 + 1)
                stt(d_q, d_q, P ** -0.5, d_Y, MUL, MUL).then_inc(d_norm, 1)
                c8 = lambda m: m.unsqueeze(1).to_broadcast([P, 2 * LT, P])
                cp(chunks(d_T), c8(ident))
                dve.wait_ge(d_len, it * 3 + 2)
                tt(d_k, d_k, d_U, MUL).then_inc(d_norm, 1)
                dve.wait_ge(d_norm, it * 2 + 2)
                cp(chunks(d_U), c8(ident)).then_inc(d_init, 1)
                dve.wait_ge(d_exp, it * 2 + 1)
                st.did(tt(d_LT, d_ET, d_bR, MUL))
                st.settle()
                st.did(tt(chunks(d_ET), chunks(d_ET), c8(causal), MUL))
                st.settle()
                finished(dve, S, it, 7)
                free(tt(d_LT, d_LT, unit(S, 7), MUL), S, 7)
                emptied(dve, S, it, 7)

                def level_mask(l):
                    tt(chunks(d_Lm[:, l % 2]), chunks(d_LT), c8(lvl_mask[l]), MUL).then_inc(d_lm, 1)

                level_mask(0)
                level_mask(1)
                finished(dve, S, it, 8)
                free(tt(d_QK, d_ET, unit(S, 8), MUL), S, 8)
                finished(dve, S, it, 9)
                for e in range(2):
                    for c in range(LT):
                        t = slice(c * P, (c + 1) * P)
                        last = ts(d_kend[:, e, t], unit(S, 9)[:, e, t], colh(3, c, it, e), None, MUL)
                free(last, S, 9)
                finished(dve, S, it, 10)
                free(cp(d_V, unit(S, 10)), S, 10)
                for l in range(7):
                    j = 11 + 3 * l
                    if l < 6:
                        finished(dve, S, it, j + 1)
                        free(tt(d_T, d_T, unit(S, j + 1), SUB), S, j + 1)
                    k = j + 2 if l < 6 else j + 1
                    finished(dve, S, it, k)
                    free(tt(d_U, d_U, unit(S, k), SUB), S, k)
                    emptied(dve, S, it, k)
                    if l < 6:
                        emptied(dve, S, it, j + 1)
                    if l + 2 < 7:
                        level_mask(l + 2)
                    if l == 0:
                        dve.wait_ge(d_exp, it * 2 + 2)
                        tt(d_qE, d_q, d_v, MUL)
                        dve.memset(d_S[:, :, :], 0.0).then_inc(d_qe, 1)
                for c in range(LT):
                    t, j = slice(c * P, (c + 1) * P), 31 + 4 * c
                    finished(dve, S, it, j)
                    for e in range(2):
                        ins = stt(d_r[:, e, :], unit(S, j)[:, e, 0:P], colh(2, c, it, e), d_V[:, e, t], MUL, ADD)
                        if e:
                            free(ins, S, j)
                        else:
                            st.did(ins)
                    emptied(dve, S, it, j)
                    st.settle()
                    for e in range(2):
                        ins = ts(d_r[:, e, :], d_r[:, e, :], colh(0, c, it, e), None, MUL)
                    ins.then_inc(d_rr, 1)
                    finished(dve, S, it, j + 3)
                    for e in range(2):
                        ins = stt(d_S[:, e, :], d_S[:, e, :], colh(4, c, it, e), unit(S, j + 3)[:, e, 0:P], MUL, ADD)
                    free(ins, S, j + 3)
                    emptied(dve, S, it, j + 3)
                dve.wait_ge(d_len, it * 3 + 3)
                st.did(stt(d_o, d_o, col("gdn_norm_w", 0), d_Y, MUL, MUL))
                st.settle()
                tt(d_out[:, bass.ds(it * 2, 2), :], d_o, d_z, MUL).then_inc(d_done, 1)
            st.leave(GDN_H // 2)

            def add_residual(stage, l, q, loop, x0, phase=None):
                dve.wait_ge(x_ready, x0)
                if not loop:
                    for j in range(8):
                        finished(dve, stage, 0, j)
                        free(stt(xT[:, j, CTX:T], unit(stage, j)[:, 0, :], dcol[:, l, q, j, 0:1], xT[:, j, CTX:T], MUL, ADD), stage, j)
                    return
                with dve.Fori(0, 4) as it:
                    st.enter(it, MOD_IT * MOD_Q * (MOD_K - 1) if phase else 0)
                    for j in range(2):
                        if phase:
                            for c in range(j * MOD_UNIT, (j + 1) * MOD_UNIT):
                                mod_chunk(phase, it, c, (2,))
                        finished(dve, stage, it, j)
                        x = xT[:, bass.ds(it * 2 + j, 1), CTX:T]
                        free(stt(x, unit(stage, j)[:, 0:1, :], dcol[:, l, q, bass.ds(it * 2 + j, 1), 0], x, MUL, ADD), stage, j)
                st.leave(4)
                if phase:
                    dve.wait_ge(mod_summed, 2 + MOD_CHUNKS * (phase + 1))
                    modulation(phase + 1, 0, 6, 1)
                    dve.wait_ge(mod_ready, 3 + phase)

            def layer_norm(name, i, x0=None):
                dve.wait_ge(n_mean, i + 1)
                for b in range(DB):
                    stt(xT[:, b, CTX:T], sc[:, 0, 1, :], -1.0 / D, xT[:, b, CTX:T], MUL, ADD).then_inc(n_cent, 1)
                deviation_of(name)
                over_deviation(xT, SEQ, x0)

            def ffn(i):
                up = f"ffn{i}_up"

                def pair(it, last):
                    split_weights(up, it, 1)
                    emptied(dve, up, it, 0)
                    for tap in (2, 0, 1):
                        for b in range(2):
                            w = dyncol(f"conv_w{i}", it * 2 + (HIDB * tap + b))
                            s = gpad[:, b, tap:tap + SEQ]
                            if tap == 2:
                                ins = ts(gconv[:, b, :], s, w, dyncol("conv_b", it * 2 + (HIDB * i + b)), MUL, ADD)
                            else:
                                ins = stt(gconv[:, b, :], s, w, gconv[:, b, :], MUL, ADD)
                            if tap != 1:
                                st.did(ins)
                        if tap != 1:
                            st.settle()
                    ins.then_inc(f_conv, 1)
                    if not last:
                        split_weights(up, it + 1, 0)
                    dve.wait_ge(f_silu, it * 1 + (HIDB // 2 * i + 1))
                    finished(dve, up, it, 1)
                    free(tt(hid2[:, bass.ds(it * 2, 2), :], gsilu, unit(up, 1), MUL), up, 1)

                with dve.Fori(0, HIDB // 2 - 1) as it:
                    st.enter(it, 2 * 2)
                    pair(it, False)
                st.leave(HIDB // 2 - 1)
                pair(HIDB // 2 - 1, True)

            add_residual("gdn_out", 2, 1, False, 32)
            split_weights("ffn0_up", 0, 0)
            dve.memset(gpad[:, :, 0:2], 0.0).then_inc(f_conv, 1)
            layer_norm("ln0", 0, DB * 2)
            ffn(0)
            add_residual("ffn0_down", 2, 3, True, 40, 2)
            split_weights("ret_head", 0, 0)
            layer_norm("ln0f", 1, DB * 3)

            dve.memset(r_tmp[:, :, 0:1], 0.0).then_inc(r_done, 1)
            dve.wait_ge(r_done, 1)
            dve.wait_ge(rtab_in, 16)
            tcos, tsin = r_tab[:, 0, :], r_tab[:, 1, :]
            S = "ret_head"

            def ret_head(it, final):
                for i in range(2):
                    split_weights(S, it, 1 + i)
                    emptied(dve, S, it, i)
                    a, b = r_raw[:, i, 0, :], r_raw[:, i, 1, :]
                    oa, ob = r_rot[:, i, 0, :], r_rot[:, i, 1, :]
                    st.did(tt(r_tmp[:, 0, :], b, tsin, MUL))
                    st.did(tt(r_tmp[:, 1, :], b, tcos, MUL))
                    st.did(tt(oa, a, tcos, MUL))
                    st.did(tt(ob, a, tsin, MUL))
                    st.settle()
                    tt(oa, oa, r_tmp[:, 0, :], SUB)
                    tt(ob, ob, r_tmp[:, 1, :], ADD).then_inc(r_rotd, 1)
                    dve.wait_ge(r_rotd, it * 2 + i + 1)
                split_weights(S, it, 3)
                split_weights(S, it, 4)
                for j in range(2):
                    finished(dve, S, it, 2 + j)
                    free(cp(r_v[:, 2 * j:2 * j + 2], unit(S, 2 + j).rearrange("p t (a n) -> p t a n", a=2)), S, 2 + j)
                split_weights(S, it, 5)
                if not final:
                    split_weights(S, it + 1, 0)
                for j in range(2):
                    finished(dve, S, it, 6 + j)
                    for i in range(2):
                        t = 2 * j + i
                        w = SEQ - t * P
                        ins = tt(r_s[:, t:t + 1, 0:w], unit(S, 6 + j)[:, i:i + 1, 0:w],
                                 r_tab[:, bass.ds(it * 1 + 2, 1), 0:w], MUL)
                    free(ins, S, 6 + j)
                for j in range(2):
                    finished(dve, S, it, 8 + j)
                    free(cp(r_o[:, 2 * j:2 * j + 2, :], unit(S, 8 + j)), S, 8 + j)
                emptied(dve, S, it, 8)
                emptied(dve, S, it, 9)
                finished(dve, S, it, 10)
                for b in range(4):
                    ins = stt(r_o[:, b, :], unit(S, 10)[:, 0, :], -1.0 / RET_DV, r_o[:, b, :], MUL, ADD)
                    if b < 3:
                        ins.then_inc(r_cent, 1)
                    else:
                        free(ins, S, 10)
                dve.wait_ge(r_dev, it * 1 + 1)
                st.did(tt(r_o, r_o, rstd[:, 0:SEQ].unsqueeze(1).to_broadcast([P, 4, SEQ]), MUL))
                st.settle()
                tt(r_out[:, bass.ds(it * 4, 4), :].rearrange("p e (a n) -> p e a n", a=2),
                   r_o.rearrange("p e (a n) -> p e a n", a=2), r_gate, MUL).then_inc(r_done, 1)

            with dve.Fori(0, RET_H - 1) as it:
                st.enter(it, 9)
                ret_head(it, False)
            st.leave(RET_H - 1)
            ret_head(RET_H - 1, True)
            add_residual("ret_out", 3, 1, False, 48)
            split_weights("ffn1_up", 0, 0)
            dve.memset(gpad[:, :, 0:2], 0.0).then_inc(f_conv, 1)
            layer_norm("ln1", 2, DB * 4)
            ffn(1)
            add_residual("ffn1_down", 3, 3, True, 56)
            layer_norm("ln1f", 3)
            for t in range(LT):
                dve.wait_ge(o_turned, t + 1)
                cp(o_tok[:, t, :], flat(sc[:, t % 2])).then_inc(o_moved, 1)


def tables():
    f = np.float32
    eye = np.eye(P, dtype=f)
    base = np.concatenate([eye, np.ones((P, P), f)], 1)
    i, j = np.arange(P)[None, :], np.arange(P)[:, None]
    swap = np.zeros((64, 64), f)
    for g in (0, 32):
        for a in range(16):
            swap[g + a, g + 16 + a], swap[g + 16 + a, g + a] = -1.0, 1.0
    rot2 = np.kron(np.eye(2, dtype=f), swap).T
    pad = np.zeros((64, P), f)
    dup = np.concatenate([np.concatenate([np.eye(64, dtype=f)] * 2, 1), pad], 0)
    rotdup = np.concatenate([np.concatenate([swap.T] * 2, 1), pad], 0)
    tok = np.arange(SEQ)
    inv = (f(10000.0) ** (-np.arange(0, 32, 2, dtype=f) / f(32))).astype(f)
    ang = np.concatenate([inv[:, None] * (tok // 64).astype(f)] * 2 + [inv[:, None] * (tok % 64).astype(f)] * 2, 0)
    ang = np.concatenate([ang, ang], 0).astype(f)
    mla = np.concatenate([rot2, dup, rotdup, np.cos(ang), np.sin(ang)], 1)
    keep = np.ones((P, T), f)
    keep[:, ::64] = 0.0
    gla = np.concatenate([keep, j <= i, j >= i], 1)
    lv = [((i // (2 * s)) == (j // (2 * s))) & ((i // s) % 2 == 1) & ((j // s) % 2 == 0) for s in LEVELS]
    last = np.zeros((P, P), f)
    last[P - 1] = 1.0
    keep = np.ones((P, SEQ), f)
    keep[:, ::P] = 0.0
    gdn = np.concatenate(lv + [j <= i, last, keep], 1)
    inv = (f(10000.0) ** (-np.linspace(0.0, 1.0, P, dtype=f))).astype(f)
    ang = (inv[:, None] * tok.astype(f)[None, :]).astype(f)
    rel = np.arange(SEQ, dtype=f)[None, :] - np.arange(P, dtype=f)[:, None]
    lg = np.log(f(1.0) - np.power(f(2.0), f(-5.0) - np.arange(RET_H, dtype=f))).astype(f)
    dec = [np.where(rel >= 0, np.exp(np.maximum(rel, f(0)) * g), f(0)) for g in lg]
    ret = np.concatenate([np.cos(ang), np.sin(ang)] + dec, 1)
    return {n: np.ascontiguousarray(a, dtype=f) for n, a in
            (("tab_base", base), ("tab_mla", mla), ("tab_gla", gla), ("tab_gdn", gdn), ("tab_ret", ret))}


INPUTS = ["x", "c", "ctx", "c_ctx", "ada_w", "ada_b", "norm_g", "mlp_w1", "mlp_w2", "mla_w_dq", "mla_g_q", "mla_w_uq",
          "mla_w_dkv", "mla_g_kv", "mla_w_ukv", "mla_w_o", "gla_w_q", "gla_w_k", "gla_w_v", "gla_w_r", "gla_w_gate1",
          "gla_w_gate2", "gla_b_gate", "gla_g_o", "gla_w_o", "c_2", "cond_w_2", "cond_b_2", "ada_w_2", "ada_b_2",
          "ln_g_2", "ln_b_2", "ffn_up_2", "ffn_conv_w_2", "ffn_conv_b_2", "ffn_down_2", "gdn_w_in_2", "gdn_conv_w_2",
          "gdn_a_log_2", "gdn_dt_bias_2", "gdn_norm_w_2", "gdn_w_out_2", "ret_w_in_2", "ret_w_out_2"]


def kernel(**inputs):
    import numpy as _np
    import concourse.bacc as _bacc
    from concourse import mybir as _mybir
    from concourse.bass_utils import run_bass_kernel_spmd as _run

    nc = _bacc.Bacc("TRN2", target_bir_lowering=False, num_devices=1)
    given = {n: _np.ascontiguousarray(inputs[n]) for n in INPUTS}
    given.update(tables())
    arrays, A = {}, {}
    for name, a in given.items():
        arrays[f"in_{name}"] = a
        A[name] = nc.dram_tensor(f"in_{name}", a.shape, _mybir.dt.from_np(a.dtype), kind="ExternalInput").ap()
    out = nc.dram_tensor("out_0", (1, SEQ, D), _mybir.dt.float32, kind="ExternalOutput").ap()
    first_and_second_block(nc, A, out)
    r = _run(nc, [arrays], core_ids=[0])
    return r.results[0]["out_0"]
```
